# Optimizing a Trainium2 kernel written in Bass

```python
import math
import jax, jax.numpy as jnp
from jax import lax
import numpy as np

D_MODEL = 1024
BATCH = 1
SEQ = 512
DEPTH = 2
DEC_BATCH = 1
DEC_SEQ = 64
PAST_LEN = 256

CHUNK = 64
N_MEM = 256
HEAD_DIM = 64
SB_HEADS = 8
SB_WIDTH = SB_HEADS * HEAD_DIM
CONV_WIDTH = 256
CONV_K = 3
HG_HEADS = 4
HG_WIDTH = HG_HEADS * HEAD_DIM
MIX_WIDTH = SB_WIDTH + CONV_WIDTH + HG_WIDTH
MEM_HEADS = 4
MEM_HEAD_DIM = D_MODEL // MEM_HEADS
D_FF = 2816
Q_BLOCK = 128
N_SUBLAYERS = 4
EPS = 1e-6
F_FLOOR = 1e-30
IN_SPLITS = (SB_WIDTH,) * 3 + (CONV_WIDTH,) * 3 + (HG_WIDTH,) * 4
IN_WIDTH = sum(IN_SPLITS)
IN_OFFSETS = tuple(int(o) for o in np.cumsum(IN_SPLITS)[:-1])

kernel_name = "hybrid_stream_sb_conv_hgrn2_step"

def rmsnorm(x, g):
    xf = x.astype(jnp.float32)
    y = xf * lax.rsqrt(jnp.mean(xf * xf, axis=-1, keepdims=True) + EPS)
    return (y * g.astype(jnp.float32)).astype(x.dtype)

def swiglu(h, w_gu, w_down):
    gate, up = jnp.split(h @ w_gu, 2, axis=-1)
    return (jax.nn.silu(gate) * up) @ w_down

def _sb_block(q, k, v, q_pos0):
    scale = 1.0 / math.sqrt(q.shape[-1])
    z = jnp.einsum('bthd,bshd->bhts', q, k).astype(jnp.float32) * scale
    t_pos = q_pos0 + jnp.arange(q.shape[1])
    s_pos = jnp.arange(k.shape[1])
    mask = s_pos[None, :] < t_pos[:, None]
    log_keep = jnp.where(mask, jax.nn.log_sigmoid(-z), 0.0)
    log_rest = lax.cumsum(log_keep, axis=3, reverse=True) - log_keep
    w = jnp.where(mask, jnp.exp(jnp.where(mask, jax.nn.log_sigmoid(z) + log_rest, 0.0)), 0.0)
    return jnp.einsum('bhts,bshd->bthd', w.astype(v.dtype), v)

def stick_breaking_attention(q, k, v, q_pos0):
    tq = q.shape[1]
    outs = []
    for start in range(0, tq, Q_BLOCK):
        stop = min(start + Q_BLOCK, tq)
        k_end = q_pos0 + stop
        outs.append(_sb_block(q[:, start:stop], k[:, :k_end], v[:, :k_end], q_pos0 + start))
    return jnp.concatenate(outs, axis=1) if len(outs) > 1 else outs[0]

def causal_short_conv(u, past, w):
    t = u.shape[1]
    full = jnp.concatenate([past, u], axis=1)
    y = full[:, 0:t] * w[0]
    for j in range(1, CONV_K):
        y = y + full[:, j:j + t] * w[j]
    return y, full[:, t:]

def hgrn_lower_bounds(logits):
    p = jax.nn.softmax(logits.astype(jnp.float32), axis=0)
    return jnp.cumsum(p, axis=0) - p[0:1]

def hgrn2_recurrence(q, log_f, k, v, s0):
    b_sz, t, h, _ = q.shape
    dv = v.shape[-1]
    pad = (-t) % CHUNK
    n = (t + pad) // CHUNK

    def blocks(a):
        a = jnp.pad(a.astype(jnp.float32), ((0, 0), (0, pad), (0, 0), (0, 0)))
        return a.reshape(b_sz, n, CHUNK, h, a.shape[-1]).transpose(1, 0, 3, 2, 4)

    causal = jnp.tril(jnp.ones((CHUNK, CHUNK), dtype=bool))[:, :, None]

    def step(s, blk):
        qc, gc, kc, vc = blk
        b = jnp.cumsum(gc, axis=2)
        inter = jnp.einsum('bhtk,bhkv->bhtv', qc * jnp.exp(b), s)
        diff = b[:, :, :, None, :] - b[:, :, None, :, :]
        decay = jnp.where(causal, jnp.exp(jnp.where(causal, diff, 0.0)), 0.0)
        scores = jnp.einsum('bhtsk,bhsk->bhts', qc[:, :, :, None, :] * decay, kc)
        o = inter + jnp.einsum('bhts,bhsv->bhtv', scores, vc)
        b_last = b[:, :, -1:, :]
        s = jnp.exp(b_last[:, :, 0, :])[..., None] * s + jnp.einsum('bhsk,bhsv->bhkv', kc * jnp.exp(b_last - b), vc)
        return s, o

    s, o = lax.scan(step, s0.astype(jnp.float32), (blocks(q), blocks(log_f), blocks(k), blocks(v)))
    o = o.transpose(1, 0, 3, 2, 4).reshape(b_sz, n * CHUNK, h, dv)[:, :t]
    return o.astype(v.dtype), s

def memory_kv(mem, g, w_k, w_v):
    b_sz, n, _ = mem.shape
    m = rmsnorm(mem, g)
    k = (m @ w_k).reshape(b_sz, n, MEM_HEADS, MEM_HEAD_DIM)
    v = (m @ w_v).reshape(b_sz, n, MEM_HEADS, MEM_HEAD_DIM)
    return k, v

def memory_attention(h, mem_k, mem_v, w_q, w_o):
    b_sz, t, _ = h.shape
    q = (h @ w_q).reshape(b_sz, t, MEM_HEADS, MEM_HEAD_DIM)
    s = jnp.einsum('bthd,bnhd->bhtn', q, mem_k).astype(jnp.float32) / math.sqrt(MEM_HEAD_DIM)
    p = jax.nn.softmax(s, axis=-1).astype(mem_v.dtype)
    o = jnp.einsum('bhtn,bnhd->bthd', p, mem_v).reshape(b_sz, t, D_MODEL)
    return o @ w_o

def trunk(x, q_pos0, sb_k_past, sb_v_past, conv_past, hg_past, mem_k, mem_v, params):
    (norm_pre, norm_post, ffn1_gu, ffn1_down, w_in, conv_w, hg_lb, hg_norm, w_out,
     w_mq, w_mo, ffn2_gu, ffn2_down) = params
    b_sz, t, _ = x.shape
    lb_all = hgrn_lower_bounds(hg_lb)
    new_k, new_v, new_conv, new_hg = [], [], [], []
    for l in range(DEPTH):
        h = rmsnorm(x, norm_pre[l, 0])
        x = x + 0.5 * rmsnorm(swiglu(h, ffn1_gu[l], ffn1_down[l]), norm_post[l, 0])
        h = rmsnorm(x, norm_pre[l, 1])
        sb_q, sb_k, sb_v, cv_b, cv_c, cv_h, hg_q, hg_f, hg_i, hg_g = jnp.split(h @ w_in[l], IN_OFFSETS, axis=-1)
        k_l = sb_k.reshape(b_sz, t, SB_HEADS, HEAD_DIM)
        v_l = sb_v.reshape(b_sz, t, SB_HEADS, HEAD_DIM)
        sb_out = stick_breaking_attention(
            sb_q.reshape(b_sz, t, SB_HEADS, HEAD_DIM),
            jnp.concatenate([sb_k_past[l], k_l], axis=1),
            jnp.concatenate([sb_v_past[l], v_l], axis=1), q_pos0).reshape(b_sz, t, SB_WIDTH)
        conv_y, conv_state = causal_short_conv(cv_c * cv_h, conv_past[l], conv_w[l])
        conv_out = cv_b * conv_y
        lb = lb_all[l]
        a = hg_f.astype(jnp.float32)
        f = lb + (1.0 - lb) * jax.nn.sigmoid(a)
        log_f = jnp.log(jnp.maximum(f, F_FLOOR))
        k_hg = (1.0 - lb) * jax.nn.sigmoid(-a)
        o_hg, s_hg = hgrn2_recurrence(
            hg_q.reshape(b_sz, t, HG_HEADS, HEAD_DIM), log_f.reshape(b_sz, t, HG_HEADS, HEAD_DIM),
            k_hg.reshape(b_sz, t, HG_HEADS, HEAD_DIM), hg_i.reshape(b_sz, t, HG_HEADS, HEAD_DIM), hg_past[l])
        o_hg = rmsnorm(o_hg, hg_norm[l].reshape(HG_HEADS, HEAD_DIM)).reshape(b_sz, t, HG_WIDTH) * jax.nn.silu(hg_g)
        mix = jnp.concatenate([sb_out, conv_out, o_hg], axis=-1) @ w_out[l]
        x = x + rmsnorm(mix, norm_post[l, 1])
        h = rmsnorm(x, norm_pre[l, 2])
        x = x + rmsnorm(memory_attention(h, mem_k[l], mem_v[l], w_mq[l], w_mo[l]), norm_post[l, 2])
        h = rmsnorm(x, norm_pre[l, 3])
        x = x + 0.5 * rmsnorm(swiglu(h, ffn2_gu[l], ffn2_down[l]), norm_post[l, 3])
        new_k.append(k_l)
        new_v.append(v_l)
        new_conv.append(conv_state)
        new_hg.append(s_hg.astype(x.dtype))
    return x, jnp.stack(new_k), jnp.stack(new_v), jnp.stack(new_conv), jnp.stack(new_hg)

def setup_inputs(seed: int = 0) -> dict:
    key = jax.random.key(seed)
    ks = jax.random.split(key, 32)
    f32 = jnp.float32

    def nrm(k, shape, scale=1.0):
        return jax.random.normal(k, shape, f32) * scale

    def wt(k, shape, fan_in):
        return jax.random.normal(k, shape, f32) * fan_in ** -0.5

    def gain(k, shape):
        return 1.0 + 0.01 * jax.random.normal(k, shape, f32)

    return {
        "x_prompt": nrm(ks[0], (BATCH, SEQ, D_MODEL)),
        "x_sample": nrm(ks[1], (DEC_BATCH, DEC_SEQ, D_MODEL)),
        "mem_prompt": nrm(ks[2], (BATCH, N_MEM, D_MODEL)),
        "cache_sb_k": nrm(ks[3], (DEPTH, DEC_BATCH, PAST_LEN, SB_HEADS, HEAD_DIM)),
        "cache_sb_v": nrm(ks[4], (DEPTH, DEC_BATCH, PAST_LEN, SB_HEADS, HEAD_DIM)),
        "cache_mem_k": nrm(ks[5], (DEPTH, DEC_BATCH, N_MEM, MEM_HEADS, MEM_HEAD_DIM)),
        "cache_mem_v": nrm(ks[6], (DEPTH, DEC_BATCH, N_MEM, MEM_HEADS, MEM_HEAD_DIM)),
        "state_conv": nrm(ks[7], (DEPTH, DEC_BATCH, CONV_K - 1, CONV_WIDTH)),
        "state_hgrn": nrm(ks[8], (DEPTH, DEC_BATCH, HG_HEADS, HEAD_DIM, HEAD_DIM), 0.5),
        "norm_pre": gain(ks[9], (DEPTH, N_SUBLAYERS, D_MODEL)),
        "norm_post": gain(ks[10], (DEPTH, N_SUBLAYERS, D_MODEL)),
        "ffn1_gu": wt(ks[11], (DEPTH, D_MODEL, 2 * D_FF), D_MODEL),
        "ffn1_down": wt(ks[12], (DEPTH, D_FF, D_MODEL), D_FF),
        "w_in": wt(ks[13], (DEPTH, D_MODEL, IN_WIDTH), D_MODEL),
        "conv_w": wt(ks[14], (DEPTH, CONV_K, CONV_WIDTH), CONV_K),
        "hg_lb": nrm(ks[15], (DEPTH, HG_WIDTH), 0.1),
        "hg_norm": gain(ks[16], (DEPTH, HG_WIDTH)),
        "w_out": wt(ks[17], (DEPTH, MIX_WIDTH, D_MODEL), MIX_WIDTH),
        "mem_norm": gain(ks[18], (DEPTH, D_MODEL)),
        "w_mk": wt(ks[19], (DEPTH, D_MODEL, D_MODEL), D_MODEL),
        "w_mv": wt(ks[20], (DEPTH, D_MODEL, D_MODEL), D_MODEL),
        "w_mq": wt(ks[21], (DEPTH, D_MODEL, D_MODEL), D_MODEL),
        "w_mo": wt(ks[22], (DEPTH, D_MODEL, D_MODEL), D_MODEL),
        "ffn2_gu": wt(ks[23], (DEPTH, D_MODEL, 2 * D_FF), D_MODEL),
        "ffn2_down": wt(ks[24], (DEPTH, D_FF, D_MODEL), D_FF),
    }

def reference(x_prompt, x_sample, mem_prompt, cache_sb_k, cache_sb_v, cache_mem_k, cache_mem_v,
              state_conv, state_hgrn, norm_pre, norm_post, ffn1_gu, ffn1_down, w_in, conv_w, hg_lb,
              hg_norm, w_out, mem_norm, w_mk, w_mv, w_mq, w_mo, ffn2_gu, ffn2_down):
    params = (norm_pre, norm_post, ffn1_gu, ffn1_down, w_in, conv_w, hg_lb, hg_norm, w_out,
              w_mq, w_mo, ffn2_gu, ffn2_down)
    mem_kv_p = [memory_kv(mem_prompt, mem_norm[l], w_mk[l], w_mv[l]) for l in range(DEPTH)]
    mem_k_p = jnp.stack([kv[0] for kv in mem_kv_p])
    mem_v_p = jnp.stack([kv[1] for kv in mem_kv_p])
    b_p = x_prompt.shape[0]
    dt = x_prompt.dtype
    empty_kv = jnp.zeros((DEPTH, b_p, 0, SB_HEADS, HEAD_DIM), dt)
    conv0 = jnp.zeros((DEPTH, b_p, CONV_K - 1, CONV_WIDTH), dt)
    hg0 = jnp.zeros((DEPTH, b_p, HG_HEADS, HEAD_DIM, HEAD_DIM), jnp.float32)
    y_prompt, sb_k_p, sb_v_p, conv_p, hg_p = trunk(
        x_prompt, 0, empty_kv, empty_kv, conv0, hg0, mem_k_p, mem_v_p, params)
    y_sample, sb_k_s, sb_v_s, conv_s, hg_s = trunk(
        x_sample, cache_sb_k.shape[2], cache_sb_k, cache_sb_v, state_conv, state_hgrn,
        cache_mem_k, cache_mem_v, params)
    return (y_prompt, y_sample, sb_k_p, sb_v_p, conv_p, hg_p, mem_k_p, mem_v_p,
            sb_k_s, sb_v_s, conv_s, hg_s)


_drawn_inputs = setup_inputs


def setup_inputs(seed=0):
    import zlib

    import numpy as np

    out = dict(_drawn_inputs(seed))
    spreads = {}
    factors = {'norm_post': 3.597, 'hg_norm': 8.0, 'mem_norm': 4.87, 'cache_sb_k': 3.784}
    for name, (base, spread) in spreads.items():
        noise = np.random.default_rng([zlib.crc32(name.encode()), seed]).standard_normal(out[name].shape)
        drawn = base * np.exp(spread * noise) if base else spread * noise
        out[name] = __import__('jax').numpy.asarray(drawn.astype(out[name].dtype))
    for name, factor in factors.items():
        out[name] = (out[name] * factor).astype(out[name].dtype)
    return out
```

```python
from contextlib import ExitStack

import concourse.bass as bass
from concourse import mybir

F32 = mybir.dt.float32
F32R = mybir.dt.float32r
U8 = mybir.dt.uint8
ALU = mybir.AluOpType
ACT = mybir.ActivationFunctionType
AX = mybir.AxisListType

P = 128
D = 1024
DEPTH = 2
KD = D // P
SEQ, DEC, PAST, NMEM = 512, 64, 256, 256
T = SEQ + DEC
HT = T // 2
FF = 2816
KF = FF // P
KU = KF // 2
SBH, HD = 8, 64
NCH = SEQ // P
EPS = 1e-6
F_FLOOR = 1e-30
LN_SPLIT = 2.0 ** -60
MH, MHD = 4, 256

Q0, B0, HQ0, K0, C0, HF0, H0, HG0, V0, HI0 = 0, 4, 6, 8, 12, 14, 16, 18, 20, 24
IN_PLACE = ([Q0 + i for i in range(4)] + [K0 + i for i in range(4)] + [V0 + i for i in range(4)]
            + [B0, B0 + 1, C0, C0 + 1, H0, H0 + 1, HQ0, HQ0 + 1, HF0, HF0 + 1, HI0, HI0 + 1, HG0, HG0 + 1])
NIN = len(IN_PLACE)

PHASES = [("F1", 2 * KF, KD), ("D1", 2 * KD, KU), ("IN", NIN, KD), ("OUT", KD, KD), ("MK", KD, KD),
          ("MV", KD, KD), ("MQ", KD, KD), ("MO", KD, KD), ("F2", 2 * KF, KD), ("D2", 2 * KD, KU)]
UNITS = sum(n for _, n, _ in PHASES)
TILES = {"F1": 2 * KF, "D1": KD, "IN": NIN, "OUT": KD, "MK": 0, "MV": 0, "MQ": KD, "MO": KD, "F2": 2 * KF, "D2": KD}
NT = sum(TILES.values())
LEVELS = 8


def unit_base(l, phase):
    names = [p[0] for p in PHASES]
    return l * UNITS + sum(n for _, n, _ in PHASES[:names.index(phase)])


def tile_base(l, phase):
    names = [p[0] for p in PHASES]
    return l * NT + sum(TILES[n] for n in names[:names.index(phase)])


def unit_words(u):
    u %= UNITS
    for _, n, k in PHASES:
        if u < n:
            return k * P
        u -= n


def hybrid_trunk(nc, i, o):
    ctx = ExitStack()
    with ctx:
        def place(name, shape, dt, words):
            return nc.alloc_sbuf_tensor_at(name, shape, dt, offset=16512 + 4 * words)

        x = place("x", [P, KD, T], F32, 0)
        H = KD * T
        h_hi = place("h_hi", [P, KD, T], F32R, H)
        h_lo = place("h_lo", [P, KD, T], F32R, H + KD * T)
        y = place("y", [P, KD, T], F32, H + KD * T)
        G = H + 2 * KD * T
        a_hi = place("a_hi", [P, KF, T], F32R, G)
        a_lo = place("a_lo", [P, KF, T], F32R, G + KF * T)
        proj = place("proj", [P, NIN, T], F32, G)
        mix_hi = place("mix_hi", [P, KD, T], F32R, G)
        mix_lo = place("mix_lo", [P, KD, T], F32R, G + KD * T)
        g = G + NIN * T
        vtok = place("vtok", [P, NCH + 1, 512], F32, g)
        itok = place("itok", [P, NCH + 1, 256], F32, g + 2560)
        kf = place("kf", [P, 2, T], F32, g + 3840)
        ot = place("ot", [P, 2, T], F32, g + 4992)
        kpast = place("kpast", [P, 4, PAST], F32, g + 6144)
        vpast = place("vpast", [P, 2, 512], F32, g + 7168)
        kpast_tok = place("kpast_tok", [P, 2, 512], F32, g + 8192)
        cu = place("cu", [P, 2, T + 4], F32, H)
        ct = place("ct", [P, 2, T], F32, H + 1160)
        ktok = place("ktok", [P, NCH + 1, 512], F32, H + 4608)
        bT = place("bT", [P, 2, T], F32, H)
        hE = place("hE", [P, 2, T], F32, H + 1152)
        hQ = place("hQ", [P, 2, T], F32, H + 2304)
        hK = place("hK", [P, 2, T], F32, H + 3456)
        sacc = place("sacc", [P, NCH * 512 + 256], F32, H + 4608)
        kotok = place("kotok", [P, NCH + 1, 256], F32, H + 6912)
        st_p = place("st_p", [P, 2, HD], F32, H + 8192)
        st_s = place("st_s", [P, 2, HD], F32, H + 8320)
        ones_w = place("ones_w", [P, P], F32, H + 8448)
        at_a = [place(f"at_a{s}", [P, 1536], F32, H + 4608 * s) for s in range(2)]
        at_s = [place(f"at_s{s}", [P, 1536], F32, H + 4608 * s + 1536) for s in range(2)]
        at_w = [place(f"at_w{s}", [P, 1536], F32, H + 4608 * s + 3072) for s in range(2)]
        qx = place("qx", [P, KD, T], F32, G)
        xo_hi = place("xo_hi", [P, KD, T], F32R, G)
        xo_lo = place("xo_lo", [P, KD, T], F32R, G + 4608)
        mtok = place("mtok", [P, 2, D], F32, G + 9216)
        m_hi = place("m_hi", [P, KD, NMEM], F32R, G + 11264)
        m_lo = place("m_lo", [P, KD, NMEM], F32R, G + 13312)
        mk_p = place("mk_p", [P, KD, NMEM], F32, G + 15360)
        mv_p = place("mv_p", [P, 2, D], F32, G + 17408)
        mk_s = place("mk_s", [P, KD, NMEM], F32, G + 19456)
        mv_s = place("mv_s", [P, 2, D], F32, G + 21504)
        pr = [place(f"pr{s}", [P, MH, NMEM], F32, H + 1024 * s) for s in range(2)]
        pT = place("pT", [P, 8, T], F32, H + 2048)
        xtok = place("xtok", [P, NCH + 1, D], F32, G)
        gst1 = place("gst1", [P, P], F32, G + 5120)
        gst2 = place("gst2", [P, P], F32, G + 5248)
        lst = place("lst", [P, LEVELS, P], F32, G + 5376)
        W = G + 2 * KF * T
        raw = place("raw", [P, 2, KU * P], F32, W)
        w_hi = place("w_hi", [P, 2, KU * P], F32R, W + 2 * KU * P)
        w_lo = place("w_lo", [P, 2, KU * P], F32R, W + 4 * KU * P)
        M = W + 6 * KU * P
        sq = place("sq", [P, 2, T], F32, M)
        gt = place("gt", [P, T], F32, M + 2 * T)
        sg = place("sg", [P, T], F32, M + 3 * T)
        ut = place("ut", [P, T], F32, M + 4 * T)
        acc = place("acc", [P, T], F32, M + 5 * T)
        rinv = place("rinv", [P, T], F32, M + 6 * T)
        m0 = M + 7 * T
        cst = place("cst", [P, 5, P], F32, m0)
        lmask = place("lmask", [P, LEVELS, P], U8, m0 + 640)
        par = place("par", [P, 164], F32, m0 + 896)
        small = place("small", [P, 64], F32, m0 + 1064)
        ident, ntri, nones, ones, bones = (cst[:, n, :] for n in range(5))
        eps = small[:, 0:1]
        lbv = small[:, 1:5]
        oml = small[:, 5:9]
        lt = small[:, 9:21]
        mss = small[:, 21:23]
        ebl = small[:, 24:34]
        mx = small[:, 34:42]
        rsum = small[:, 42:50]
        rrec = small[:, 50:58]

        PL = [ctx.enter_context(nc.psum_tensor(f"PL{s}", [P, 2, 512], F32)) for s in range(2)]
        PX = [ctx.enter_context(nc.psum_tensor(f"PX{s}", [P, 2, 512], F32)) for s in range(2)]
        BK = [PX[0][:, 0, :], PX[0][:, 1, :], PX[1][:, 0, :], PX[1][:, 1, :],
              PL[0][:, 0, :], PL[0][:, 1, :], PL[1][:, 0, :], PL[1][:, 1, :]]
        PAIR = [PX[0], PX[1], PL[0], PL[1]]

        def sem(name):
            return ctx.enter_context(nc.semaphore(name))

        cst_l = sem("cst_loaded")
        xin_l = sem("x_loaded")
        w_l = [sem(f"w_loaded{s}") for s in range(2)]
        whi_r, wlo_r = sem("w_hi_ready"), sem("w_lo_ready")
        unit_d = sem("unit_products_done")
        tile_e = sem("psum_tile_emptied")
        mkv_e = sem("memory_tile_emptied")
        sq_r, acc_r, ms_r, rs_r, rinv_r = (sem(n) for n in ("square_ready", "squares_added", "mean_square_ready",
                                                            "root_ready", "rinv_ready"))
        x_r, hi_r, lo_r, y_r = sem("x_ready"), sem("h_hi_ready"), sem("h_lo_ready"), sem("y_scaled")
        xt_d = sem("x_transposed")
        par_d, par_r = sem("gains_transposed"), sem("gains_ready")
        sg_r, ut_r, pr_r, ahi_r, alo_r = (sem(n) for n in ("silu_ready", "up_ready", "inner_ready",
                                                                 "a_hi_ready", "a_lo_ready"))
        dch, ach, pch = sem("vector_step"), sem("scalar_step"), sem("pool_step")
        cache_l, conv_l = sem("caches_loaded"), sem("conv_state_loaded")
        tp_d, tp_e = sem("token_major_done"), sem("token_major_emptied")
        kout_s = sem("k_rows_stored")
        mixst_s = sem("mix_outputs_stored")
        cu_r, cvr, cvhi = sem("conv_input_ready"), sem("conv_ready"), sem("conv_hi_ready")
        sig_r, f_r, ln_r = sem("sigmoids_ready"), sem("forget_ready"), sem("logs_ready")
        e_in, e_r, qk_r = sem("decay_exponent_ready"), sem("decay_ready"), sem("decayed_qk_ready")
        sc_d, sc_e = sem("scores_done"), sem("scores_kept")
        kk_r, kt_d, kt_e = sem("kout_ready"), sem("kout_transposed"), sem("kout_emptied")
        ho_d, ho_e, hs_d, hs_r = sem("hg_out_done"), sem("hg_out_emptied"), sem("hg_state_done"), sem("hg_state_ready")
        s0_l, hst_s = sem("hg_state_loaded"), sem("hg_state_stored")
        osq_r, oms_d, ors_r, hgo_r, hghi = (sem(n) for n in ("o_square_ready", "o_mean_done", "o_root_ready", "o_gated", "o_hi_ready"))
        mixlo_r = sem("mix_lo_ready")
        z_d, l_r, sp_r, spm_r, r_d, wx_r, wm_r, av_d, avhi_r, avlo_r = (
            sem(n) for n in ("z_done", "log1p_ready", "softplus_ready", "softplus_masked", "rest_done", "weights_ready",
                             "weights_masked", "attended", "attended_hi", "attended_lo"))
        mem_l, mss_r, mrs_r, mn_r, mt_d, mhi_r, mlo_r = (
            sem(n) for n in ("mem_loaded", "mem_squares", "mem_root", "mem_normed", "mem_transposed", "m_hi_ready", "m_lo_ready"))
        ck_l, cv_l, ck_d, ck_e, kr_d, kr_e, kr_s, mv_s_sem = (
            sem(n) for n in ("cache_k_loaded", "cache_v_loaded", "cache_k_transposed", "cache_k_emptied",
                             "k_rows_done", "k_rows_emptied", "mem_k_stored", "mem_v_stored"))
        qx_r = sem("queries_ready")
        xs_d, mx_r, xe_r, pn_r, pt_d, pt_e, xa_d, xahi_r, xalo_r = (
            sem(n) for n in ("x_scores_done", "x_max_ready", "x_exp_ready", "x_probs_ready", "probs_transposed",
                             "probs_emptied", "x_attended", "x_attended_hi", "x_attended_lo"))
        yt_d, yt_e, y_s = sem("y_transposed"), sem("y_emptied"), sem("y_stored")

        gpre = lambda l, n, k: par[:, (l * 4 + n) * 8 + k:(l * 4 + n) * 8 + k + 1]
        gpost = lambda l, n, k: par[:, 64 + (l * 4 + n) * 8 + k:64 + (l * 4 + n) * 8 + k + 1]
        gmem = lambda l, k: par[:, 128 + l * 8 + k:129 + l * 8 + k]
        cw = lambda l, j, c: par[:, 144 + l * 6 + j * 2 + c:145 + l * 6 + j * 2 + c]
        gh = lambda l, c: par[:, 160 + l * 2 + c:161 + l * 2 + c]

        halves = lambda ap: ap.rearrange("p (h t) -> p h t", h=2)
        POST = {"D1": 0, "OUT": 1, "MO": 2, "D2": 3}
        NU = DEPTH * UNITS
        NXA = NCH + 1
        rows = lambda b: P if b < NCH else DEC
        NJ = 2 + SBH
        tiles_of = lambda job: 3 if job < 2 else NCH
        Z_BASE = [sum(tiles_of(n) for n in range(job)) for job in range(NJ + 1)]
        NZT = Z_BASE[NJ]
        M_END = [sum(1 if n < 2 else NCH for n in range(job + 1)) for job in range(NJ)]
        NMASK = M_END[-1]
        SW = SBH // 2 * DEC
        W_OFF = [0, 512, 896, 1152]

        block = ctx.enter_context(nc.Block())

        @block.sync
        def _(sp):
            def view(w):
                return w.rearrange("(k p) m -> p k m", p=P)

            def stream(a, n, kt, src):
                def load(r, s):
                    sp.dma_start(raw[:, s, 0:kt * P].rearrange("p (k m) -> p k m", k=kt), src(r, s)).then_inc(w_l[s], 16)
                first = 0
                if a == 0:
                    load(0, 0)
                    load(0, 1)
                    first = 1
                with sp.Fori(first, n // 2) as r:
                    for s in range(2):
                        sp.wait_ge(wlo_r, r * 2 + (a + s - 1))
                        load(r, s)

            for l in range(DEPTH):
                for f, (pu, pd, gu, dn) in enumerate((("F1", "D1", i["ffn1_gu"], i["ffn1_down"]),
                                                      ("F2", "D2", i["ffn2_gu"], i["ffn2_down"]))):
                    if f == 1:
                        for ph, w in (("IN", "w_in"), ("OUT", "w_out"), ("MK", "w_mk"), ("MV", "w_mv"), ("MQ", "w_mq"), ("MO", "w_mo")):
                            v = view(i[w][l])
                            n = NIN if ph == "IN" else KD
                            stream(unit_base(l, ph), n, KD, lambda r, s, v=v: v[:, :, bass.ds(r * 256 + s * P, P)])
                    v = view(gu[l])
                    stream(unit_base(l, pu), 2 * KF, KD, lambda r, s, v=v: v[:, :, bass.ds(r * P + s * FF, P)])
                    v = view(dn[l])
                    stream(unit_base(l, pd), 2 * KD, KU, lambda r, s, v=v: v[:, s * KU:(s + 1) * KU, bass.ds(r * P, P)])

        @block.tensor
        def _(pe):
            mm = nc.tensor.matmul

            def products(s, kt, out, lhs, rhs, first, last):
                n = 0
                for k in range(kt):
                    for a, b in ((0, 0), (0, 1), (1, 0)):
                        m = mm(out, lhs(a, k), rhs(b, k), start=(first and n == 0), stop=(last and n == 3 * kt - 1))
                        n += 1
                return m

            wt = lambda s: (lambda part, k: (w_hi, w_lo)[part][:, s, k * P:(k + 1) * P])

            def unit(u, s, hi, lo, kt=KD, k0=0, first=True, last=True, slot=None, gate=None):
                pe.wait_ge(wlo_r, u + 1)
                slot = s if slot is None else slot
                n = 0
                for k in range(kt):
                    if gate:
                        gate(k)
                    for a, b in ((0, 0), (0, 1), (1, 0)):
                        for h in range(2):
                            m = mm(PL[slot][:, h, 0:HT], wt(s)(a, k), (hi, lo)[b][:, k0 + k, h * HT:(h + 1) * HT],
                                   start=(first and n == 0), stop=(last and n == 3 * kt - 1))
                        n += 1
                m.then_inc(unit_d, 1)

            def mean_square(n):
                pe.wait_ge(acc_r, KD * (n + 1))
                if n:
                    pe.wait_ge(rs_r, n)
                for h in range(2):
                    m = mm(PX[0][:, h, 0:HT], ones, acc[:, h * HT:(h + 1) * HT], start=True, stop=True)
                m.then_inc(ms_r, 1)

            def h_gate(pn):
                def gate(k):
                    pe.wait_ge(hi_r, KD * pn + k + 1)
                    pe.wait_ge(lo_r, KD * pn + k + 1)
                return gate

            def ffn(l, pu, pd, pn, f):
                a, t = unit_base(l, pu), tile_base(l, pu)
                for s in range(2):
                    if t + s >= 2:
                        pe.wait_ge(tile_e, t + s - 1)
                    unit(a + s, s, h_hi, h_lo, gate=h_gate(pn) if s == 0 else None)
                    if s == 0:
                        mean_square(2 * pn)
                with pe.Fori(1, KF) as r:
                    for s in range(2):
                        pe.wait_ge(tile_e, r * 2 + (t + s - 1))
                        unit(r * 2 + (a + s), s, h_hi, h_lo)
                b, t = unit_base(l, pd), tile_base(l, pd)
                for m in range(KD):
                    pe.wait_ge(tile_e, t + m - 1)
                    for s in range(2):
                        if m == 0:
                            pe.wait_ge(alo_r, KF * f + (KU if s == 0 else KF))
                            pe.wait_ge(ahi_r, KF * f + (KU if s == 0 else KF))
                        unit(b + 2 * m + s, s, a_hi, a_lo, kt=KU, k0=s * KU, first=(s == 0), last=(s == 1), slot=m % 2)
                mean_square(2 * pn + 1)

            pe.wait_ge(cst_l, 16 * 8)
            nc.tensor.transpose(BK[0][:, 0:P], gst1[:, :], ident)
            nc.tensor.transpose(BK[1][:, 0:36], gst2[0:36, :], cst[0:36, 0, 0:36]).then_inc(par_d, 1)
            pe.wait_ge(xin_l, 32)
            for k in range(KD):
                if k >= 2:
                    pe.wait_ge(x_r, k - 1)
                for b in range(NXA):
                    m = nc.tensor.transpose(PL[k % 2][:, b // NCH, (b % NCH) * P:(b % NCH) * P + rows(b)],
                                            xtok[0:rows(b), b, k * P:(k + 1) * P], cst[0:rows(b), 0, 0:rows(b)])
                m.then_inc(xt_d, 1)
            for l in range(DEPTH):
                if l == 0:
                    pe.wait_ge(x_r, KD)
                ffn(l, "F1", "D1", 4 * l, 2 * l)
                pn = 4 * l + 1
                a, t = unit_base(l, "IN"), tile_base(l, "IN")
                for s in range(2):
                    pe.wait_ge(tile_e, t + s - 1)
                    unit(a + s, s, h_hi, h_lo, gate=h_gate(pn) if s == 0 else None)
                    if s == 0:
                        mean_square(2 * pn)
                with pe.Fori(1, NIN // 2) as r:
                    for s in range(2):
                        pe.wait_ge(tile_e, r * 2 + (t + s - 1))
                        unit(r * 2 + (a + s), s, h_hi, h_lo)
                pe.wait_ge(tile_e, t + NIN)
                pe.wait_ge(cache_l, 32 * (l + 1))
                n = 0
                for kind in range(3):
                    for b in range(NXA):
                        if n >= 4:
                            pe.wait_ge(tp_e, 17 * l + n - 3)
                        c0 = b * P if b < NCH else SEQ
                        for q in range(4 if kind < 2 else 2):
                            m = nc.tensor.transpose(BK[n % 4][0:rows(b), q * P:(q + 1) * P],
                                                    proj[:, (K0, V0, HI0)[kind] + q, c0:c0 + rows(b)], ident)
                        m.then_inc(tp_d, 1)
                        n += 1
                for half in range(2):
                    pe.wait_ge(tp_e, 17 * l + n - 3)
                    for q in range(2):
                        for b in range(2):
                            m = nc.tensor.transpose(BK[n % 4][:, (2 * q + b) * P:(2 * q + b + 1) * P],
                                                    kpast_tok[:, b, (2 * half + q) * P:(2 * half + q + 1) * P], ident)
                    m.then_inc(tp_d, 1)
                    n += 1
                pe.wait_ge(tp_e, 17 * (l + 1))
                n = 0
                for lev in range(LEVELS):
                    if lev:
                        pe.wait_ge(qk_r, (LEVELS - 1) * l + lev)
                    else:
                        pe.wait_ge(f_r, l + 1)
                    qq = proj[:, HQ0:HQ0 + 2, :] if lev == 0 else hQ[:, :, :]
                    kk = kf[:, :, :] if lev == 0 else hK[:, :, :]
                    for c in range(NXA if lev < LEVELS - 1 else NCH):
                        if n >= 4:
                            pe.wait_ge(sc_e, (5 * LEVELS - 1) * l + n - 3)
                        nt, c0 = rows(c), c * P
                        for h in range(4):
                            e, j = 64 * (h % 2), h // 2
                            m = mm(PAIR[n % 4][0:nt, h % 2, j * nt:(j + 1) * nt], kk[e:e + 64, j, c0:c0 + nt],
                                   qq[e:e + 64, j, c0:c0 + nt], start=True, stop=True)
                        m.then_inc(sc_d, 1)
                        n += 1
                pe.wait_ge(kk_r, l + 1)
                pe.wait_ge(sc_e, (5 * LEVELS - 1) * (l + 1))
                for c in range(NXA):
                    if c >= 4:
                        pe.wait_ge(kt_e, NXA * l + c - 3)
                    for j in range(2):
                        m = nc.tensor.transpose(BK[c % 4][0:rows(c), j * P:(j + 1) * P], hK[:, j, c * P:c * P + rows(c)], ident)
                    m.then_inc(kt_d, 1)
                pe.wait_ge(kt_e, NXA * (l + 1))
                pe.wait_ge(s0_l, 16 * (l + 1))
                for c in range(NXA):
                    nt, c0 = rows(c), c * P
                    st = st_p if c < NCH else st_s
                    if c >= 2:
                        pe.wait_ge(ho_e, NXA * l + c - 1)
                    if 0 < c < NCH:
                        pe.wait_ge(hs_r, NXA * l + c)
                    ob, sbk = BK[4 + c % 2], BK[6 + c % 2]
                    for h in range(4):
                        e, j = 64 * (h % 2), h // 2
                        inter = c > 0
                        m = mm(ob[e:e + 64, j * P:j * P + nt], itok[:, c, h * 64:(h + 1) * 64],
                               sacc[:, c * 512 + (2 * (h % 2) + j) * nt:c * 512 + (2 * (h % 2) + j + 1) * nt], start=True, stop=not inter)
                        if inter:
                            m = mm(ob[e:e + 64, j * P:j * P + nt], st[e:e + 64, j, :], hQ[e:e + 64, j, c0:c0 + nt],
                                   start=False, stop=True)
                    m.then_inc(ho_d, 1)
                    if c >= 2:
                        pe.wait_ge(hs_r, NXA * l + c - 1)
                    for h in range(4):
                        e, j = 64 * (h % 2), h // 2
                        m = mm(sbk[e:e + 64, j * 64:(j + 1) * 64], kotok[0:nt, c, h * 64:(h + 1) * 64],
                               itok[0:nt, c, h * 64:(h + 1) * 64], start=True, stop=True)
                    m.then_inc(hs_d, 1)
                pe.wait_ge(osq_r, l + 1)
                for j in range(2):
                    for h in range(2):
                        m = mm(PX[j][:, h, 0:HT], bones, hE[:, j, h * HT:(h + 1) * HT], start=True, stop=True)
                m.then_inc(oms_d, 1)
                pe.wait_ge(hgo_r, l + 1)
                pe.wait_ge(hs_r, NXA * (l + 1))
                pe.wait_ge(ho_e, NXA * (l + 1))

                def scores(job):
                    bk = BK[4 * (job % 2):4 * (job % 2) + 4]
                    if job >= 2:
                        pe.wait_ge(avhi_r, NJ * l + job - 1)
                        pe.wait_ge(avlo_r, NJ * l + job - 1)
                    if job < 2:
                        for j in range(3):
                            nk = P if j < 2 else DEC
                            for h in range(job, SBH, 2):
                                e = 64 * (h % 2)
                                ks = (kpast[e:e + 64, h // 2, j * P:(j + 1) * P] if j < 2
                                      else proj[e:e + 64, K0 + h // 2, SEQ:T])
                                m = mm(bk[j][0:nk, h // 2 * DEC:(h // 2 + 1) * DEC], ks, proj[e:e + 64, Q0 + h // 2, SEQ:T],
                                       start=(h == job), stop=True, skip_group_check=True)
                            m.then_inc(z_d, 1)
                    else:
                        h = job - 2
                        e = 64 * (h % 2)
                        for j in range(NCH):
                            m = mm(bk[j][:, 0:SEQ - j * P], proj[e:e + 64, K0 + h // 2, j * P:(j + 1) * P],
                                   proj[e:e + 64, Q0 + h // 2, j * P:SEQ], start=True, stop=True, skip_group_check=True)
                            m.then_inc(z_d, 1)

                def rest(job):
                    bk = BK[4 * (job % 2):4 * (job % 2) + 4]
                    s = at_s[job % 2]
                    pe.wait_ge(spm_r, NMASK * l + M_END[job])
                    nj = tiles_of(job)
                    for j in reversed(range(nj)):
                        if job < 2:
                            nk = P if j < 2 else DEC
                            m = mm(bk[j][0:nk, 0:SW], ntri[0:nk, 0:nk], s[0:nk, j * 512:j * 512 + SW], start=False, stop=True,
                                   skip_group_check=True)
                            for j2 in range(j + 1, 3):
                                n2 = P if j2 < 2 else DEC
                                m = mm(bk[j][0:nk, 0:SW], nones[0:n2, 0:nk], s[0:n2, j2 * 512:j2 * 512 + SW], start=False,
                                       stop=True, skip_group_check=True)
                        else:
                            m = mm(bk[j][:, 0:SEQ - j * P], ntri, s[:, W_OFF[j]:W_OFF[j] + SEQ - j * P], start=False,
                                   stop=True, skip_group_check=True)
                            for j2 in range(j + 1, nj):
                                m = mm(bk[j][:, (j2 - j) * P:SEQ - j * P], nones, s[:, W_OFF[j2]:W_OFF[j2] + SEQ - j2 * P],
                                       start=False, stop=True, skip_group_check=True)
                        m.then_inc(r_d, 1)

                def attend(job):
                    bk = BK[4 * (job % 2) + 3]
                    w = at_w[job % 2]
                    pe.wait_ge(wm_r, NMASK * l + M_END[job])
                    if job < 2:
                        for h in range(job, SBH, 2):
                            e = 64 * (h % 2)
                            for j in range(3):
                                nk = P if j < 2 else DEC
                                vv = (vpast[:, j, h * 64:(h + 1) * 64] if j < 2 else vtok[0:DEC, NCH, h * 64:(h + 1) * 64])
                                m = mm(bk[e:e + 64, (h // 2) * 64:(h // 2 + 1) * 64], vv,
                                       w[0:nk, j * 512 + h // 2 * DEC:j * 512 + (h // 2 + 1) * DEC], start=(j == 0), stop=(j == 2))
                    else:
                        h = job - 2
                        e = 64 * (h % 2)
                        for j in range(NCH):
                            m = mm(bk[e:e + 64, j * P:SEQ], vtok[:, j, h * 64:(h + 1) * 64],
                                   w[:, W_OFF[j]:W_OFF[j] + SEQ - j * P], start=(j == 0), stop=(j == NCH - 1),
                                   skip_group_check=True)
                    m.then_inc(av_d, 1)

                scores(0)
                scores(1)
                for job in range(NJ):
                    rest(job)
                    attend(job)
                    if job + 2 < NJ:
                        scores(job + 2)
                a, t = unit_base(l, "OUT"), tile_base(l, "OUT")
                pn = 4 * l + 1
                pe.wait_ge(avhi_r, NJ * (l + 1))
                pe.wait_ge(avlo_r, NJ * (l + 1))
                pe.wait_ge(mixlo_r, 4 * (l + 1))
                for m in range(KD):
                    pe.wait_ge(tile_e, t + m - 1)
                    unit(a + m, m % 2, mix_hi, mix_lo)
                mean_square(2 * pn + 1)
                pe.wait_ge(mn_r, l + 1)
                for n in range(4):
                    if n >= 2:
                        pe.wait_ge(mlo_r, 4 * l + n - 1)
                    for q in range(2):
                        for b in range(2):
                            m = nc.tensor.transpose(BK[2 + n % 2][:, (2 * q + b) * P:(2 * q + b + 1) * P],
                                                    mtok[:, b, (2 * n + q) * P:(2 * n + q + 1) * P], ident)
                    m.then_inc(mt_d, 1)
                pe.wait_ge(mhi_r, 4 * (l + 1))
                pe.wait_ge(mlo_r, 4 * (l + 1))
                pe.wait_ge(tile_e, t + KD)
                for v in range(2):
                    a = unit_base(l, "MV" if v else "MK")
                    for m in range(KD):
                        n = KD * v + m
                        if n >= 2:
                            pe.wait_ge(mkv_e, 16 * l + n - 1)
                        pe.wait_ge(wlo_r, a + m + 1)
                        s = m % 2
                        if v == 0:
                            last = products(s, KD, PL[s][:, 0, 0:NMEM], wt(s), lambda part, k: (m_hi, m_lo)[part][:, k, :], True, True)
                        else:
                            for b in range(2):
                                last = products(s, KD, PL[s][:, b, 0:P],
                                                lambda part, k: (m_hi, m_lo)[part][:, k, b * P:(b + 1) * P], wt(s), True, True)
                        last.then_inc(unit_d, 1)
                pn = 4 * l + 2
                a, t = unit_base(l, "MQ"), tile_base(l, "MQ")
                pe.wait_ge(mkv_e, 16 * (l + 1))
                for m in range(KD):
                    if m >= 2:
                        pe.wait_ge(tile_e, t + m - 1)
                    unit(a + m, m % 2, h_hi, h_lo, gate=h_gate(pn) if m == 0 else None)
                    if m == 0:
                        mean_square(2 * pn)
                pe.wait_ge(ck_l, 16 * (l + 1))
                for n in range(4):
                    if n >= 2:
                        pe.wait_ge(ck_e, 4 * l + n - 1)
                    for q in range(2):
                        for b in range(2):
                            m = nc.tensor.transpose(BK[2 + n % 2][:, (2 * q + b) * P:(2 * q + b + 1) * P],
                                                    mtok[:, b, (2 * n + q) * P:(2 * n + q + 1) * P], ident)
                    m.then_inc(ck_d, 1)
                pe.wait_ge(ck_e, 4 * (l + 1))
                for n in range(4):
                    if n >= 2:
                        pe.wait_ge(kr_e, 4 * l + n - 1)
                    for q in range(4):
                        m = nc.tensor.transpose(BK[2 + n % 2][:, q * P:(q + 1) * P],
                                                mk_p[:, 4 * (n % 2) + q, (n // 2) * P:(n // 2 + 1) * P], ident)
                    m.then_inc(kr_d, 1)
                pe.wait_ge(kr_e, 4 * (l + 1))
                pe.wait_ge(tile_e, t + KD)
                pe.wait_ge(rs_r, 2 * pn + 1)

                def x_scores(b):
                    nt, c0 = rows(b), b * P
                    if b >= 2:
                        pe.wait_ge(xe_r, 4 * (NXA * l + b - 1))
                    for h in range(MH):
                        for kk in range(2):
                            m = mm(PL[b % 2][0:nt, h // 2, (h % 2) * NMEM:(h % 2 + 1) * NMEM], qx[:, 2 * h + kk, c0:c0 + nt],
                                   (mk_p if b < NCH else mk_s)[:, 2 * h + kk, :], start=(kk == 0), stop=(kk == 1))
                    m.then_inc(xs_d, 1)

                def x_turn(b):
                    nt = rows(b)
                    pe.wait_ge(pn_r, 4 * (NXA * l + b + 1))
                    if b >= 2:
                        pe.wait_ge(pt_e, NXA * l + b - 1)
                    for hc in range(8):
                        m = nc.tensor.transpose(PX[b % 2][:, hc // 4, (hc % 4) * P:(hc % 4) * P + nt],
                                                pr[b % 2][0:nt, hc // 2, (hc % 2) * P:(hc % 2 + 1) * P], cst[0:nt, 0, 0:nt])
                    m.then_inc(pt_d, 1)

                x_scores(0)
                for b in range(NXA):
                    if b + 1 < NXA:
                        x_scores(b + 1)
                    x_turn(b)
                pe.wait_ge(pt_e, NXA * (l + 1))
                pe.wait_ge(xe_r, 4 * NXA * (l + 1))
                pe.wait_ge(cv_l, 16 * (l + 1))
                for n in range(8):
                    h, dt = n // 2, n % 2
                    if n >= 2:
                        pe.wait_ge(xalo_r, 8 * l + n - 1)
                    for grp in range(2):
                        v = mv_p if grp == 0 else mv_s
                        c0, nt = (0, SEQ) if grp == 0 else (SEQ, DEC)
                        for c in range(2):
                            m = mm(PL[n % 2][:, grp, 0:nt], v[:, c, n * P:(n + 1) * P], pT[:, 2 * h + c, c0:c0 + nt],
                                   start=(c == 0), stop=(c == 1))
                    m.then_inc(xa_d, 1)
                a, t = unit_base(l, "MO"), tile_base(l, "MO")
                pe.wait_ge(xalo_r, 8 * (l + 1))
                for m in range(KD):
                    if m >= 2:
                        pe.wait_ge(tile_e, t + m - 1)
                    unit(a + m, m % 2, xo_hi, xo_lo)
                mean_square(2 * pn + 1)
                ffn(l, "F2", "D2", 4 * l + 3, 2 * l + 1)
            pe.wait_ge(x_r, KD * (4 * DEPTH + 1))
            for n in range(2 * NXA):
                b, half = n // 2, n % 2
                if n >= 4:
                    pe.wait_ge(yt_e, n - 3)
                if n == 0:
                    pe.wait_ge(rs_r, 8 * DEPTH)
                for q in range(4):
                    m = nc.tensor.transpose(BK[n % 4][0:rows(b), q * P:(q + 1) * P], x[:, 4 * half + q, b * P:b * P + rows(b)], ident)
                m.then_inc(yt_d, 1)

        @block.scalar
        def _(act):
            A = nc.scalar.activation
            chain = [0]

            def link(ins):
                chain[0] += 1
                ins.then_inc(ach, 1)
                act.wait_ge(ach, chain[0])

            def split(u, s, words, wait=True):
                act.wait_ge(w_l[s], u * 8 + (16 - 8 * s))
                A(w_hi[:, s, 0:words], raw[:, s, 0:words], ACT.Copy).then_inc(whi_r, 1)

            def step(u, py=None):
                act.wait_ge(unit_d, u)
                if u + 1 < NU:
                    split(u + 1, (u + 1) % 2, unit_words(u + 1))

            def pre_piece(pn, k):
                act.wait_ge(x_r, KD * pn + k + 1)
                l, n = pn // 4, pn % 4
                A(h_hi[:, k, :], x[:, k, :], ACT.Copy, scale=gpre(l, n, k)).then_inc(hi_r, 1)
                c = KD * 2 * pn + k
                if c >= 2:
                    act.wait_ge(acc_r, c - 1)
                A(sq[:, k % 2, :], x[:, k, :], ACT.Square).then_inc(sq_r, 1)

            def root(n):
                act.wait_ge(ms_r, n + 1)
                A(halves(rinv[:, :]), PX[0][:, :, 0:HT], ACT.Sqrt, scale=1.0 / D, bias=eps).then_inc(rs_r, 1)

            def post_square(pn, m):
                c = KD * (2 * pn + 1) + m
                act.wait_ge(acc_r, c - 1)
                A(halves(sq[:, m % 2, :]), PL[m % 2][:, :, 0:HT], ACT.Square).then_inc(sq_r, 1)

            def ffn(l, pu, pd, pn, f):
                a = unit_base(l, pu)
                root(2 * pn)

                def first(r, words):
                    u = r * 2 + (a + 1)
                    act.wait_ge(unit_d, u)
                    split(u + 1, 0, words)
                    act.wait_ge(tile_e, r * 2 + (tile_base(l, pu) + 1))
                    A(sg[:, :], gt[:, :], ACT.Silu).then_inc(sg_r, 1)

                def second(r, words):
                    u = r * 2 + (a + 2)
                    act.wait_ge(unit_d, u)
                    split(u + 1, 1, words)
                    act.wait_ge(pr_r, r + (KF * f + 1))
                    A(a_hi[:, bass.ds(r, 1), :], ut[:, :].rearrange("p (o t) -> p o t", o=1), ACT.Copy).then_inc(ahi_r, 1)

                with act.Fori(0, KF - 1) as r:
                    first(r, KD * P)
                    second(r, KD * P)
                first(KF - 1, KU * P)
                second(KF - 1, KU * P)
                b = unit_base(l, pd)
                for u in range(b + 1, b + 2 * KD + 1):
                    step(u)
                    if (u - b) % 2 == 0:
                        post_square(pn, (u - b) // 2 - 1)
                act.wait_ge(tile_e, tile_base(l, pd))
                root(2 * pn + 1)

            split(0, 0, unit_words(0))
            split(1, 1, unit_words(1))
            act.wait_ge(par_r, 3)
            A(lt[:, 2:6], lt[:, 2:6], ACT.Exp).then_inc(par_r, 1)
            for k in range(KD):
                pre_piece(0, k)
            for l in range(DEPTH):
                ffn(l, "F1", "D1", 4 * l, 2 * l)
                pn = 4 * l + 1
                for k in range(KD):
                    pre_piece(pn, k)
                root(2 * pn)
                a = unit_base(l, "IN")
                for u in range(a + 1, a + NIN + 1):
                    step(u)
                for n in range(17):
                    act.wait_ge(tp_d, 17 * l + n + 1)
                    kind, b = n // NXA, n % NXA
                    if n < 15:
                        dst = (ktok, vtok, itok)[kind][0:rows(b), b, :]
                        w = 512 if kind < 2 else 256
                        A(dst, BK[n % 4][0:rows(b), 0:w], ACT.Copy).then_inc(tp_e, 1)
                    else:
                        q = 2 * (n - 15)
                        A(kpast[:, q:q + 2, :], BK[n % 4].rearrange("p (q t) -> p q t", q=2), ACT.Copy).then_inc(tp_e, 1)
                act.wait_ge(cvr, l + 1)
                A(mix_hi[:, 4:6, :], ct[:, :, :], ACT.Copy).then_inc(cvhi, 1)
                hf = proj[:, HF0:HF0 + 2, :]
                act.wait_ge(cvhi, l + 1)
                act.wait_ge(mixlo_r, 4 * l + 2)
                act.wait_ge(mixst_s, 64 * (l + 1))
                A(kf[:, :, :], hf, ACT.Sigmoid, scale=-1.0).then_inc(sig_r, 1)
                A(bT[:, :, :], hf, ACT.Sigmoid).then_inc(sig_r, 1)
                act.wait_ge(f_r, l + 1)
                A(hE[:, :, :], bT[:, :, :], ACT.Ln).then_inc(ln_r, 1)
                A(hQ[:, :, :], hK[:, :, :], ACT.Ln, scale=1.0 / LN_SPLIT).then_inc(ln_r, 1)
                for lev in range(1, LEVELS + 2):
                    if lev == LEVELS:
                        act.wait_ge(qk_r, (LEVELS - 1) * (l + 1))
                    else:
                        act.wait_ge(e_in, LEVELS * l + min(lev, LEVELS))
                    if lev < LEVELS:
                        link(A(hE[:, :, :], hE[:, :, :], ACT.Abs))
                        A(hE[:, :, :], hE[:, :, :], ACT.Exp, scale=-1.0).then_inc(e_r, 1)
                    elif lev == LEVELS:
                        A(hE[:, :, :], bT[:, :, :], ACT.Exp).then_inc(e_r, 1)
                    else:
                        A(hE[:, :, :], hE[:, :, :], ACT.Exp, scale=-1.0).then_inc(e_r, 1)
                for c in range(NXA):
                    act.wait_ge(kt_d, NXA * l + c + 1)
                    A(kotok[0:rows(c), c, :], BK[c % 4][0:rows(c), 0:256], ACT.Copy).then_inc(kt_e, 1)
                for c in range(NXA):
                    act.wait_ge(ho_d, NXA * l + c + 1)
                    A(ot[:, :, c * P:c * P + rows(c)], BK[4 + c % 2][:, 0:256].rearrange("p (j t) -> p j t", j=2)[:, :, 0:rows(c)],
                      ACT.Copy).then_inc(ho_e, 1)
                act.wait_ge(ho_e, NXA * (l + 1))
                act.wait_ge(qk_r, (LEVELS - 1) * (l + 1))
                act.wait_ge(kk_r, l + 1)
                A(hE[:, :, :], ot[:, :, :], ACT.Square).then_inc(osq_r, 1)
                act.wait_ge(oms_d, l + 1)
                for j in range(2):
                    A(halves(hQ[:, j, :]), PX[j][:, :, 0:HT], ACT.Sqrt, scale=1.0 / HD, bias=eps).then_inc(ors_r, 1)
                act.wait_ge(kt_d, NXA * (l + 1))
                A(hK[:, :, :], proj[:, HG0:HG0 + 2, :], ACT.Silu).then_inc(ors_r, 1)
                act.wait_ge(hgo_r, l + 1)
                A(mix_hi[:, 6:8, :], ot[:, :, :], ACT.Copy).then_inc(hghi, 1)

                def front(job):
                    bk = BK[4 * (job % 2):4 * (job % 2) + 4]
                    a_ = at_a[job % 2]
                    zb = NZT * l + Z_BASE[job]
                    if job < 2:
                        act.wait_ge(hgo_r, l + 1)
                        act.wait_ge(hghi, l + 1)
                        act.wait_ge(mixlo_r, 4 * (l + 1))
                        for j in range(3):
                            act.wait_ge(z_d, zb + j + 1)
                            nk = P if j < 2 else DEC
                            link(A(a_[0:nk, j * 512:j * 512 + SW], bk[j][0:nk, 0:SW], ACT.Abs))
                        full = a_[:, 0:1024].rearrange("p (j n) -> p j n", j=2)[:, :, 0:SW]
                        own = a_[0:DEC, 1024:1024 + SW]
                        link(A(full, full, ACT.Exp, scale=-1.0))
                        link(A(own, own, ACT.Exp, scale=-1.0))
                        A(full, full, ACT.Ln, bias=1.0).then_inc(l_r, 1)
                        A(own, own, ACT.Ln, bias=1.0).then_inc(l_r, 1)
                    else:
                        for j in range(NCH):
                            act.wait_ge(z_d, zb + j + 1)
                            link(A(a_[:, W_OFF[j]:W_OFF[j] + SEQ - j * P], bk[j][:, 0:SEQ - j * P], ACT.Abs))
                        link(A(a_[:, 0:1280], a_[:, 0:1280], ACT.Exp, scale=-1.0))
                        A(a_[:, 0:1280], a_[:, 0:1280], ACT.Ln, bias=1.0).then_inc(l_r, 2)

                def back(job):
                    bk = BK[4 * (job % 2):4 * (job % 2) + 4]
                    w = at_w[job % 2]
                    rb = NZT * l + Z_BASE[job]
                    nj = tiles_of(job)
                    for n, j in enumerate(reversed(range(nj))):
                        act.wait_ge(r_d, rb + n + 1)
                        if job < 2:
                            nk = P if j < 2 else DEC
                            A(w[0:nk, j * 512:j * 512 + SW], bk[j][0:nk, 0:SW], ACT.Exp).then_inc(wx_r, 1)
                        else:
                            A(w[:, W_OFF[j]:W_OFF[j] + SEQ - j * P], bk[j][:, 0:SEQ - j * P], ACT.Exp).then_inc(wx_r, 1)

                def evac(job):
                    bk = BK[4 * (job % 2) + 3]
                    act.wait_ge(av_d, NJ * l + job + 1)
                    if job < 2:
                        A(mix_hi[64 * job:64 * job + 64, 0:4, SEQ:T], bk[64 * job:64 * job + 64, 0:256].rearrange("p (q t) -> p q t", q=4), ACT.Copy).then_inc(avhi_r, 1)
                    else:
                        e, p_ = 64 * (job % 2), (job - 2) // 2
                        A(mix_hi[e:e + 64, p_, 0:SEQ], bk[e:e + 64, :], ACT.Copy).then_inc(avhi_r, 1)

                front(0)
                for job in range(NJ):
                    if job + 1 < NJ:
                        front(job + 1)
                    back(job)
                    evac(job)
                a = unit_base(l, "OUT")
                pn = 4 * l + 1
                act.wait_ge(mem_l, 16 * (l + 1))
                for b in range(2):
                    A(mk_s[:, 4 * b:4 * b + 4, :].rearrange("p k n -> p (k n)"), mtok[:, b, :], ACT.Square,
                      accum_out=mss[:, b:b + 1]).then_inc(mss_r, 1)
                act.wait_ge(mss_r, 2 * (l + 1))
                A(mss, mss, ACT.Sqrt, scale=1.0 / D, bias=eps).then_inc(mrs_r, 1)
                for m in range(KD):
                    step(a + m + 1)
                    post_square(pn, m)
                act.wait_ge(tile_e, tile_base(l, "OUT"))
                root(2 * pn + 1)
                for n in range(4):
                    act.wait_ge(mt_d, 4 * l + n + 1)
                    for q in range(2):
                        ins = A(m_hi[:, 2 * n + q, :], BK[2 + n % 2][:, q * 256:(q + 1) * 256], ACT.Copy, scale=gmem(l, 2 * n + q))
                    ins.then_inc(mhi_r, 1)
                a = unit_base(l, "MK")
                for m in range(2 * KD):
                    if m < KD:
                        pre_piece(pn + 1, m)
                    step(a + m + 1)
                    s = m % 2
                    if m < KD:
                        A(mk_p[:, m, :], PL[s][:, 0, 0:NMEM], ACT.Copy).then_inc(mkv_e, 1)
                    else:
                        A(mv_p[:, :, (m - KD) * P:(m - KD + 1) * P], PL[s][:, :, 0:P], ACT.Copy).then_inc(mkv_e, 1)
                pn = 4 * l + 2
                a = unit_base(l, "MQ")
                root(2 * pn)
                for m in range(KD):
                    step(a + m + 1)
                for n in range(4):
                    act.wait_ge(ck_d, 4 * l + n + 1)
                    A(mk_s[:, 2 * n:2 * n + 2, :], BK[2 + n % 2].rearrange("p (q t) -> p q t", q=2), ACT.Copy).then_inc(ck_e, 1)
                for n in range(4):
                    act.wait_ge(kr_d, 4 * l + n + 1)
                    A(mtok[:, n // 2, (n % 2) * 512:(n % 2 + 1) * 512], BK[2 + n % 2], ACT.Copy).then_inc(kr_e, 1)
                def x_exp(b):
                    nt, c0 = rows(b), 4 * (b % 2)
                    act.wait_ge(mx_r, NXA * l + b + 1)
                    for h in range(MH):
                        A(pr[b % 2][0:nt, h, :], PL[b % 2][0:nt, h // 2, (h % 2) * NMEM:(h % 2 + 1) * NMEM], ACT.Exp,
                          scale=1.0 / 16.0, bias=mx[0:nt, c0 + h:c0 + h + 1], accum_out=rsum[0:nt, c0 + h:c0 + h + 1]).then_inc(xe_r, 1)

                def x_keep(b):
                    nt = rows(b)
                    act.wait_ge(pt_d, NXA * l + b + 1)
                    A(pT[:, :, b * P:b * P + nt], PX[b % 2][:, :, :].rearrange("p a (q t) -> p (a q) t", q=4)[:, :, 0:nt],
                      ACT.Copy).then_inc(pt_e, 1)

                for b in range(NXA):
                    if b >= 2:
                        act.wait_ge(pt_d, NXA * l + b - 1)
                    x_exp(b)
                    if b:
                        x_keep(b - 1)
                x_keep(NXA - 1)
                for n in range(8):
                    act.wait_ge(xa_d, 8 * l + n + 1)
                    A(xo_hi[:, n, 0:SEQ], PL[n % 2][:, 0, :], ACT.Copy).then_inc(xahi_r, 1)
                    A(xo_hi[:, n, SEQ:T], PL[n % 2][:, 1, 0:DEC], ACT.Copy).then_inc(xahi_r, 1)
                a = unit_base(l, "MO")
                for m in range(KD):
                    step(a + m + 1)
                    post_square(pn, m)
                act.wait_ge(tile_e, tile_base(l, "MO"))
                root(2 * pn + 1)
                for k in range(KD):
                    pre_piece(4 * l + 3, k)
                ffn(l, "F2", "D2", 4 * l + 3, 2 * l + 1)
                if l + 1 < DEPTH:
                    for k in range(KD):
                        pre_piece(4 * l + 4, k)
            for n in range(2 * NXA):
                b, half = n // 2, n % 2
                act.wait_ge(yt_d, n + 1)
                A(xtok[0:rows(b), b, half * 512:(half + 1) * 512], BK[n % 4][0:rows(b), :], ACT.Copy).then_inc(yt_e, 1)

        @block.vector
        def _(v):
            TT, TS, STT = nc.vector.tensor_tensor, nc.vector.tensor_scalar, nc.vector.scalar_tensor_tensor
            chain = [0]

            def link(ins):
                chain[0] += 1
                ins.then_inc(dch, 1)
                v.wait_ge(dch, chain[0])

            f32 = lambda ap: ap.bitcast(F32)

            def split(u, s, words):
                v.wait_ge(whi_r, u + 1)
                TT(w_lo[:, s, 0:words], raw[:, s, 0:words], f32(w_hi[:, s, 0:words]), ALU.subtract).then_inc(wlo_r, 1)

            def step(u):
                v.wait_ge(unit_d, u)
                if u + 1 < NU:
                    split(u + 1, (u + 1) % 2, unit_words(u + 1))

            def h_lo_piece(pn, k):
                v.wait_ge(hi_r, KD * pn + k + 1)
                STT(h_lo[:, k, :], x[:, k, :], gpre(pn // 4, pn % 4, k), f32(h_hi[:, k, :]), ALU.mult, ALU.subtract).then_inc(lo_r, 1)

            def reciprocal(n):
                v.wait_ge(rs_r, n + 1)
                nc.vector.reciprocal(rinv[:, :], rinv[:, :]).then_inc(rinv_r, 1)
                v.wait_ge(rinv_r, n + 1)

            def y_tile(l, pn, m):
                v.wait_ge(sq_r, KD * (2 * pn + 1) + m + 1)
                TS(halves(y[:, m, :]), PL[m % 2][:, :, 0:HT], gpost(l, pn % 4, m), None, ALU.mult).then_inc(tile_e, 1)

            def update(pn, k, weight):
                TT(y[:, k, :], y[:, k, :], rinv[:, :], ALU.mult).then_inc(y_r, 1)
                v.wait_ge(y_r, KD * pn + k + 1)
                STT(x[:, k, :], y[:, k, :], weight, x[:, k, :], ALU.mult, ALU.add).then_inc(x_r, 1)

            def ffn(l, pu, pd, pn, f):
                a = unit_base(l, pu)
                reciprocal(2 * pn)

                def pair(r, words):
                    v.wait_ge(unit_d, r * 2 + (a + 1))
                    split(r * 2 + (a + 2), 0, words)
                    TT(halves(gt[:, :]), PL[0][:, :, 0:HT], halves(rinv[:, :]), ALU.mult).then_inc(tile_e, 1)
                    v.wait_ge(unit_d, r * 2 + (a + 2))
                    split(r * 2 + (a + 3), 1, words)
                    TT(halves(ut[:, :]), PL[1][:, :, 0:HT], halves(rinv[:, :]), ALU.mult).then_inc(tile_e, 1)
                    v.wait_ge(tile_e, r * 2 + (tile_base(l, pu) + 2))
                    v.wait_ge(sg_r, r + (KF * f + 1))
                    TT(ut[:, :], ut[:, :], sg[:, :], ALU.mult).then_inc(pr_r, 1)
                    v.wait_ge(ahi_r, r + (KF * f + 1))
                    o1 = "p (o t) -> p o t"
                    TT(a_lo[:, bass.ds(r, 1), :], ut[:, :].rearrange(o1, o=1), f32(a_hi[:, bass.ds(r, 1), :]), ALU.subtract).then_inc(alo_r, 1)

                with v.Fori(0, KF - 1) as r:
                    pair(r, KD * P)
                pair(KF - 1, KU * P)
                b = unit_base(l, pd)
                for u in range(b + 1, b + 2 * KD + 1):
                    step(u)
                    if (u - b) % 2 == 0:
                        y_tile(l, pn, (u - b) // 2 - 1)
                reciprocal(2 * pn + 1)

            nc.vector.memset(eps, EPS).then_inc(dch, 1)
            chain[0] += 1
            v.wait_ge(dch, chain[0])
            split(0, 0, unit_words(0))
            split(1, 1, unit_words(1))
            v.wait_ge(par_d, 1)
            nc.vector.tensor_copy(lmask[:, :, :], lst[:, :, :])
            nc.vector.tensor_copy(par[:, 0:128], BK[0][:, 0:128]).then_inc(par_r, 1)
            nc.vector.tensor_copy(par[:, 128:164], BK[1][:, 0:36]).then_inc(par_r, 1)
            v.wait_ge(par_r, 2)
            link(TT(lt[:, 0:2], par[:, 156:158], par[:, 158:160], ALU.max))
            link(TT(lt[:, 2:4], par[:, 156:158], lt[:, 0:2], ALU.subtract))
            TT(lt[:, 4:6], par[:, 158:160], lt[:, 0:2], ALU.subtract).then_inc(par_r, 1)
            v.wait_ge(par_r, 4)
            link(TT(lt[:, 6:8], lt[:, 2:4], lt[:, 4:6], ALU.add))
            link(nc.vector.reciprocal(lt[:, 8:10], lt[:, 6:8]))
            link(TT(lt[:, 2:4], lt[:, 2:4], lt[:, 8:10], ALU.mult))
            link(TT(lt[:, 4:6], lt[:, 4:6], lt[:, 8:10], ALU.mult))
            link(TT(lbv[:, 0:2], lt[:, 2:4], lt[:, 2:4], ALU.subtract))
            link(TT(lt[:, 10:12], lt[:, 2:4], lt[:, 4:6], ALU.add))
            link(TT(lbv[:, 2:4], lt[:, 10:12], lt[:, 2:4], ALU.subtract))
            link(TS(oml, lbv, -1.0, 1.0, ALU.mult, ALU.add))
            for k in range(KD):
                v.wait_ge(xt_d, k + 1)
                link(nc.vector.tensor_copy(x[:, k, 0:SEQ], PL[k % 2][:, 0, :]))
                nc.vector.tensor_copy(x[:, k, SEQ:T], PL[k % 2][:, 1, 0:DEC]).then_inc(x_r, 1)
            for k in range(KD):
                h_lo_piece(0, k)
            for l in range(DEPTH):
                ffn(l, "F1", "D1", 4 * l, 2 * l)
                for k in range(KD):
                    update(4 * l, k, 0.5)
                    if k:
                        h_lo_piece(4 * l + 1, k - 1)
                h_lo_piece(4 * l + 1, KD - 1)
                pn = 4 * l + 1
                a = unit_base(l, "IN")
                for m in range(NIN):
                    step(a + m + 1)
                    if m == 0:
                        reciprocal(2 * pn)
                    STT(halves(proj[:, IN_PLACE[m], :]), PL[m % 2][:, :, 0:HT], 0.125 if m < 4 else 1.0, halves(rinv[:, :]),
                        ALU.mult, ALU.mult).then_inc(tile_e, 1)
                v.wait_ge(tile_e, tile_base(l, "IN") + NIN)
                v.wait_ge(conv_l, 16 * 2 * (l + 1))
                for c in range(2):
                    link(nc.vector.memset(cu[:, c, 0:2], 0.0))
                    link(TT(cu[:, c, 2:2 + SEQ], proj[:, C0 + c, 0:SEQ], proj[:, H0 + c, 0:SEQ], ALU.mult))
                    TT(cu[:, c, 4 + SEQ:4 + T], proj[:, C0 + c, SEQ:T], proj[:, H0 + c, SEQ:T], ALU.mult).then_inc(cu_r, 1)
                    v.wait_ge(cu_r, 2 * l + c + 1)
                    for s0, c0, n in ((0, 0, SEQ), (SEQ + 2, SEQ, DEC)):
                        link(TS(ct[:, c, c0:c0 + n], cu[:, c, s0:s0 + n], cw(l, 0, c), None, ALU.mult))
                        for j in (1, 2):
                            link(STT(ct[:, c, c0:c0 + n], cu[:, c, s0 + j:s0 + j + n], cw(l, j, c), ct[:, c, c0:c0 + n], ALU.mult, ALU.add))
                link(TT(ct[:, 0, :], ct[:, 0, :], proj[:, B0, :], ALU.mult))
                TT(ct[:, 1, :], ct[:, 1, :], proj[:, B0 + 1, :], ALU.mult).then_inc(cvr, 1)
                v.wait_ge(cvhi, l + 1)
                for c in range(2):
                    TT(mix_lo[:, 4 + c, :], ct[:, c, :], f32(mix_hi[:, 4 + c, :]), ALU.subtract).then_inc(mixlo_r, 1)
                v.wait_ge(kout_s, 16 * 2 * (l + 1))
                link(nc.vector.memset(ones_w[:, :], 1.0))
                v.wait_ge(sig_r, 2 * (l + 1))
                for c in range(2):
                    n = 2 * l + c
                    link(TS(kf[:, c, :], kf[:, c, :], oml[:, n:n + 1], None, ALU.mult))
                    link(TS(bT[:, c, :], bT[:, c, :], oml[:, n:n + 1], lbv[:, n:n + 1], ALU.mult, ALU.add))
                link(TS(bT[:, :, :], bT[:, :, :], F_FLOOR, None, ALU.max))
                link(TS(hK[:, :, :], bT[:, :, :], LN_SPLIT, None, ALU.min))
                TS(bT[:, :, :], bT[:, :, :], LN_SPLIT, None, ALU.max).then_inc(f_r, 1)
                v.wait_ge(ln_r, 2 * (l + 1))
                link(TT(hE[:, :, :], hE[:, :, :], hQ[:, :, :], ALU.add))
                for c in range(2):
                    for b in range(NXA):
                        c0, n = b * P, rows(b)
                        link(nc.vector.tensor_tensor_scan(bT[:, c, c0:c0 + n], ones_w[:, 0:n], hE[:, c, c0:c0 + n], 0.0, ALU.mult, ALU.add))
                link(nc.vector.memset(sacc[:, :], 0.0))
                link(nc.vector.memset(itok[DEC:P, NCH, :], 0.0))
                n = [0]

                def keep(lev):
                    for c in range(NXA if lev < LEVELS - 1 else NCH):
                        v.wait_ge(sc_d, (5 * LEVELS - 1) * l + n[0] + 1)
                        nt = rows(c)
                        nc.vector.copy_predicated(
                            sacc[0:nt, c * 512:c * 512 + 4 * nt].rearrange("p (e j t) -> p e j t", e=2, j=2),
                            lmask[0:nt, lev:lev + 1, 0:nt].rearrange("p (a o) t -> p a o t", a=1).broadcast_to([nt, 2, 2, nt]),
                            PAIR[n[0] % 4][0:nt, :, 0:2 * nt].rearrange("p e (j t) -> p e j t", j=2)).then_inc(sc_e, 1)
                        n[0] += 1
                        v.wait_ge(sc_e, (5 * LEVELS - 1) * l + n[0])

                q_, k_ = proj[:, HQ0:HQ0 + 2, :], kf[:, :, :]
                ec = (LEVELS + 1) * l
                for lev in range(1, LEVELS):
                    w = 1 << lev
                    if lev < LEVELS - 1:
                        bb = bT[:, :, :].rearrange("p c (n w) -> p (c n) w", w=w)
                        TT(hE[:, :, :].rearrange("p c (n w) -> p (c n) w", w=w), bb,
                           bb[:, :, w // 2 - 1:w // 2].broadcast_to([P, 2 * T // w, w]), ALU.subtract).then_inc(e_in, 1)
                    else:
                        for c in range(2):
                            bb = bT[:, c, 0:SEQ].rearrange("p (n w) -> p n w", w=w)
                            ins = TT(hE[:, c, 0:SEQ].rearrange("p (n w) -> p n w", w=w), bb,
                                     bb[:, :, w // 2 - 1:w // 2].broadcast_to([P, NCH, w]), ALU.subtract)
                            link(ins) if c == 0 else ins.then_inc(e_in, 1)
                    keep(lev - 1)
                    v.wait_ge(e_r, ec + lev)
                    link(TT(hQ[:, :, :], q_, hE[:, :, :], ALU.mult))
                    TT(hK[:, :, :], k_, hE[:, :, :], ALU.mult).then_inc(qk_r, 1)
                    v.wait_ge(qk_r, (LEVELS - 1) * l + lev)
                keep(LEVELS - 1)
                v.wait_ge(sc_d, (5 * LEVELS - 1) * (l + 1))
                v.wait_ge(e_r, ec + LEVELS)
                link(TT(hQ[:, :, :], q_, hE[:, :, :], ALU.mult))
                for c in range(2):
                    link(nc.vector.tensor_copy(ebl[:, 5 * c:5 * c + 4], hE[:, c, P - 1:SEQ:P]))
                    link(nc.vector.tensor_copy(ebl[:, 5 * c + 4:5 * c + 5], hE[:, c, T - 1:T]))
                for c in range(2):
                    bb = bT[:, c, 0:SEQ].rearrange("p (n w) -> p n w", w=P)
                    link(TT(hE[:, c, 0:SEQ].rearrange("p (n w) -> p n w", w=P), bb, bb[:, :, P - 1:P].broadcast_to([P, NCH, P]), ALU.subtract))
                    ins = TS(hE[:, c, SEQ:T], bT[:, c, SEQ:T], bT[:, c, T - 1:T], None, ALU.subtract)
                    link(ins) if c == 0 else ins.then_inc(e_in, 1)
                v.wait_ge(e_r, ec + LEVELS + 1)
                TT(hK[:, :, :], k_, hE[:, :, :], ALU.mult).then_inc(kk_r, 1)
                v.wait_ge(kk_r, l + 1)
                v.wait_ge(s0_l, 16 * (l + 1))
                for c in range(NXA):
                    v.wait_ge(hs_d, NXA * l + c + 1)
                    sbk = BK[6 + c % 2]
                    if c == 0:
                        nc.vector.tensor_copy(st_p[:, :, :], sbk[:, 0:P].rearrange("p (j t) -> p j t", j=2)).then_inc(hs_r, 1)
                    else:
                        st = st_p if c < NCH else st_s
                        v.wait_ge(ho_d, NXA * l + c + 1)
                        link(STT(st[:, 0, :], st[:, 0, :], ebl[:, c:c + 1], sbk[:, 0:64], ALU.mult, ALU.add))
                        STT(st[:, 1, :], st[:, 1, :], ebl[:, 5 + c:6 + c], sbk[:, 64:128], ALU.mult, ALU.add).then_inc(hs_r, 1)
                    v.wait_ge(hs_r, NXA * l + c + 1)
                v.wait_ge(ors_r, 3 * (l + 1))
                link(nc.vector.reciprocal(hQ[:, :, :], hQ[:, :, :]))
                for c in range(2):
                    link(STT(ot[:, c, :], ot[:, c, :], gh(l, c), hQ[:, c, :], ALU.mult, ALU.mult))
                v.wait_ge(hst_s, 32 * (l + 1))
                TT(ot[:, :, :], ot[:, :, :], hK[:, :, :], ALU.mult).then_inc(hgo_r, 1)
                v.wait_ge(hghi, l + 1)
                for c in range(2):
                    TT(mix_lo[:, 6 + c, :], ot[:, c, :], f32(mix_hi[:, 6 + c, :]), ALU.subtract).then_inc(mixlo_r, 1)

                def softplus(job):
                    bk = BK[4 * (job % 2):4 * (job % 2) + 4]
                    a_, s_ = at_a[job % 2], at_s[job % 2]
                    v.wait_ge(l_r, 2 * NJ * l + 2 * job + 2)
                    if job >= 2:
                        v.wait_ge(wx_r, NZT * l + Z_BASE[job - 1])
                    for j in range(tiles_of(job)):
                        if job < 2:
                            nk = P if j < 2 else DEC
                            STT(s_[0:nk, j * 512:j * 512 + SW], bk[j][0:nk, 0:SW], 0.0, a_[0:nk, j * 512:j * 512 + SW],
                                ALU.max, ALU.add).then_inc(sp_r, 1)
                        else:
                            c0, n_ = W_OFF[j], SEQ - j * P
                            STT(s_[:, c0:c0 + n_], bk[j][:, 0:n_], 0.0, a_[:, c0:c0 + n_], ALU.max, ALU.add).then_inc(sp_r, 1)

                def evac(job):
                    bk = BK[4 * (job % 2) + 3]
                    v.wait_ge(avhi_r, NJ * l + job + 1)
                    if job < 2:
                        r_ = slice(64 * job, 64 * job + 64)
                        TT(mix_lo[r_, 0:4, SEQ:T], bk[r_, 0:256].rearrange("p (q t) -> p q t", q=4), f32(mix_hi[r_, 0:4, SEQ:T]),
                           ALU.subtract).then_inc(avlo_r, 1)
                    else:
                        e, p_ = 64 * (job % 2), (job - 2) // 2
                        TT(mix_lo[e:e + 64, p_, 0:SEQ], bk[e:e + 64, :], f32(mix_hi[e:e + 64, p_, 0:SEQ]), ALU.subtract).then_inc(avlo_r, 1)

                softplus(0)
                for job in range(NJ):
                    if job + 1 < NJ:
                        softplus(job + 1)
                    evac(job)
                pn = 4 * l + 1
                a = unit_base(l, "OUT")
                v.wait_ge(mrs_r, l + 1)
                link(nc.vector.reciprocal(mss, mss))
                for b in range(2):
                    ins = TS(mtok[:, b, :], mtok[:, b, :], mss[:, b:b + 1], None, ALU.mult)
                    link(ins) if b == 0 else ins.then_inc(mn_r, 1)
                for m in range(KD):
                    step(a + m + 1)
                    y_tile(l, pn, m)
                reciprocal(2 * pn + 1)
                for n_ in range(4):
                    v.wait_ge(mhi_r, 4 * l + n_ + 1)
                    for q in range(2):
                        k = 2 * n_ + q
                        ins = STT(m_lo[:, k, :], BK[2 + n_ % 2][:, q * 256:(q + 1) * 256], gmem(l, k), f32(m_hi[:, k, :]), ALU.mult, ALU.subtract)
                    ins.then_inc(mlo_r, 1)
                a = unit_base(l, "MK")
                for m in range(2 * KD):
                    if m < KD:
                        update(pn, m, 1.0)
                    step(a + m + 1)
                    if m < KD:
                        h_lo_piece(pn + 1, m)
                pn = 4 * l + 2
                a = unit_base(l, "MQ")
                for m in range(KD):
                    step(a + m + 1)
                    if m == 0:
                        reciprocal(2 * pn)
                    TT(halves(qx[:, m, :]), PL[m % 2][:, :, 0:HT], halves(rinv[:, :]), ALU.mult).then_inc(tile_e, 1)
                def x_max(b):
                    nt, c0 = rows(b), 4 * (b % 2)
                    v.wait_ge(xs_d, NXA * l + b + 1)
                    link(nc.vector.tensor_reduce(mx[0:nt, c0:c0 + 4],
                                                 PL[b % 2][0:nt, :, :].rearrange("p a (q n) -> p (a q) n", q=2), AX.X, ALU.max))
                    TS(mx[0:nt, c0:c0 + 4], mx[0:nt, c0:c0 + 4], -1.0 / 16.0, None, ALU.mult).then_inc(mx_r, 1)

                def x_norm(b):
                    nt, c0 = rows(b), 4 * (b % 2)
                    v.wait_ge(xe_r, 4 * (NXA * l + b + 1))
                    link(nc.vector.reciprocal(rrec[0:nt, c0:c0 + 4], rsum[0:nt, c0:c0 + 4]))
                    for h in range(MH):
                        TS(pr[b % 2][0:nt, h, :], pr[b % 2][0:nt, h, :], rrec[0:nt, c0 + h:c0 + h + 1], None, ALU.mult).then_inc(pn_r, 1)

                x_max(0)
                for b in range(NXA):
                    if b + 1 < NXA:
                        x_max(b + 1)
                    x_norm(b)
                for n_ in range(8):
                    v.wait_ge(xahi_r, 2 * (8 * l + n_ + 1))
                    link(TT(xo_lo[:, n_, 0:SEQ], PL[n_ % 2][:, 0, :], f32(xo_hi[:, n_, 0:SEQ]), ALU.subtract))
                    TT(xo_lo[:, n_, SEQ:T], PL[n_ % 2][:, 1, 0:DEC], f32(xo_hi[:, n_, SEQ:T]), ALU.subtract).then_inc(xalo_r, 1)
                a = unit_base(l, "MO")
                for m in range(KD):
                    step(a + m + 1)
                    y_tile(l, pn, m)
                reciprocal(2 * pn + 1)
                for k in range(KD):
                    update(pn, k, 1.0)
                    if k:
                        h_lo_piece(pn + 1, k - 1)
                h_lo_piece(pn + 1, KD - 1)
                ffn(l, "F2", "D2", 4 * l + 3, 2 * l + 1)
                for k in range(KD):
                    update(4 * l + 3, k, 0.5)
                    if k and l + 1 < DEPTH:
                        h_lo_piece(4 * l + 4, k - 1)
                if l + 1 < DEPTH:
                    h_lo_piece(4 * l + 4, KD - 1)

        @block.gpsimd
        def _(pool):
            def add_squares(n):
                if n:
                    pool.wait_ge(ms_r, n)
                for k in range(KD):
                    c = KD * n + k
                    pool.wait_ge(sq_r, c + 1)
                    if k == 0:
                        nc.gpsimd.tensor_copy(acc[:, :], sq[:, 0, :]).then_inc(acc_r, 1)
                    else:
                        pool.wait_ge(acc_r, c)
                        nc.gpsimd.tensor_tensor(acc[:, :], acc[:, :], sq[:, k % 2, :], ALU.add).then_inc(acc_r, 1)

            dma = pool.dma_start
            dma(cst[:, :, :], i["cf"].rearrange("n p m -> p n m")).then_inc(cst_l, 16)
            dma(lst[:, :, :], i["lm"].rearrange("n p m -> p n m")).then_inc(cst_l, 16)
            dma(gst1[0:64, :], i["norm_pre"].rearrange("l n (k p) -> (l n k) p", p=P)).then_inc(cst_l, 16)
            dma(gst1[64:128, :], i["norm_post"].rearrange("l n (k p) -> (l n k) p", p=P)).then_inc(cst_l, 16)
            dma(gst2[0:16, :], i["mem_norm"].rearrange("l (k p) -> (l k) p", p=P)).then_inc(cst_l, 16)
            dma(gst2[16:28, :], i["conv_w"].rearrange("l j (k p) -> (l j k) p", p=P)).then_inc(cst_l, 16)
            dma(gst2[28:32, :], i["hg_lb"].rearrange("l (k p) -> (l k) p", p=P)).then_inc(cst_l, 16)
            dma(gst2[32:36, :], i["hg_norm"].rearrange("l (k p) -> (l k) p", p=P)).then_inc(cst_l, 16)
            dma(xtok[:, 0:NCH, :], i["x_prompt"][0].rearrange("(b p) d -> p b d", p=P)).then_inc(xin_l, 16)
            dma(xtok[0:DEC, NCH, :], i["x_sample"][0]).then_inc(xin_l, 16)
            add_squares(0)
            for l in range(DEPTH):
                add_squares(8 * l + 1)
                add_squares(8 * l + 2)
                pool.wait_ge(tile_e, tile_base(l, "IN"))
                dma(kpast_tok[:, :, :], i["cache_sb_k"][l, 0].rearrange("(b p) h d -> p b (h d)", p=P)).then_inc(cache_l, 16)
                dma(vpast[:, :, :], i["cache_sb_v"][l, 0].rearrange("(b p) h d -> p b (h d)", p=P)).then_inc(cache_l, 16)
                pool.wait_ge(unit_d, unit_base(l, "IN") + NIN)
                for c in range(2):
                    with nc.allow_non_contiguous_dma(reason="two rows of the convolution's state, feature-major"):
                        dma(cu[:, c, SEQ + 2:SEQ + 4], i["state_conv"][l, 0][:, c * P:(c + 1) * P].rearrange("r p -> p r")).then_inc(conv_l, 16)
                pool.wait_ge(tp_e, 17 * l + NXA)
                dma(o["sb_k_p"][l, 0].rearrange("(b p) h d -> p b (h d)", p=P), ktok[:, 0:NCH, :]).then_inc(kout_s, 16)
                dma(o["sb_k_s"][l, 0].rearrange("p h d -> p (h d)"), ktok[0:DEC, NCH, :]).then_inc(kout_s, 16)
                pool.wait_ge(tp_e, 17 * l + 2 * NXA)
                dma(o["sb_v_p"][l, 0].rearrange("(b p) h d -> p b (h d)", p=P), vtok[:, 0:NCH, :]).then_inc(y_s, 16)
                dma(o["sb_v_s"][l, 0].rearrange("p h d -> p (h d)"), vtok[0:DEC, NCH, :]).then_inc(y_s, 16)
                pool.wait_ge(cu_r, 2 * (l + 1))
                for c in range(2):
                    with nc.allow_non_contiguous_dma(reason="two rows of the convolution's state, feature-major"):
                        dma(o["conv_p"][l, 0][:, c * P:(c + 1) * P].rearrange("r p -> p r"), cu[:, c, SEQ:SEQ + 2]).then_inc(mixst_s, 16)
                        dma(o["conv_s"][l, 0][:, c * P:(c + 1) * P].rearrange("r p -> p r"), cu[:, c, T + 2:T + 4]).then_inc(mixst_s, 16)
                dma(st_s[:, :, :], i["state_hgrn"][l, 0].rearrange("(j e) k v -> (e k) j v", j=2)).then_inc(s0_l, 16)
                pool.wait_ge(hs_r, NXA * (l + 1))
                dma(o["hg_p"][l, 0].rearrange("(j e) k v -> (e k) j v", j=2), st_p[:, :, :]).then_inc(hst_s, 16)
                dma(o["hg_s"][l, 0].rearrange("(j e) k v -> (e k) j v", j=2), st_s[:, :, :]).then_inc(hst_s, 16)

                def mask(buf, job, done):
                    if job < 2:
                        ap = buf[0:DEC, 1024:1024 + SW].rearrange("p (h t) -> p h t", t=DEC)
                        nc.gpsimd.affine_select(out=ap, in_=ap, compare_op=ALU.is_gt, fill=0.0, base=0,
                                                pattern=[[0, SBH // 2], [1, DEC]], channel_multiplier=-1).then_inc(done, 1)
                        return
                    for c in W_OFF:
                        nc.gpsimd.affine_select(out=buf[:, c:c + P], in_=buf[:, c:c + P], compare_op=ALU.is_gt, fill=0.0,
                                                base=0, pattern=[[1, P]], channel_multiplier=-1).then_inc(done, 1)

                for job in range(NJ):
                    pool.wait_ge(sp_r, NZT * l + Z_BASE[job + 1])
                    mask(at_s[job % 2], job, spm_r)
                    if job:
                        pool.wait_ge(wx_r, NZT * l + Z_BASE[job])
                        mask(at_w[(job - 1) % 2], job - 1, wm_r)
                pool.wait_ge(wx_r, NZT * (l + 1))
                mask(at_w[1], NJ - 1, wm_r)
                pool.wait_ge(avlo_r, NJ * (l + 1))
                pool.wait_ge(avhi_r, NJ * (l + 1))
                pool.wait_ge(mixlo_r, 4 * (l + 1))
                pool.wait_ge(y_s, 48 * l + 32)
                dma(mtok[:, :, :], i["mem_prompt"][0].rearrange("(b p) d -> p b d", p=P)).then_inc(mem_l, 16)
                dma(mv_s[:, :, :], i["cache_mem_v"][l, 0].rearrange("(b p) h d -> p b (h d)", p=P)).then_inc(cv_l, 16)
                add_squares(8 * l + 3)
                pool.wait_ge(mt_d, 4 * (l + 1))
                dma(mtok[:, :, :], i["cache_mem_k"][l, 0].rearrange("(b p) h d -> p b (h d)", p=P)).then_inc(ck_l, 16)
                add_squares(8 * l + 4)
                pool.wait_ge(mkv_e, 16 * (l + 1))
                dma(o["mem_v"][l, 0].rearrange("(b p) h d -> p b (h d)", p=P), mv_p[:, :, :]).then_inc(y_s, 16)
                pool.wait_ge(kr_e, 4 * (l + 1))
                dma(o["mem_k"][l, 0].rearrange("(b p) h d -> p b (h d)", p=P), mtok[:, :, :]).then_inc(kr_s, 16)
                add_squares(8 * l + 5)
                pool.wait_ge(y_s, 48 * (l + 1))
                pool.wait_ge(kr_s, 16 * (l + 1))
                add_squares(8 * l + 6)
                add_squares(8 * l + 7)
                if l + 1 < DEPTH:
                    add_squares(8 * l + 8)
            pool.wait_ge(yt_e, 2 * NXA)
            dma(o["y_p"][0].rearrange("(b p) d -> p b d", p=P), xtok[:, 0:NCH, :]).then_inc(y_s, 16)
            dma(o["y_s"][0], xtok[0:DEC, NCH, :]).then_inc(y_s, 16)
            pool.wait_ge(y_s, 48 * DEPTH + 32)
            pool.wait_ge(kout_s, 32 * DEPTH)
            pool.wait_ge(mixst_s, 64 * DEPTH)
            pool.wait_ge(hst_s, 32 * DEPTH)
            pool.wait_ge(kr_s, 16 * DEPTH)


_INS = ["x_prompt", "x_sample", "mem_prompt", "cache_sb_k", "cache_sb_v", "cache_mem_k", "cache_mem_v", "state_conv",
        "state_hgrn", "norm_pre", "norm_post", "ffn1_gu", "ffn1_down", "w_in", "conv_w", "hg_lb", "hg_norm", "w_out",
        "mem_norm", "w_mk", "w_mv", "w_mq", "w_mo", "ffn2_gu", "ffn2_down"]
_OUTS = [("y_p", (1, SEQ, D)), ("y_s", (1, DEC, D)),
         ("sb_k_p", (DEPTH, 1, SEQ, SBH, HD)), ("sb_v_p", (DEPTH, 1, SEQ, SBH, HD)),
         ("conv_p", (DEPTH, 1, 2, 256)), ("hg_p", (DEPTH, 1, 4, 64, 64)),
         ("mem_k", (DEPTH, 1, NMEM, MH, MHD)), ("mem_v", (DEPTH, 1, NMEM, MH, MHD)),
         ("sb_k_s", (DEPTH, 1, DEC, SBH, HD)), ("sb_v_s", (DEPTH, 1, DEC, SBH, HD)),
         ("conv_s", (DEPTH, 1, 2, 256)), ("hg_s", (DEPTH, 1, 4, 64, 64))]


def constants():
    import numpy as np
    s, t = np.arange(P)[:, None], np.arange(P)[None, :]
    cf = np.stack([s == t, -1.0 * (s >= t), -np.ones((P, P)), np.ones((P, P)), s // 64 == t // 64]).astype(np.float32)
    lm = np.stack([s == t] + [((s ^ t) >> (n - 1) == 1) & (t > s) for n in range(1, LEVELS)]).astype(np.float32)
    return cf, lm


def kernel(**inputs):
    import numpy as _np
    import concourse.bacc as _bacc
    from concourse import mybir as _mybir
    from concourse.bass_utils import run_bass_kernel_spmd as _run

    nc = _bacc.Bacc("TRN2", target_bir_lowering=False, num_devices=1)
    arrays, ins, outs = {}, {}, {}
    given = {name: _np.ascontiguousarray(inputs[name]) for name in _INS}
    given["cf"], given["lm"] = constants()
    for name, a in given.items():
        arrays[f"in_{name}_dram"] = a
        ins[name] = nc.dram_tensor(f"in_{name}_dram", a.shape, _mybir.dt.from_np(a.dtype), kind="ExternalInput").ap()
    for n, (name, shape) in enumerate(_OUTS):
        outs[name] = nc.dram_tensor(f"out_{n}_dram", shape, _mybir.dt.from_np(_np.dtype("float32")), kind="ExternalOutput").ap()
    hybrid_trunk(nc, ins, outs)
    r = _run(nc, [arrays], core_ids=[0])
    return tuple(r.results[0][f"out_{n}_dram"] for n in range(len(_OUTS)))
```

```python
from contextlib import ExitStack

import concourse.bass as bass
from concourse import mybir

F32 = mybir.dt.float32
F32R = mybir.dt.float32r
BF16 = mybir.dt.bfloat16
U8 = mybir.dt.uint8
ALU = mybir.AluOpType
ACT = mybir.ActivationFunctionType
AX = mybir.AxisListType

P = 128
D = 1024
DEPTH = 2
KD = D // P
SEQ, DEC, PAST, NMEM = 512, 64, 256, 256
T = SEQ + DEC
HT = T // 2
FF = 2816
KF = FF // P
KU = KF // 2
SBH, HD = 8, 64
NCH = SEQ // P
EPS = 1e-6
F_FLOOR = 1e-30
NEG = -1e30
LN_SPLIT = 2.0 ** -60
MH, MHD = 4, 256

Q0, B0, HQ0, K0, C0, HF0, H0, HG0, V0, HI0 = 0, 4, 6, 8, 12, 14, 16, 18, 20, 24
IN_PLACE = ([HQ0, HQ0 + 1, HF0, HF0 + 1, HI0, HI0 + 1, HG0, HG0 + 1]
            + [Q0 + i for i in range(4)] + [K0 + i for i in range(4)] + [V0 + i for i in range(4)]
            + [B0, B0 + 1, C0, C0 + 1, H0, H0 + 1])
NHG = 8
NIN = len(IN_PLACE)

PHASES = [("F1", 2 * KF, KD), ("D1", 2 * KD, KU), ("IN", NIN, KD), ("OUT", KD, KD), ("MK", KD, KD),
          ("MVQ", 2 * KD, KD), ("MO", KD, KD), ("F2", 2 * KF, KD), ("D2", 2 * KD, KU)]
UNITS = sum(n for _, n, _ in PHASES)
TILES = {"F1": 2 * KF, "D1": KD, "IN": NIN, "OUT": KD, "MK": 0, "MVQ": KD, "MO": KD, "F2": 2 * KF, "D2": KD}
NT = sum(TILES.values())
Z_OFF = [0, SEQ, 2 * SEQ, 2 * SEQ - P]
ZW = 2 * SEQ + 2 * P
SW = SBH // 2 * DEC
LEVELS = 7
U_SIG, U_FORGET, U_LN, U_SCAN, U_GATE, U_ITOK, U_DIAG = 4, 5, 6, 7, 8, 9, 10
U_LEV = 8
U_KEND = U_LEV + LEVELS + 1
U_QDEC = U_KEND + 1
U_KTOK = U_KEND + 2
U_OUT = U_KTOK + 1
U_SQ, U_NORM = U_OUT + NCH, U_OUT + NCH + 1


def unit_base(l, phase):
    names = [p[0] for p in PHASES]
    return l * UNITS + sum(n for _, n, _ in PHASES[:names.index(phase)])


def tile_base(l, phase):
    names = [p[0] for p in PHASES]
    return l * NT + sum(TILES[n] for n in names[:names.index(phase)])


def unit_words(u):
    u %= UNITS
    for _, n, k in PHASES:
        if u < n:
            return k * P
        u -= n


def hybrid_trunk(nc, i, o):
    ctx = ExitStack()
    with ctx:
        def place(name, shape, dt, words):
            return nc.alloc_sbuf_tensor_at(name, shape, dt, offset=16512 + 4 * words)

        x = place("x", [P, KD, T], F32, 0)
        H = KD * T
        h_hi = place("h_hi", [P, KD, T], F32R, H)
        h_lo = place("h_lo", [P, KD, T], F32R, H + KD * T)
        y = place("y", [P, KD, T], F32, H + KD * T)
        G = H + 2 * KD * T
        a_hi = place("a_hi", [P, KF, T], F32R, G)
        a_lo = place("a_lo", [P, KF, T], F32R, G + KF * T)
        proj = place("proj", [P, NIN, T], F32, G)
        mix_hi = place("mix_hi", [P, KD, T], F32R, G)
        mix_lo = place("mix_lo", [P, KD, T], F32R, G + KD * T)
        g = G + NIN * T
        vtok = place("vtok", [P, NCH + 1, 512], F32, g)
        kpast = place("kpast", [P, 4, PAST], F32, g + 6144)
        vpast = place("vpast", [P, 2, 512], F32, g + 7168)
        kpast_tok = place("kpast_tok", [P, 2, 512], F32, g + 8192)
        cu = place("cu", [P, 2, T + 4], F32, H)
        ct = place("ct", [P, 2, T], F32, H + 1160)
        ktok = place("ktok", [P, NCH + 1, 512], F32, H + 4608)
        sacc = place("sacc", [P, 4 * SEQ], F32, g)
        kotok = place("kotok", [P, NCH + 1, 256], F32, g + 2048)
        hE = place("hE", [P, 2, T], F32, g + 3328)
        ot = place("ot", [P, 2, T], F32, g + 4480)
        kf = place("kf", [P, 2, T], F32, g + 5632)
        hQK = [place(f"hQK{s}", [P, 2, T], F32, g + 6784 + 1152 * s) for s in range(2)]
        itok = place("itok", [P, NCH + 1, 256], F32, g + 9088)
        at_a, at_s, at_w, at_c = ([place(f"at_{n}{s}", [P, w], F32, H + 4480 * s + w0) for s in range(2)]
                                  for n, w, w0 in (("a", ZW, 0), ("s", ZW, ZW), ("w", ZW, 2 * ZW), ("c", 640, 3 * ZW)))
        qx = place("qx", [P, KD, T], F32, G)
        xo_hi = place("xo_hi", [P, KD, T], F32R, G)
        xo_lo = place("xo_lo", [P, KD, T], F32R, G + 4608)
        mtok = place("mtok", [P, 2, D], F32, G + 9216)
        m_hi = place("m_hi", [P, KD, NMEM], F32R, G + 11264)
        m_lo = place("m_lo", [P, KD, NMEM], F32R, G + 13312)
        mk_p = place("mk_p", [P, KD, NMEM], F32, G + 15360)
        mv_p = place("mv_p", [P, 2, D], F32, G + 17408)
        mk_s = place("mk_s", [P, KD, NMEM], F32, G + 19456)
        mv_s = place("mv_s", [P, 2, D], F32, G + 21504)
        pr = [place(f"pr{s}", [P, MH, NMEM], F32, H + 1024 * s) for s in range(2)]
        pT = place("pT", [P, 8, T], F32, H + 2048)
        mvT = place("mvT", [P, KD, NMEM], F32, G + 4608)
        xtok = place("xtok", [P, NCH + 1, D], F32, G)
        gst1 = place("gst1", [P, P], F32, G + 5120)
        gst2 = place("gst2", [P, P], F32, G + 5248)
        lst = place("lst", [P, LEVELS + 1, P], F32, G + 5376)
        W = G + 2 * KF * T
        raw = place("raw", [P, 2, KU * P], F32, W)
        w_hi = place("w_hi", [P, 2, KU * P], F32R, W + 2 * KU * P)
        w_lo = place("w_lo", [P, 2, KU * P], F32R, W + 4 * KU * P)
        M = W + 6 * KU * P
        sq = place("sq", [P, 2, T], F32, M)
        gt = place("gt", [P, T], F32, M + 2 * T)
        sg = place("sg", [P, T], F32, M + 3 * T)
        ut = place("ut", [P, T], F32, M + 4 * T)
        bT = place("bT", [P, 2, T], F32, M + 2 * T)
        st_p = place("st_p", [P, 2, HD], F32, M + 4 * T)
        st_s = place("st_s", [P, 2, HD], F32, M + 4 * T + P)
        sacc_s = place("sacc_s", [P, 4 * DEC], F32, M + 4 * T + 2 * P)
        acc = place("acc", [P, T], F32, M + 5 * T)
        rinv = place("rinv", [P, T], F32, M + 6 * T)
        m0 = M + 7 * T
        cst = place("cst", [P, 5, P], F32, m0)
        lmask = place("lmask", [P, LEVELS, P], U8, m0 + 640)
        par = place("par", [P, 164], F32, m0 + 896)
        small = place("small", [P, 80], F32, m0 + 1064)
        identb = place("identb", [P, P], BF16, m0 + 1144)
        negb = place("negb", [P, P], BF16, m0 + 1208)
        ident, ntri, nones, ones, bones = (cst[:, n, :] for n in range(5))
        eps = small[:, 0:1]
        lbv = small[:, 1:5]
        oml = small[:, 5:9]
        lt = small[:, 9:21]
        mss = small[:, 21:23]
        mtk, rtok, ntk = small[:, 34:39], small[:, 39:44], small[:, 44:49]
        ebl = small[:, 24:34]
        mx = small[:, 49:57]
        rsum = small[:, 57:65]
        rrec = small[:, 65:73]

        PS = ctx.enter_context(nc.psum_tensor("PS", [P, 8, 512], F32))
        BK = [PS[:, n, :] for n in range(8)]
        PX = [PS[:, 2 * n:2 * n + 2, :] for n in range(2)]
        PL = [PS[:, 4 + 2 * n:6 + 2 * n, :] for n in range(2)]
        PAIR = PX + PL
        SET = [PS[:, 3 * n:3 * n + 3, :].rearrange("p b t -> p (b t)") for n in range(2)]

        def sem(name):
            return ctx.enter_context(nc.semaphore(name))

        cst_l = sem("cst_loaded")
        xin_l = sem("x_loaded")
        w_l = [sem(f"w_loaded{s}") for s in range(2)]
        whi_r, wlo_r = sem("w_hi_ready"), sem("w_lo_ready")
        unit_d = sem("unit_products_done")
        tile_e = sem("psum_tile_emptied")
        mkv_e = sem("memory_tile_emptied")
        sq_r, acc_r, ms_r, rs_r, mt_r, y0_r, rt_r, bc_d = (sem(n) for n in ("square_ready", "squares_added", "mean_square_ready",
                                                            "rinv_ready", "mean_squares_by_token", "root_estimated", "root_refined", "rinv_spread"))
        x_r, hi_r, lo_r, y_r = sem("x_ready"), sem("h_hi_ready"), sem("h_lo_ready"), sem("y_scaled")
        xt_d = sem("x_transposed")
        par_d, par_r = sem("gains_transposed"), sem("gains_ready")
        sg_r, ut_r, pr_r, ahi_r, alo_r = (sem(n) for n in ("silu_ready", "up_ready", "inner_ready",
                                                                 "a_hi_ready", "a_lo_ready"))
        dch, ach, pch = sem("vector_step"), sem("scalar_step"), sem("pool_step")
        cache_l, conv_l = sem("caches_loaded"), sem("conv_state_loaded")
        tp_d, tp_e = sem("token_major_done"), sem("token_major_emptied")
        kout_s = sem("k_rows_stored")
        mixst_s = sem("mix_outputs_stored")
        cu_r, cvr, cvhi = sem("conv_input_ready"), sem("conv_ready"), sem("conv_hi_ready")
        sig_r, f_r, ln_r = sem("sigmoids_ready"), sem("forget_ready"), sem("logs_ready")
        e_in, e_r, qk_r = sem("decay_exponent_ready"), sem("decay_ready"), sem("decayed_qk_ready")
        sc_d, sc_e = sem("scores_done"), sem("scores_kept")
        it_d, it_e, qk0_r, dg_d, dg_e, qd_r, hu_r = (sem(n) for n in (
            "i_transposed", "i_rows_ready", "qk_own_ready", "diagonal_done", "diagonal_used", "q_decayed", "newton_begun"))
        kk_r, kt_d, kt_e = sem("kout_ready"), sem("kout_transposed"), sem("kout_emptied")
        ho_d, ho_e, hs_d, hs_r = sem("hg_out_done"), sem("hg_out_emptied"), sem("hg_state_done"), sem("hg_state_ready")
        s0_l, hst_s = sem("hg_state_loaded"), sem("hg_state_stored")
        osq_r, oms_d, ors_r, hgo_r, hghi = (sem(n) for n in ("o_square_ready", "o_mean_done", "o_root_ready", "o_gated", "o_hi_ready"))
        mixlo_r = sem("mix_lo_ready")
        z_d, l_r, sp_r, sum_r, r_d, wx_r, av_d, avhi_r, avlo_r = (
            sem(n) for n in ("z_done", "log1p_ready", "softplus_ready", "later_tiles_summed", "rest_done", "weights_ready",
                             "attended", "attended_hi", "attended_lo"))
        mem_l, mss_r, mrs_r, mn_r, mt_d, mhi_r, mlo_r = (
            sem(n) for n in ("mem_loaded", "mem_squares", "mem_root", "mem_normed", "mem_transposed", "m_hi_ready", "m_lo_ready"))
        ck_l, cv_l, ck_d, ck_e, kr_d, kr_e, kr_s, mv_s_sem = (
            sem(n) for n in ("cache_k_loaded", "cache_v_loaded", "cache_k_transposed", "cache_k_emptied",
                             "k_rows_done", "k_rows_emptied", "mem_k_stored", "mem_v_stored"))
        qx_r = sem("queries_ready")
        xs_d, mx_r, xe_r, pn_r, pt_d, pt_e, xa_d, xahi_r, xalo_r = (
            sem(n) for n in ("x_scores_done", "x_max_ready", "x_exp_ready", "x_probs_ready", "probs_transposed",
                             "probs_emptied", "x_attended", "x_attended_hi", "x_attended_lo"))
        yt_d, yt_e, y_s = sem("y_transposed"), sem("y_emptied"), sem("y_stored")

        gpre = lambda l, n, k: par[:, (l * 4 + n) * 8 + k:(l * 4 + n) * 8 + k + 1]
        gpost = lambda l, n, k: par[:, 64 + (l * 4 + n) * 8 + k:64 + (l * 4 + n) * 8 + k + 1]
        gmem = lambda l, k: par[:, 128 + l * 8 + k:129 + l * 8 + k]
        cw = lambda l, j, c: par[:, 144 + l * 6 + j * 2 + c:145 + l * 6 + j * 2 + c]
        gh = lambda l, c: par[:, 160 + l * 2 + c:161 + l * 2 + c]

        added = lambda n: (2 * KD - 3) * (n // 2) + (KD - 1) * (n % 2)
        def part(ap, n, second):
            w = 1 << n
            c0 = w // 2 * second
            if n < LEVELS:
                return ap[:, :, :].rearrange("p c (n w) -> p (c n) w", w=w)[:, :, c0:c0 + w // 2]
            return ap[:, :, 0:SEQ].rearrange("p c (n w) -> p c n w", w=w)[:, :, :, c0:c0 + w // 2]

        flat = lambda pair: pair.rearrange("p b t -> p (b t)")
        halves = lambda ap: ap.rearrange("p (h t) -> p h t", h=2)
        POST = {"D1": 0, "OUT": 1, "MO": 2, "D2": 3}
        NU = DEPTH * UNITS
        NXA = NCH + 1
        rows = lambda b: P if b < NCH else DEC
        NJ = 2 + SBH

        block = ctx.enter_context(nc.Block())

        @block.sync
        def _(sp):
            def view(w):
                return w.rearrange("(k p) m -> p k m", p=P)

            def stream(a, n, kt, src):
                def load(r, s):
                    sp.dma_start(raw[:, s, 0:kt * P].rearrange("p (k m) -> p k m", k=kt), src(r, s)).then_inc(w_l[s], 16)
                first = 0
                if a == 0:
                    load(0, 0)
                    load(0, 1)
                    first = 1
                with sp.Fori(first, n // 2) as r:
                    for s in range(2):
                        sp.wait_ge(wlo_r, r * 2 + (a + s - 1))
                        load(r, s)

            for l in range(DEPTH):
                for f, (pu, pd, gu, dn) in enumerate((("F1", "D1", i["ffn1_gu"], i["ffn1_down"]),
                                                      ("F2", "D2", i["ffn2_gu"], i["ffn2_down"]))):
                    if f == 1:
                        for ph, w in (("IN", "w_in"), ("OUT", "w_out"), ("MK", "w_mk"), ("MVQ", "w_mv"), ("MO", "w_mo")):
                            v = view(i[w][l])
                            if ph == "IN":
                                a = unit_base(l, ph)
                                c0 = (NIN - NHG) * P
                                stream(a, NHG, KD, lambda r, s, v=v: v[:, :, bass.ds(r * 256 + (c0 + s * P), P)])
                                stream(a + NHG, NIN - NHG, KD, lambda r, s, v=v: v[:, :, bass.ds(r * 256 + s * P, P)])
                                continue
                            if ph == "MVQ":
                                v = (v, view(i["w_mq"][l]))
                                stream(unit_base(l, ph), 2 * KD, KD, lambda r, s, v=v: v[s][:, :, bass.ds(r * P, P)])
                                continue
                            stream(unit_base(l, ph), KD, KD, lambda r, s, v=v: v[:, :, bass.ds(r * 256 + s * P, P)])
                    v = view(gu[l])
                    stream(unit_base(l, pu), 2 * KF, KD, lambda r, s, v=v: v[:, :, bass.ds(r * P + s * FF, P)])
                    v = view(dn[l])
                    stream(unit_base(l, pd), 2 * KD, KU, lambda r, s, v=v: v[:, s * KU:(s + 1) * KU, bass.ds(r * P, P)])

        @block.tensor
        def _(pe):
            mm = nc.tensor.matmul

            def products(s, kt, out, lhs, rhs, first, last):
                n = 0
                for k in range(kt):
                    for a, b in ((0, 0), (0, 1), (1, 0)):
                        m = mm(out, lhs(a, k), rhs(b, k), start=(first and n == 0), stop=(last and n == 3 * kt - 1))
                        n += 1
                return m

            wt = lambda s: (lambda part, k: (w_hi, w_lo)[part][:, s, k * P:(k + 1) * P])

            def unit(u, s, hi, lo, kt=KD, k0=0, first=True, last=True, slot=None, gate=None, middle=None):
                pe.wait_ge(wlo_r, u + 1)
                slot = s if slot is None else slot
                n = 0
                for k in range(kt):
                    if gate:
                        gate(k)
                    if middle and k in middle:
                        middle[k]()
                    for a, b in ((0, 0), (0, 1), (1, 0)):
                        for h in range(2):
                            m = mm(PL[slot][:, h, 0:HT], wt(s)(a, k), (hi, lo)[b][:, k0 + k, h * HT:(h + 1) * HT],
                                   start=(first and n == 0), stop=(last and n == 3 * kt - 1))
                        n += 1
                m.then_inc(unit_d, 1)

            def mean_square(n):
                pe.wait_ge(acc_r, added(n + 1))
                if n:
                    pe.wait_ge(rs_r, n)
                parts = [acc[:, :]]
                if n % 2:
                    parts.append(sq[:, ((KD - 1) * (n + 1) - 1) % 2, :])
                for part in parts:
                    if part is not parts[0]:
                        pe.wait_ge(sq_r, KD * (n + 1))
                    for b in range(NXA):
                        c0 = b * P if b < NCH else T - P
                        m = mm(PX[0][:, 1, 504 + b:505 + b], part[:, c0:c0 + P], ones[:, 0:1], start=(b == 0 and part is parts[0]),
                               stop=(part is parts[-1]), skip_group_check=True)
                m.then_inc(ms_r, 1)

            def spread(n):
                pe.wait_ge(rt_r, n + 1)
                for b in range(NXA):
                    r0 = P - rows(b)
                    m = mm(PX[0][:, b // NCH, (b % NCH) * P:(b % NCH) * P + rows(b)], rtok[r0:P, b:b + 1].broadcast_to([rows(b), P]),
                           cst[r0:P, 0, r0:P], start=True, stop=True, skip_group_check=True)
                m.then_inc(bc_d, 1)

            def h_gate(pn):
                def gate(k):
                    pe.wait_ge(hi_r, KD * pn + k + 1)
                    pe.wait_ge(lo_r, KD * pn + k + 1)
                return gate

            def ffn(l, pu, pd, pn, f):
                a, t = unit_base(l, pu), tile_base(l, pu)
                for s in range(2):
                    if t + s >= 2:
                        pe.wait_ge(tile_e, t + s - 1)
                    unit(a + s, s, h_hi, h_lo, gate=h_gate(pn) if s == 0 else None)
                    if s == 0:
                        mean_square(2 * pn)
                    else:
                        spread(2 * pn)
                with pe.Fori(1, KF) as r:
                    for s in range(2):
                        pe.wait_ge(tile_e, r * 2 + (t + s - 1))
                        unit(r * 2 + (a + s), s, h_hi, h_lo)
                b, t = unit_base(l, pd), tile_base(l, pd)
                for m in range(KD):
                    pe.wait_ge(tile_e, t + m - 1)
                    for s in range(2):
                        if m == 0:
                            pe.wait_ge(alo_r, KF * f + (KU if s == 0 else KF))
                            pe.wait_ge(ahi_r, KF * f + (KU if s == 0 else KF))
                        unit(b + 2 * m + s, s, a_hi, a_lo, kt=KU, k0=s * KU, first=(s == 0), last=(s == 1), slot=m % 2)
                mean_square(2 * pn + 1)
                spread(2 * pn + 1)

            pe.wait_ge(cst_l, 16 * 8)
            nc.tensor.transpose(BK[0][:, 0:P], gst1[:, :], ident)
            nc.tensor.transpose(BK[1][:, 0:36], gst2[0:36, :], cst[0:36, 0, 0:36]).then_inc(par_d, 1)
            pe.wait_ge(xin_l, 32)
            for k in range(KD):
                if k >= 2:
                    pe.wait_ge(x_r, k - 1)
                for b in range(NXA):
                    m = nc.tensor.transpose(PL[k % 2][:, b // NCH, (b % NCH) * P:(b % NCH) * P + rows(b)],
                                            xtok[0:rows(b), b, k * P:(k + 1) * P], cst[0:rows(b), 0, 0:rows(b)])
                m.then_inc(xt_d, 1)
            for l in range(DEPTH):
                if l == 0:
                    pe.wait_ge(x_r, KD)
                ffn(l, "F1", "D1", 4 * l, 2 * l)
                pn = 4 * l + 1
                a, t = unit_base(l, "IN"), tile_base(l, "IN")
                for s in range(2):
                    pe.wait_ge(tile_e, t + s - 1)
                    unit(a + s, s, h_hi, h_lo, gate=h_gate(pn) if s == 0 else None)
                    if s == 0:
                        mean_square(2 * pn)
                    else:
                        spread(2 * pn)
                with pe.Fori(1, NHG // 2) as r:
                    for s in range(2):
                        pe.wait_ge(tile_e, r * 2 + (t + s - 1))
                        unit(r * 2 + (a + s), s, h_hi, h_lo)

                def i_rows():
                    pe.wait_ge(tile_e, t + NHG)
                    pe.wait_ge(rs_r, 2 * pn + 1)
                    for b in range(NXA):
                        for q in range(2):
                            m = nc.tensor.transpose(flat(PX[b // 4])[0:rows(b), b % 4 * 256 + q * P:b % 4 * 256 + (q + 1) * P],
                                                    proj[:, HI0 + q, b * P:b * P + rows(b)], ident)
                    m.then_inc(it_d, 1)

                def diagonal():
                    pe.wait_ge(it_e, 2 * (l + 1))
                    pe.wait_ge(qk0_r, l + 1)
                    for j in range(2):
                        for h in range(2):
                            m = mm(PX[j][:, h, 0:HT], bones, hQK[0][:, j, h * HT:(h + 1) * HT], start=True, stop=True)
                    m.then_inc(dg_d, 1)

                def level(n):
                    pe.wait_ge(qk_r, LEVELS * l + n)
                    if n == 1:
                        pe.wait_ge(dg_e, l + 1)
                    else:
                        pe.wait_ge(sc_e, LEVELS * l + n - 1)
                    w = 1 << n
                    for c in range(NXA if n < LEVELS else NCH):
                        nt, c0 = rows(c), c * P
                        for h in range(4):
                            e, j = 64 * (h % 2), h // 2
                            o0 = j * 256 + (c % NCH) * 64
                            qq = hQK[n % 2][e:e + 64, j, c0:c0 + nt].rearrange("p (n w) -> p n w", w=w)[:, :, w // 2:w]
                            m = mm(PX[c // NCH][0:nt, h % 2, o0:o0 + nt // 2].rearrange("p (n w) -> p n w", w=w // 2),
                                   hQK[n % 2][e:e + 64, j, c0:c0 + nt], qq, start=True, stop=True)
                    m.then_inc(sc_d, 1)

                def k_rows():
                    pe.wait_ge(kk_r, l + 1)
                    pe.wait_ge(sc_e, LEVELS * (l + 1))
                    for c in range(NXA):
                        for j in range(2):
                            m = nc.tensor.transpose(flat(PX[c // 4])[0:rows(c), c % 4 * 256 + j * P:c % 4 * 256 + (j + 1) * P],
                                                    hQK[0][:, j, c * P:c * P + rows(c)], ident)
                    m.then_inc(kt_d, 1)

                def chunk(c):
                    nt, c0 = rows(c), c * P
                    st = st_p if c < NCH else st_s
                    if c == 0:
                        pe.wait_ge(kt_e, 2 * (l + 1))
                        pe.wait_ge(qd_r, l + 1)
                        pe.wait_ge(s0_l, 16 * (l + 1))
                    else:
                        pe.wait_ge(hs_r, NXA * l + c)
                    if c >= 2:
                        pe.wait_ge(ho_e, NXA * l + c - 1)
                    ob, sbk = BK[c % 2], BK[2 + c % 2]
                    for h in range(4):
                        e, j = 64 * (h % 2), h // 2
                        q = 2 * (h % 2) + j
                        inter = c > 0
                        own = sacc[:, q * SEQ + c0:q * SEQ + c0 + P] if c < NCH else sacc_s[:, q * DEC:(q + 1) * DEC]
                        m = mm(ob[e:e + 64, j * P:j * P + nt], itok[:, c, h * 64:(h + 1) * 64], own, start=True, stop=not inter)
                        if inter:
                            m = mm(ob[e:e + 64, j * P:j * P + nt], st[e:e + 64, j, :], hQK[1][e:e + 64, j, c0:c0 + nt],
                                   start=False, stop=True)
                    m.then_inc(ho_d, 1)
                    for h in range(4):
                        e, j = 64 * (h % 2), h // 2
                        m = mm(sbk[e:e + 64, j * 64:(j + 1) * 64], kotok[0:nt, c, h * 64:(h + 1) * 64],
                               itok[0:nt, c, h * 64:(h + 1) * 64], start=True, stop=True)
                    m.then_inc(hs_d, 1)

                def head_squares():
                    pe.wait_ge(osq_r, l + 1)
                    for j in range(2):
                        for h in range(2):
                            m = mm(PX[j][:, h, 0:HT], bones, hE[:, j, h * HT:(h + 1) * HT], start=True, stop=True)
                    m.then_inc(oms_d, 1)

                for m in range(NHG, NIN):
                    beside = {}
                    if m == U_ITOK:
                        beside[6] = i_rows
                    elif m == U_DIAG:
                        beside[6] = diagonal
                    elif U_DIAG < m <= U_DIAG + LEVELS:
                        n = m - U_DIAG
                        beside[6] = lambda n=n: level(n)
                    elif m == U_KTOK:
                        beside[6] = k_rows
                    elif U_OUT <= m < U_OUT + NXA:
                        beside[6] = lambda c=m - U_OUT: chunk(c)
                    elif m == U_NORM:
                        beside[6] = head_squares
                    pe.wait_ge(tile_e, t + m - 1)
                    unit(a + m, m % 2, h_hi, h_lo, middle=beside)
                pe.wait_ge(tile_e, t + NIN)
                pe.wait_ge(hu_r, l + 1)
                def rows_of(n, bank, first):
                    b = n % NXA
                    c0 = b * P if b < NCH else SEQ
                    for q in range(4):
                        m = nc.tensor.transpose(BK[bank][0:rows(b), q * P:(q + 1) * P],
                                                proj[:, first + q, c0:c0 + rows(b)], ident)
                    m.then_inc(tp_d, 1)

                for n in range(NXA):
                    if n >= 4:
                        pe.wait_ge(tp_e, 12 * l + n - 3)
                    rows_of(n, n % 4, K0)
                pe.wait_ge(cache_l, 32 * (l + 1))
                for half in range(2):
                    n = NXA + half
                    pe.wait_ge(tp_e, 12 * l + n - 3)
                    for q in range(2):
                        for b in range(2):
                            m = nc.tensor.transpose(BK[n % 4][:, (2 * q + b) * P:(2 * q + b + 1) * P],
                                                    kpast_tok[:, b, (2 * half + q) * P:(2 * half + q + 1) * P], ident)
                    m.then_inc(tp_d, 1)
                pe.wait_ge(tp_e, 12 * l + NXA + 2)
                def scores(job):
                    z = SET[job % 2]
                    if job >= 2:
                        pe.wait_ge(wx_r, NJ * l + job - 1)
                    if job < 2:
                        e = 64 * job
                        for j in range(3):
                            nk = P if j < 2 else DEC
                            for h in range(job, SBH, 2):
                                ks = (kpast[e:e + 64, h // 2, j * P:(j + 1) * P] if j < 2
                                      else proj[e:e + 64, K0 + h // 2, SEQ:T])
                                c0 = j * SW + h // 2 * DEC
                                mm(z[0:nk, c0:c0 + DEC], ks, proj[e:e + 64, Q0 + h // 2, SEQ:T],
                                   start=(h == job and j != 1), stop=True, skip_group_check=True)
                        for q in range(SBH // 2):
                            m = mm(z[0:DEC, 2 * SW + q * DEC:2 * SW + (q + 1) * DEC], identb[e:e + 64, e:e + 64], negb[e:e + 64, e:e + 64],
                                   start=False, stop=True, skip_group_check=True)
                    else:
                        h = job - 2
                        e = 64 * (h % 2)
                        for j in range(NCH):
                            mm(z[:, Z_OFF[j]:Z_OFF[j] + SEQ - j * P], proj[e:e + 64, K0 + h // 2, j * P:(j + 1) * P],
                               proj[e:e + 64, Q0 + h // 2, j * P:SEQ], start=(j < 3), stop=True, skip_group_check=True)
                        for j in range(NCH):
                            m = mm(z[:, Z_OFF[j]:Z_OFF[j] + P], identb[:, :], negb[:, :], start=False, stop=True, skip_group_check=True)
                    m.then_inc(z_d, 1)

                def rest(job):
                    z, s, c = SET[job % 2], at_s[job % 2], at_c[job % 2]
                    pe.wait_ge(sp_r, NJ * l + job + 1)
                    if job < 2:
                        for j in range(3):
                            nk = P if j < 2 else DEC
                            m = mm(z[0:nk, j * SW:(j + 1) * SW], ntri[0:nk, 0:nk], s[0:nk, j * SW:(j + 1) * SW], start=False, stop=True,
                               skip_group_check=True)
                            for j2 in range(j + 1, 3):
                                n2 = P if j2 < 2 else DEC
                                m = mm(z[0:nk, j * SW:(j + 1) * SW], nones[0:n2, 0:nk], s[0:n2, j2 * SW:(j2 + 1) * SW], start=False,
                                       stop=True, skip_group_check=True)
                    else:
                        for j in range(NCH):
                            c0, n_ = Z_OFF[j], SEQ - j * P
                            mm(z[:, c0:c0 + n_], ntri, s[:, c0:c0 + n_], start=False, stop=True, skip_group_check=True)
                        pe.wait_ge(sum_r, SBH * l + job - 1)
                        for j, later in ((2, s[:, Z_OFF[3]:Z_OFF[3] + P]), (1, c[:, 0:256]), (0, c[:, 256:640])):
                            m = mm(z[:, Z_OFF[j] + P:Z_OFF[j] + SEQ - j * P], nones, later, start=False, stop=True, skip_group_check=True)
                    m.then_inc(r_d, 1)

                def attend(job):
                    bk, w = BK[6 + job % 2], at_w[job % 2]
                    pe.wait_ge(wx_r, NJ * l + job + 1)
                    if job >= 2:
                        pe.wait_ge(avhi_r, NJ * l + job - 1)
                        pe.wait_ge(avlo_r, NJ * l + job - 1)
                    if job < 2:
                        for h in range(job, SBH, 2):
                            e = 64 * (h % 2)
                            for j in range(3):
                                nk = P if j < 2 else DEC
                                vv = (vpast[:, j, h * 64:(h + 1) * 64] if j < 2 else vtok[0:DEC, NCH, h * 64:(h + 1) * 64])
                                c0 = j * SW + h // 2 * DEC
                                m = mm(bk[e:e + 64, (h // 2) * 64:(h // 2 + 1) * 64], vv, w[0:nk, c0:c0 + DEC],
                                       start=(j == 0), stop=(j == 2))
                    else:
                        h = job - 2
                        e = 64 * (h % 2)
                        for j in range(NCH):
                            m = mm(bk[e:e + 64, j * P:SEQ], vtok[:, j, h * 64:(h + 1) * 64],
                                   w[:, Z_OFF[j]:Z_OFF[j] + SEQ - j * P], start=(j == 0), stop=(j == NCH - 1),
                                   skip_group_check=True)
                    m.then_inc(av_d, 1)

                scores(0)
                scores(1)
                for n in range(NXA):
                    if n >= 2:
                        pe.wait_ge(tp_e, 12 * l + NXA + n + 1)
                    rows_of(n, 6 + n % 2, V0)
                pe.wait_ge(tp_e, 12 * (l + 1))
                for job in range(NJ + 1):
                    if job < NJ:
                        rest(job)
                    if job:
                        attend(job - 1)
                    if job + 2 < NJ:
                        scores(job + 2)
                a, t = unit_base(l, "OUT"), tile_base(l, "OUT")
                pn = 4 * l + 1
                pe.wait_ge(avhi_r, NJ * (l + 1))
                pe.wait_ge(avlo_r, NJ * (l + 1))
                pe.wait_ge(mixlo_r, 4 * (l + 1))
                for m in range(KD):
                    pe.wait_ge(tile_e, t + m - 1)
                    unit(a + m, m % 2, mix_hi, mix_lo)
                mean_square(2 * pn + 1)
                spread(2 * pn + 1)
                pe.wait_ge(mn_r, l + 1)
                for n in range(4):
                    if n >= 2:
                        pe.wait_ge(mlo_r, 4 * l + n - 1)
                    for q in range(2):
                        for b in range(2):
                            m = nc.tensor.transpose(BK[2 + n % 2][:, (2 * q + b) * P:(2 * q + b + 1) * P],
                                                    mtok[:, b, (2 * n + q) * P:(2 * n + q + 1) * P], ident)
                    m.then_inc(mt_d, 1)
                pe.wait_ge(mhi_r, 4 * (l + 1))
                pe.wait_ge(mlo_r, 4 * (l + 1))
                pe.wait_ge(tile_e, t + KD)
                def memory_unit(u, n):
                    pe.wait_ge(wlo_r, u + 1)
                    s = u % 2
                    products(s, KD, PL[s][:, 0, 0:NMEM], wt(s), lambda part, k: (m_hi, m_lo)[part][:, k, :], True, True).then_inc(unit_d, 1)

                a = unit_base(l, "MK")
                for m in range(KD):
                    if m >= 2:
                        pe.wait_ge(mkv_e, 16 * l + m - 1)
                    memory_unit(a + m, m)
                pn = 4 * l + 2
                a, t = unit_base(l, "MVQ"), tile_base(l, "MVQ")
                for m in range(KD):
                    pe.wait_ge(mkv_e, 16 * l + KD + m - (1 if m == 0 else 0))
                    memory_unit(a + 2 * m, KD + m)
                    pe.wait_ge(mkv_e, 16 * l + KD)
                    if m == 1:
                        spread(2 * pn)
                    if m:
                        pe.wait_ge(tile_e, t + m)
                    unit(a + 2 * m + 1, 1, h_hi, h_lo, gate=h_gate(pn) if m == 0 else None)
                    if m == 0:
                        mean_square(2 * pn)
                pe.wait_ge(ck_l, 16 * (l + 1))
                for n in range(4):
                    if n >= 2:
                        pe.wait_ge(ck_e, 4 * l + n - 1)
                    for q in range(2):
                        for b in range(2):
                            m = nc.tensor.transpose(BK[2 + n % 2][:, (2 * q + b) * P:(2 * q + b + 1) * P],
                                                    mtok[:, b, (2 * n + q) * P:(2 * n + q + 1) * P], ident)
                    m.then_inc(ck_d, 1)
                pe.wait_ge(ck_e, 4 * (l + 1))
                for n in range(8):
                    if n >= 2:
                        pe.wait_ge(kr_e, 8 * l + n - 1)
                    c, n4 = n // 2 % 2, n % 2
                    for q in range(4):
                        m = nc.tensor.transpose(BK[2 + n % 2][:, q * P:(q + 1) * P],
                                                (mk_p if n < 4 else mvT)[:, 4 * n4 + q, c * P:(c + 1) * P], ident)
                    m.then_inc(kr_d, 1)
                pe.wait_ge(kr_e, 8 * (l + 1))
                pe.wait_ge(tile_e, t + KD)
                pe.wait_ge(rs_r, 2 * pn + 1)

                def x_scores(b):
                    nt, c0 = rows(b), b * P
                    if b >= 2:
                        pe.wait_ge(xe_r, 4 * (NXA * l + b - 1))
                    for h in range(MH):
                        for kk in range(2):
                            m = mm(PL[b % 2][0:nt, h // 2, (h % 2) * NMEM:(h % 2 + 1) * NMEM], qx[:, 2 * h + kk, c0:c0 + nt],
                                   (mk_p if b < NCH else mk_s)[:, 2 * h + kk, :], start=(kk == 0), stop=(kk == 1))
                    m.then_inc(xs_d, 1)

                def x_turn(b):
                    nt = rows(b)
                    pe.wait_ge(pn_r, 4 * (NXA * l + b + 1))
                    if b >= 2:
                        pe.wait_ge(pt_e, NXA * l + b - 1)
                    for hc in range(8):
                        m = nc.tensor.transpose(PX[b % 2][:, hc // 4, (hc % 4) * P:(hc % 4) * P + nt],
                                                pr[b % 2][0:nt, hc // 2, (hc % 2) * P:(hc % 2 + 1) * P], cst[0:nt, 0, 0:nt])
                    m.then_inc(pt_d, 1)

                x_scores(0)
                x_scores(1)
                for b in range(NXA):
                    if b + 2 < NXA:
                        x_scores(b + 2)
                    x_turn(b)
                pe.wait_ge(pt_e, NXA * (l + 1))
                pe.wait_ge(xe_r, 4 * NXA * (l + 1))
                pe.wait_ge(cv_l, 16 * (l + 1))
                for n in range(8):
                    h, dt = n // 2, n % 2
                    if n >= 2:
                        pe.wait_ge(xalo_r, 8 * l + n - 1)
                    for grp in range(2):
                        v = mv_p if grp == 0 else mv_s
                        c0, nt = (0, SEQ) if grp == 0 else (SEQ, DEC)
                        for c in range(2):
                            m = mm(PL[n % 2][:, grp, 0:nt], v[:, c, n * P:(n + 1) * P], pT[:, 2 * h + c, c0:c0 + nt],
                                   start=(c == 0), stop=(c == 1))
                    m.then_inc(xa_d, 1)
                a, t = unit_base(l, "MO"), tile_base(l, "MO")
                pe.wait_ge(xalo_r, 8 * (l + 1))
                for m in range(KD):
                    if m >= 2:
                        pe.wait_ge(tile_e, t + m - 1)
                    unit(a + m, m % 2, xo_hi, xo_lo)
                mean_square(2 * pn + 1)
                spread(2 * pn + 1)
                ffn(l, "F2", "D2", 4 * l + 3, 2 * l + 1)
            pe.wait_ge(x_r, KD * (4 * DEPTH + 1))
            for n in range(2 * NXA):
                b, half = n // 2, n % 2
                if n >= 4:
                    pe.wait_ge(yt_e, n - 3)
                if n == 0:
                    pe.wait_ge(rs_r, 8 * DEPTH)
                for q in range(4):
                    m = nc.tensor.transpose(BK[n % 4][0:rows(b), q * P:(q + 1) * P], x[:, 4 * half + q, b * P:b * P + rows(b)], ident)
                m.then_inc(yt_d, 1)

        @block.scalar
        def _(act):
            A = nc.scalar.activation
            chain = [0]

            def link(ins):
                chain[0] += 1
                ins.then_inc(ach, 1)
                act.wait_ge(ach, chain[0])

            def split(u, s, words, wait=True):
                act.wait_ge(w_l[s], u * 8 + (16 - 8 * s))
                A(w_hi[:, s, 0:words], raw[:, s, 0:words], ACT.Copy).then_inc(whi_r, 1)

            def step(u, pn=None):
                act.wait_ge(unit_d, u)
                if pn is not None:
                    post_square(pn, KD - 1)
                if u + 1 < NU:
                    split(u + 1, (u + 1) % 2, unit_words(u + 1))

            def square_to(n, k):
                if k == 0:
                    if n:
                        act.wait_ge(ms_r, n)
                    return acc[:, :]
                c = (KD - 1) * n + k - 1
                if c >= 2:
                    n2, k2 = (c - 2) // (KD - 1), (c - 2) % (KD - 1) + 1
                    if n2 % 2 and k2 == KD - 1:
                        act.wait_ge(ms_r, n2 + 1)
                    else:
                        act.wait_ge(acc_r, added(n2) + k2)
                return sq[:, c % 2, :]

            def pre_piece(pn, k):
                act.wait_ge(x_r, KD * pn + k + 1)
                l, n = pn // 4, pn % 4
                A(h_hi[:, k, :], x[:, k, :], ACT.Copy, scale=gpre(l, n, k)).then_inc(hi_r, 1)
                A(square_to(2 * pn, k), x[:, k, :], ACT.Square).then_inc(sq_r, 1)

            def root(n):
                act.wait_ge(mt_r, n + 1)
                link(A(rtok, mtk, ACT.Ln))
                A(rtok, rtok, ACT.Exp, scale=-0.5).then_inc(y0_r, 1)
                act.wait_ge(bc_d, n + 1)
                A(rinv[:, :], PX[0][:, :, :].rearrange("p h t -> p (h t)")[:, 0:T], ACT.Copy).then_inc(rs_r, 1)

            def post_square(pn, m):
                A(halves(square_to(2 * pn + 1, m)), PL[m % 2][:, :, 0:HT], ACT.Square).then_inc(sq_r, 1)

            def ffn(l, pu, pd, pn, f):
                a = unit_base(l, pu)

                def first(r, words, norm=False):
                    u = r * 2 + (a + 1)
                    act.wait_ge(unit_d, u)
                    split(u + 1, 0, words)
                    if norm:
                        root(2 * pn)
                        nc.scalar.preload_act_table_set("silu_and_others")
                    act.wait_ge(tile_e, r * 2 + (tile_base(l, pu) + 1))
                    A(sg[:, :], gt[:, :], ACT.Silu).then_inc(sg_r, 1)

                def second(r, words):
                    u = r * 2 + (a + 2)
                    act.wait_ge(unit_d, u)
                    split(u + 1, 1, words)
                    act.wait_ge(pr_r, r + (KF * f + 1))
                    A(a_hi[:, bass.ds(r, 1), :], ut[:, :].rearrange("p (o t) -> p o t", o=1), ACT.Copy).then_inc(ahi_r, 1)

                first(0, KD * P, norm=True)
                second(0, KD * P)
                with act.Fori(1, KF - 1) as r:
                    first(r, KD * P)
                    second(r, KD * P)
                first(KF - 1, KU * P)
                second(KF - 1, KU * P)
                nc.scalar.preload_act_table_set("natural_log_exp_and_others")
                b = unit_base(l, pd)
                for u in range(b + 1, b + 2 * KD + 1):
                    step(u, pn if u == b + 2 * KD else None)
                    if (u - b) % 2 == 0 and u < b + 2 * KD:
                        post_square(pn, (u - b) // 2 - 1)
                act.wait_ge(tile_e, tile_base(l, pd))
                root(2 * pn + 1)

            nc.scalar.preload_act_table_set("natural_log_exp_and_others")
            split(0, 0, unit_words(0))
            split(1, 1, unit_words(1))
            act.wait_ge(par_r, 3)
            A(lt[:, 2:6], lt[:, 2:6], ACT.Exp).then_inc(par_r, 1)
            for k in range(KD):
                pre_piece(0, k)
            for l in range(DEPTH):
                ffn(l, "F1", "D1", 4 * l, 2 * l)
                pn = 4 * l + 1
                for k in range(KD):
                    pre_piece(pn, k)
                a = unit_base(l, "IN")
                for u in range(a + 1, a + NIN + 1):
                    step(u)
                    m = u - a - 1
                    if m == 0:
                        root(2 * pn)
                    if m == U_SIG:
                        act.wait_ge(tile_e, tile_base(l, "IN") + 4)
                        hf = proj[:, HF0:HF0 + 2, :]
                        A(kf[:, :, :], hf, ACT.Sigmoid, scale=-1.0).then_inc(sig_r, 1)
                        A(bT[:, :, :], hf, ACT.Sigmoid).then_inc(sig_r, 1)
                        nc.scalar.preload_act_table_set("natural_log_exp_and_others")
                    if m == U_LN:
                        act.wait_ge(f_r, l + 1)
                        A(hE[:, :, :], bT[:, :, :], ACT.Ln).then_inc(ln_r, 1)
                        A(hQK[0][:, :, :], hQK[1][:, :, :], ACT.Ln, scale=1.0 / LN_SPLIT).then_inc(ln_r, 1)
                    if m == U_GATE:
                        act.wait_ge(tile_e, tile_base(l, "IN") + NHG)
                        gate = proj[:, HG0:HG0 + 2, :]
                        A(gate, gate, ACT.Silu).then_inc(sig_r, 1)
                        nc.scalar.preload_act_table_set("natural_log_exp_and_others")
                    if m == U_ITOK:
                        act.wait_ge(it_d, l + 1)
                        A(itok[:, 0:NCH, :].rearrange("p b n -> p (b n)"), flat(PX[0]), ACT.Copy).then_inc(it_e, 1)
                        A(itok[0:DEC, NCH, :], BK[2][0:DEC, 0:256], ACT.Copy).then_inc(it_e, 1)
                    if 0 < m - U_LEV <= LEVELS:
                        n = m - U_LEV
                        act.wait_ge(e_in, (LEVELS + 1) * l + n)
                        A(part(hE, n, 0), part(hE, n, 0), ACT.Exp, scale=-1.0)
                        A(part(hE, n, 1), part(hE, n, 1), ACT.Exp).then_inc(e_r, 1)
                    if m == U_KEND:
                        act.wait_ge(e_in, (LEVELS + 1) * (l + 1))
                        A(hE[:, :, :], hE[:, :, :], ACT.Exp, scale=-1.0).then_inc(e_r, 1)
                    if m == U_QDEC:
                        act.wait_ge(kk_r, l + 1)
                        A(hE[:, :, :], bT[:, :, :], ACT.Exp).then_inc(e_r, 1)
                    if m == U_KTOK:
                        act.wait_ge(kt_d, l + 1)
                        A(kotok[:, 0:NCH, :].rearrange("p b n -> p (b n)"), flat(PX[0]), ACT.Copy).then_inc(kt_e, 1)
                        A(kotok[0:DEC, NCH, :], BK[2][0:DEC, 0:256], ACT.Copy).then_inc(kt_e, 1)
                    if m == U_SQ:
                        act.wait_ge(ho_e, NXA * (l + 1))
                        A(hE[:, :, :], ot[:, :, :], ACT.Square).then_inc(osq_r, 1)
                    if m == U_NORM:
                        act.wait_ge(oms_d, l + 1)
                        for j in range(2):
                            ins = A(halves(hE[:, j, :]), PX[j][:, :, 0:HT], ACT.Ln, scale=1.0 / HD, bias=eps)
                        link(ins)
                        A(hE[:, :, :], hE[:, :, :], ACT.Exp, scale=-0.5).then_inc(ors_r, 1)
                for n in range(NXA + 2):
                    act.wait_ge(tp_d, 12 * l + n + 1)
                    if n < NXA:
                        A(ktok[0:rows(n), n, :], BK[n % 4][0:rows(n), :], ACT.Copy).then_inc(tp_e, 1)
                    else:
                        q = 2 * (n - NXA)
                        A(kpast[:, q:q + 2, :], BK[n % 4].rearrange("p (q t) -> p q t", q=2), ACT.Copy).then_inc(tp_e, 1)
                act.wait_ge(cvr, l + 1)
                A(mix_hi[:, 4:6, :], ct[:, :, :], ACT.Copy).then_inc(cvhi, 1)

                def front(job):
                    z, a_ = SET[job % 2], at_a[job % 2]
                    act.wait_ge(z_d, NJ * l + job + 1)
                    if job == 0:
                        act.wait_ge(mixlo_r, 4 * l + 2)
                        act.wait_ge(cvhi, l + 1)
                        act.wait_ge(mixst_s, 64 * (l + 1))
                    if job == 1:
                        act.wait_ge(kout_s, 16 * 2 * (l + 1))
                    for r_, c0, c1 in ((P, 0, 2 * SW), (DEC, 2 * SW, 3 * SW)) if job < 2 else ((P, 0, ZW),):
                        part = a_[0:r_, c0:c1]
                        link(A(part, z[0:r_, c0:c1], ACT.Abs))
                        link(A(part, part, ACT.Exp, scale=-1.0))
                        ins = A(part, part, ACT.Ln, bias=1.0)
                    ins.then_inc(l_r, 1)

                def back(job):
                    z, w = SET[job % 2], at_w[job % 2]
                    act.wait_ge(r_d, NJ * l + job + 1)
                    if job >= 2:
                        act.wait_ge(av_d, NJ * l + job - 1)
                    if job < 2:
                        A(w[:, 0:2 * SW], z[:, 0:2 * SW], ACT.Exp)
                        A(w[0:DEC, 2 * SW:3 * SW], z[0:DEC, 2 * SW:3 * SW], ACT.Exp).then_inc(wx_r, 1)
                    else:
                        A(w[:, :], z[:, 0:ZW], ACT.Exp).then_inc(wx_r, 1)

                def evac(job):
                    bk = BK[6 + job % 2]
                    act.wait_ge(av_d, NJ * l + job + 1)
                    if job < 2:
                        A(mix_hi[64 * job:64 * job + 64, 0:4, SEQ:T], bk[64 * job:64 * job + 64, 0:256].rearrange("p (q t) -> p q t", q=4), ACT.Copy).then_inc(avhi_r, 1)
                    else:
                        e, p_ = 64 * (job % 2), (job - 2) // 2
                        A(mix_hi[e:e + 64, p_, 0:SEQ], bk[e:e + 64, :], ACT.Copy).then_inc(avhi_r, 1)

                nc.scalar.preload_act_table_set("natural_log_exp_and_others")
                front(0)
                for b in range(NXA):
                    act.wait_ge(tp_d, 12 * l + NXA + 2 + b + 1)
                    A(vtok[0:rows(b), b, :], BK[6 + b % 2][0:rows(b), :], ACT.Copy).then_inc(tp_e, 1)
                front(1)
                for job in range(NJ + 1):
                    if job < NJ:
                        back(job)
                    if job:
                        evac(job - 1)
                    if job + 2 < NJ:
                        front(job + 2)
                    if job == 4:
                        act.wait_ge(hgo_r, l + 1)
                        A(mix_hi[:, 6:8, :], ot[:, :, :], ACT.Copy).then_inc(hghi, 1)
                a = unit_base(l, "OUT")
                pn = 4 * l + 1
                act.wait_ge(mem_l, 16 * (l + 1))
                for b in range(2):
                    A(mk_s[:, 4 * b:4 * b + 4, :].rearrange("p k n -> p (k n)"), mtok[:, b, :], ACT.Square,
                      accum_out=mss[:, b:b + 1]).then_inc(mss_r, 1)
                act.wait_ge(mss_r, 2 * (l + 1))
                A(mss, mss, ACT.Sqrt, scale=1.0 / D, bias=eps).then_inc(mrs_r, 1)
                nc.scalar.preload_act_table_set("natural_log_exp_and_others")
                for m in range(KD):
                    step(a + m + 1, pn if m == KD - 1 else None)
                    if m < KD - 1:
                        post_square(pn, m)
                act.wait_ge(tile_e, tile_base(l, "OUT"))
                root(2 * pn + 1)
                for n in range(4):
                    act.wait_ge(mt_d, 4 * l + n + 1)
                    for q in range(2):
                        ins = A(m_hi[:, 2 * n + q, :], BK[2 + n % 2][:, q * 256:(q + 1) * 256], ACT.Copy, scale=gmem(l, 2 * n + q))
                    ins.then_inc(mhi_r, 1)
                a = unit_base(l, "MK")
                for m in range(KD):
                    pre_piece(pn + 1, m)
                    step(a + m + 1)
                    A(mk_p[:, m, :], PL[m % 2][:, 0, 0:NMEM], ACT.Copy).then_inc(mkv_e, 1)
                pn = 4 * l + 2
                a = unit_base(l, "MVQ")
                for m in range(KD):
                    step(a + 2 * m + 1)
                    A(mvT[:, m, :], PL[0][:, 0, 0:NMEM], ACT.Copy).then_inc(mkv_e, 1)
                    step(a + 2 * m + 2)
                    if m == 0:
                        root(2 * pn)
                for n in range(4):
                    act.wait_ge(ck_d, 4 * l + n + 1)
                    A(mk_s[:, 2 * n:2 * n + 2, :], BK[2 + n % 2].rearrange("p (q t) -> p q t", q=2), ACT.Copy).then_inc(ck_e, 1)
                for n in range(8):
                    act.wait_ge(kr_d, 8 * l + n + 1)
                    A((mtok if n < 4 else mv_p)[:, n // 2 % 2, (n % 2) * 512:(n % 2 + 1) * 512], BK[2 + n % 2], ACT.Copy).then_inc(kr_e, 1)
                def x_exp(b):
                    nt, c0 = rows(b), 4 * (b % 2)
                    act.wait_ge(mx_r, NXA * l + b + 1)
                    for h in range(MH):
                        A(pr[b % 2][0:nt, h, :], PL[b % 2][0:nt, h // 2, (h % 2) * NMEM:(h % 2 + 1) * NMEM], ACT.Exp,
                          scale=1.0 / 16.0, bias=mx[0:nt, c0 + h:c0 + h + 1], accum_out=rsum[0:nt, c0 + h:c0 + h + 1]).then_inc(xe_r, 1)

                def x_keep(b):
                    nt = rows(b)
                    act.wait_ge(pt_d, NXA * l + b + 1)
                    A(pT[:, :, b * P:b * P + nt], PX[b % 2][:, :, :].rearrange("p a (q t) -> p (a q) t", q=4)[:, :, 0:nt],
                      ACT.Copy).then_inc(pt_e, 1)

                for b in range(NXA):
                    if b >= 2:
                        act.wait_ge(pt_d, NXA * l + b - 1)
                    x_exp(b)
                    if b:
                        x_keep(b - 1)
                x_keep(NXA - 1)
                for n in range(8):
                    act.wait_ge(xa_d, 8 * l + n + 1)
                    A(xo_hi[:, n, 0:SEQ], PL[n % 2][:, 0, :], ACT.Copy).then_inc(xahi_r, 1)
                    A(xo_hi[:, n, SEQ:T], PL[n % 2][:, 1, 0:DEC], ACT.Copy).then_inc(xahi_r, 1)
                a = unit_base(l, "MO")
                for m in range(KD):
                    step(a + m + 1, pn if m == KD - 1 else None)
                    if m < KD - 1:
                        post_square(pn, m)
                act.wait_ge(tile_e, tile_base(l, "MO"))
                root(2 * pn + 1)
                for k in range(KD):
                    pre_piece(4 * l + 3, k)
                ffn(l, "F2", "D2", 4 * l + 3, 2 * l + 1)
                if l + 1 < DEPTH:
                    for k in range(KD):
                        pre_piece(4 * l + 4, k)
            for n in range(2 * NXA):
                b, half = n // 2, n % 2
                act.wait_ge(yt_d, n + 1)
                A(xtok[0:rows(b), b, half * 512:(half + 1) * 512], BK[n % 4][0:rows(b), :], ACT.Copy).then_inc(yt_e, 1)

        @block.vector
        def _(v):
            TT, TS, STT = nc.vector.tensor_tensor, nc.vector.tensor_scalar, nc.vector.scalar_tensor_tensor
            chain = [0]

            def link(ins):
                chain[0] += 1
                ins.then_inc(dch, 1)
                v.wait_ge(dch, chain[0])

            f32 = lambda ap: ap.bitcast(F32)

            def split(u, s, words):
                v.wait_ge(whi_r, u + 1)
                TT(w_lo[:, s, 0:words], raw[:, s, 0:words], f32(w_hi[:, s, 0:words]), ALU.subtract).then_inc(wlo_r, 1)

            def step(u):
                v.wait_ge(unit_d, u)
                if u + 1 < NU:
                    split(u + 1, (u + 1) % 2, unit_words(u + 1))

            def h_lo_piece(pn, k):
                v.wait_ge(hi_r, KD * pn + k + 1)
                STT(h_lo[:, k, :], x[:, k, :], gpre(pn // 4, pn % 4, k), f32(h_hi[:, k, :]), ALU.mult, ALU.subtract).then_inc(lo_r, 1)

            def root(n):
                v.wait_ge(ms_r, n + 1)
                TS(mtk, PX[0][:, 1, 504:504 + NXA], 1.0 / D, EPS, ALU.mult, ALU.add).then_inc(mt_r, 1)
                v.wait_ge(y0_r, n + 1)
                link(TT(ntk, rtok, rtok, ALU.mult))
                link(TT(ntk, ntk, mtk, ALU.mult))
                link(TS(ntk, ntk, -0.5, 1.5, ALU.mult, ALU.add))
                TT(rtok, rtok, ntk, ALU.mult).then_inc(rt_r, 1)
                v.wait_ge(rs_r, n + 1)

            def y_tile(l, pn, m):
                v.wait_ge(sq_r, KD * (2 * pn + 1) + m + 1)
                TS(halves(y[:, m, :]), PL[m % 2][:, :, 0:HT], gpost(l, pn % 4, m), None, ALU.mult).then_inc(tile_e, 1)

            def update(pn, k, weight):
                TT(y[:, k, :], y[:, k, :], rinv[:, :], ALU.mult).then_inc(y_r, 1)
                v.wait_ge(y_r, KD * pn + k + 1)
                STT(x[:, k, :], y[:, k, :], weight, x[:, k, :], ALU.mult, ALU.add).then_inc(x_r, 1)

            def ffn(l, pu, pd, pn, f):
                a = unit_base(l, pu)

                def pair(r, words, norm=False):
                    v.wait_ge(unit_d, r * 2 + (a + 1))
                    split(r * 2 + (a + 2), 0, words)
                    if norm:
                        root(2 * pn)
                    TT(halves(gt[:, :]), PL[0][:, :, 0:HT], halves(rinv[:, :]), ALU.mult).then_inc(tile_e, 1)
                    v.wait_ge(unit_d, r * 2 + (a + 2))
                    split(r * 2 + (a + 3), 1, words)
                    TT(halves(ut[:, :]), PL[1][:, :, 0:HT], halves(rinv[:, :]), ALU.mult).then_inc(tile_e, 1)
                    v.wait_ge(tile_e, r * 2 + (tile_base(l, pu) + 2))
                    v.wait_ge(sg_r, r + (KF * f + 1))
                    TT(ut[:, :], ut[:, :], sg[:, :], ALU.mult).then_inc(pr_r, 1)
                    v.wait_ge(ahi_r, r + (KF * f + 1))
                    o1 = "p (o t) -> p o t"
                    TT(a_lo[:, bass.ds(r, 1), :], ut[:, :].rearrange(o1, o=1), f32(a_hi[:, bass.ds(r, 1), :]), ALU.subtract).then_inc(alo_r, 1)

                pair(0, KD * P, norm=True)
                with v.Fori(1, KF - 1) as r:
                    pair(r, KD * P)
                pair(KF - 1, KU * P)
                b = unit_base(l, pd)
                for u in range(b + 1, b + 2 * KD + 1):
                    step(u)
                    if (u - b) % 2 == 0:
                        y_tile(l, pn, (u - b) // 2 - 1)
                root(2 * pn + 1)

            nc.vector.memset(eps, EPS).then_inc(dch, 1)
            chain[0] += 1
            v.wait_ge(dch, chain[0])
            split(0, 0, unit_words(0))
            split(1, 1, unit_words(1))
            v.wait_ge(par_d, 1)
            nc.vector.tensor_copy(lmask[:, :, :], lst[:, 0:LEVELS, :])
            nc.vector.tensor_copy(negb[:, :], lst[:, LEVELS, :])
            nc.vector.tensor_copy(identb[:, :], ident)
            nc.vector.tensor_copy(par[:, 0:128], BK[0][:, 0:128]).then_inc(par_r, 1)
            nc.vector.tensor_copy(par[:, 128:164], BK[1][:, 0:36]).then_inc(par_r, 1)
            v.wait_ge(par_r, 2)
            link(TT(lt[:, 0:2], par[:, 156:158], par[:, 158:160], ALU.max))
            link(TT(lt[:, 2:4], par[:, 156:158], lt[:, 0:2], ALU.subtract))
            TT(lt[:, 4:6], par[:, 158:160], lt[:, 0:2], ALU.subtract).then_inc(par_r, 1)
            v.wait_ge(par_r, 4)
            link(TT(lt[:, 6:8], lt[:, 2:4], lt[:, 4:6], ALU.add))
            link(nc.vector.reciprocal(lt[:, 8:10], lt[:, 6:8]))
            link(TT(lt[:, 2:4], lt[:, 2:4], lt[:, 8:10], ALU.mult))
            link(TT(lt[:, 4:6], lt[:, 4:6], lt[:, 8:10], ALU.mult))
            link(TT(lbv[:, 0:2], lt[:, 2:4], lt[:, 2:4], ALU.subtract))
            link(TT(lt[:, 10:12], lt[:, 2:4], lt[:, 4:6], ALU.add))
            link(TT(lbv[:, 2:4], lt[:, 10:12], lt[:, 2:4], ALU.subtract))
            link(TS(oml, lbv, -1.0, 1.0, ALU.mult, ALU.add))
            for k in range(KD):
                v.wait_ge(xt_d, k + 1)
                link(nc.vector.tensor_copy(x[:, k, 0:SEQ], PL[k % 2][:, 0, :]))
                nc.vector.tensor_copy(x[:, k, SEQ:T], PL[k % 2][:, 1, 0:DEC]).then_inc(x_r, 1)
            for k in range(KD):
                h_lo_piece(0, k)
            for l in range(DEPTH):
                ffn(l, "F1", "D1", 4 * l, 2 * l)
                for k in range(KD):
                    update(4 * l, k, 0.5)
                    if k:
                        h_lo_piece(4 * l + 1, k - 1)
                h_lo_piece(4 * l + 1, KD - 1)
                pn = 4 * l + 1
                a = unit_base(l, "IN")
                q_ = proj[:, HQ0:HQ0 + 2, :]
                ec, bt = (LEVELS + 2) * l, bT[:, :, :]

                def forget():
                    v.wait_ge(sig_r, 3 * l + 2)
                    for c in range(2):
                        n = 2 * l + c
                        TS(kf[:, c, :], kf[:, c, :], oml[:, n:n + 1], None, ALU.mult)
                        ins = TS(bT[:, c, :], bT[:, c, :], oml[:, n:n + 1], lbv[:, n:n + 1], ALU.mult, ALU.add)
                    link(ins)
                    link(TS(bt, bt, F_FLOOR, None, ALU.max))
                    link(TS(hQK[1][:, :, :], bt, LN_SPLIT, None, ALU.min))
                    TS(bt, bt, LN_SPLIT, None, ALU.max).then_inc(f_r, 1)

                def scan():
                    v.wait_ge(ln_r, 2 * (l + 1))
                    link(TT(hE[:, :, :], hE[:, :, :], hQK[0][:, :, :], ALU.add))
                    for c in range(2):
                        for b in range(NXA):
                            c0, n = b * P, rows(b)
                            nc.vector.tensor_tensor_scan(bT[:, c, c0:c0 + n], ones[:, 0:n], hE[:, c, c0:c0 + n], 0.0, ALU.mult, ALU.add)
                    TT(hQK[0][:, :, :], q_, kf[:, :, :], ALU.mult).then_inc(qk0_r, 1)
                    nc.vector.memset(sacc[:, :], 0.0)
                    nc.vector.memset(itok[DEC:P, NCH, :], 0.0)
                    link(nc.vector.memset(sacc_s[:, :], 0.0))

                def exponent(n):
                    if n < LEVELS:
                        w = 1 << n
                        bb = bt.rearrange("p c (n w) -> p (c n) w", w=w)
                        TT(hE[:, :, :].rearrange("p c (n w) -> p (c n) w", w=w), bb,
                           bb[:, :, w // 2 - 1:w // 2].broadcast_to([P, 2 * T // w, w]), ALU.subtract).then_inc(e_in, 1)
                        return
                    at = P // 2 - 1 if n == LEVELS else P - 1
                    for c in range(2):
                        bb = bT[:, c, 0:SEQ].rearrange("p (n w) -> p n w", w=P)
                        ins = TT(hE[:, c, 0:SEQ].rearrange("p (n w) -> p n w", w=P), bb,
                                 bb[:, :, at:at + 1].broadcast_to([P, NCH, P]), ALU.subtract)
                        if n > LEVELS:
                            ins = TS(hE[:, c, SEQ:T], bT[:, c, SEQ:T], bT[:, c, T - 1:T], None, ALU.subtract)
                    ins.then_inc(e_in, 1)

                def decay(n):
                    v.wait_ge(e_r, ec + n)
                    TT(part(hQK[n % 2], n, 0), part(kf, n, 0), part(hE, n, 0), ALU.mult)
                    TT(part(hQK[n % 2], n, 1), part(proj[:, HQ0:HQ0 + 2, :], n, 1), part(hE, n, 1), ALU.mult).then_inc(qk_r, 1)
                    v.wait_ge(qk_r, LEVELS * l + n)

                def keep(n):
                    v.wait_ge(sc_d, LEVELS * l + n)
                    w = 1 << n
                    for nt, q, dst, src in (((P, 4 * NCH, sacc, PX[0]),) + (((DEC, 4, sacc_s, PX[1]),) if n < LEVELS else ())):
                        src_ = flat(src)[0:nt, :].rearrange("p (q t) -> p q t", q=q)[:, :, 0:nt // 2]
                        mask = lmask[0:nt, n - 1:n, 0:nt].rearrange("p o (n w) -> p o n w", w=w)[:, :, :, w // 2:w]
                        ins = nc.vector.copy_predicated(
                            dst[0:nt, :].rearrange("p (q n w) -> p q n w", q=q, w=w)[:, :, :, w // 2:w],
                            mask.broadcast_to([nt, q, nt // w, w // 2]),
                            src_.rearrange("p q (n w) -> p q n w", w=w // 2))
                    ins.then_inc(sc_e, 1)
                    v.wait_ge(sc_e, LEVELS * l + n)

                def state(c):
                    v.wait_ge(hs_d, NXA * l + c + 1)
                    sbk = BK[2 + c % 2]
                    if c == 0:
                        nc.vector.tensor_copy(st_p[:, :, :], sbk[:, 0:P].rearrange("p (j t) -> p j t", j=2)).then_inc(hs_r, 1)
                    else:
                        st = st_p if c < NCH else st_s
                        STT(st[:, 0, :], st[:, 0, :], ebl[:, c:c + 1], sbk[:, 0:64], ALU.mult, ALU.add)
                        STT(st[:, 1, :], st[:, 1, :], ebl[:, 5 + c:6 + c], sbk[:, 64:128], ALU.mult, ALU.add).then_inc(hs_r, 1)
                    v.wait_ge(hs_r, NXA * l + c + 1)
                    o_ = ot[:, :, c * P:c * P + rows(c)]
                    TT(o_, o_, BK[c % 2][:, 0:256].rearrange("p (j t) -> p j t", j=2)[:, :, 0:rows(c)], ALU.add).then_inc(ho_e, 1)

                for m in range(NIN):
                    step(a + m + 1)
                    if m == 0:
                        root(2 * pn)
                    place_ = IN_PLACE[m]
                    STT(halves(proj[:, place_, :]), PL[m % 2][:, :, 0:HT], 0.125 if Q0 <= place_ < Q0 + 4 else 1.0, halves(rinv[:, :]),
                        ALU.mult, ALU.mult).then_inc(tile_e, 1)
                    if m == U_FORGET:
                        forget()
                    if m == U_SCAN:
                        scan()
                    if m == U_DIAG:
                        v.wait_ge(dg_d, l + 1)
                        for j in range(2):
                            ins = TT(halves(ot[:, j, :]), PX[j][:, :, 0:HT], halves(proj[:, HI0 + j, :]), ALU.mult)
                        ins.then_inc(dg_e, 1)
                    if 0 < m - U_DIAG <= LEVELS:
                        keep(m - U_DIAG)
                    if 0 < m - U_LEV <= LEVELS:
                        decay(m - U_LEV)
                    if 0 <= m - U_LEV <= LEVELS:
                        exponent(m - U_LEV + 1)
                    if m == U_KEND:
                        v.wait_ge(e_r, ec + LEVELS + 1)
                        TT(hQK[0][:, :, :], kf[:, :, :], hE[:, :, :], ALU.mult).then_inc(kk_r, 1)
                    if m == U_QDEC:
                        v.wait_ge(e_r, ec + LEVELS + 2)
                        TT(hQK[1][:, :, :], q_, hE[:, :, :], ALU.mult).then_inc(qd_r, 1)
                        for c in range(2):
                            nc.vector.tensor_copy(ebl[:, 5 * c:5 * c + 4], hE[:, c, P - 1:SEQ:P])
                            ins = nc.vector.tensor_copy(ebl[:, 5 * c + 4:5 * c + 5], hE[:, c, T - 1:T])
                        link(ins)
                    if 0 <= m - U_OUT < NXA:
                        state(m - U_OUT)
                    if m == U_NORM:
                        v.wait_ge(ors_r, l + 1)
                        for j in range(2):
                            ins = STT(halves(bT[:, j, :]), PX[j][:, :, 0:HT], HD * EPS, halves(hE[:, j, :]), ALU.add, ALU.mult)
                        ins.then_inc(hu_r, 1)
                v.wait_ge(tile_e, tile_base(l, "IN") + NIN)
                v.wait_ge(conv_l, 16 * 2 * (l + 1))
                for c in range(2):
                    link(nc.vector.memset(cu[:, c, 0:2], 0.0))
                    link(TT(cu[:, c, 2:2 + SEQ], proj[:, C0 + c, 0:SEQ], proj[:, H0 + c, 0:SEQ], ALU.mult))
                    TT(cu[:, c, 4 + SEQ:4 + T], proj[:, C0 + c, SEQ:T], proj[:, H0 + c, SEQ:T], ALU.mult).then_inc(cu_r, 1)
                    v.wait_ge(cu_r, 2 * l + c + 1)
                    for s0, c0, n in ((0, 0, SEQ), (SEQ + 2, SEQ, DEC)):
                        link(TS(ct[:, c, c0:c0 + n], cu[:, c, s0:s0 + n], cw(l, 0, c), None, ALU.mult))
                        for j in (1, 2):
                            link(STT(ct[:, c, c0:c0 + n], cu[:, c, s0 + j:s0 + j + n], cw(l, j, c), ct[:, c, c0:c0 + n], ALU.mult, ALU.add))
                link(TT(ct[:, 0, :], ct[:, 0, :], proj[:, B0, :], ALU.mult))
                TT(ct[:, 1, :], ct[:, 1, :], proj[:, B0 + 1, :], ALU.mult).then_inc(cvr, 1)
                v.wait_ge(cvhi, l + 1)
                for c in range(2):
                    TT(mix_lo[:, 4 + c, :], ct[:, c, :], f32(mix_hi[:, 4 + c, :]), ALU.subtract).then_inc(mixlo_r, 1)
                def head_norm(piece):
                    if piece == 0:
                        v.wait_ge(hu_r, l + 1)
                        v.wait_ge(sig_r, 3 * (l + 1))
                        link(TT(bt, bt, hE[:, :, :], ALU.mult))
                        link(TS(bt, bt, -0.5 / HD, 1.5, ALU.mult, ALU.add))
                    elif piece == 1:
                        link(TT(ot[:, :, :], ot[:, :, :], hE[:, :, :], ALU.mult))
                        for c in range(2):
                            ins = STT(ot[:, c, :], ot[:, c, :], gh(l, c), bT[:, c, :], ALU.mult, ALU.mult)
                        link(ins)
                    elif piece == 2:
                        TT(ot[:, :, :], ot[:, :, :], proj[:, HG0:HG0 + 2, :], ALU.mult).then_inc(hgo_r, 1)
                    elif piece == 4:
                        v.wait_ge(hghi, l + 1)
                        for c in range(2):
                            TT(mix_lo[:, 6 + c, :], ot[:, c, :], f32(mix_hi[:, 6 + c, :]), ALU.subtract).then_inc(mixlo_r, 1)

                def softplus(job):
                    z, a_, s_, c_ = SET[job % 2], at_a[job % 2], at_s[job % 2], at_c[job % 2]
                    v.wait_ge(l_r, NJ * l + job + 1)
                    if job >= 2:
                        v.wait_ge(r_d, NJ * l + job - 1)
                    if job < 2:
                        STT(s_[:, 0:2 * SW], z[:, 0:2 * SW], 0.0, a_[:, 0:2 * SW], ALU.max, ALU.add)
                        own = slice(2 * SW, 3 * SW)
                        STT(s_[0:DEC, own], z[0:DEC, own], 0.0, a_[0:DEC, own], ALU.max, ALU.add).then_inc(sp_r, 1)
                        return
                    STT(s_[:, :], z[:, 0:ZW], 0.0, a_[:, :], ALU.max, ALU.add).then_inc(sp_r, 1)
                    v.wait_ge(sp_r, NJ * l + job + 1)
                    o1, o2, o3 = Z_OFF[1], Z_OFF[2], Z_OFF[3]
                    nc.vector.tensor_copy(c_[:, 0:P], s_[:, o2:o2 + P])
                    nc.vector.tensor_copy(c_[:, 256:384], s_[:, o1:o1 + P])
                    link(TT(c_[:, P:256], s_[:, o2 + P:o2 + 256], s_[:, o3:o3 + P], ALU.add))
                    TT(c_[:, 384:640], s_[:, o1 + P:o1 + 384], c_[:, 0:256], ALU.add).then_inc(sum_r, 1)

                def evac(job):
                    bk = BK[6 + job % 2]
                    v.wait_ge(avhi_r, NJ * l + job + 1)
                    if job < 2:
                        r_ = slice(64 * job, 64 * job + 64)
                        TT(mix_lo[r_, 0:4, SEQ:T], bk[r_, 0:256].rearrange("p (q t) -> p q t", q=4), f32(mix_hi[r_, 0:4, SEQ:T]),
                           ALU.subtract).then_inc(avlo_r, 1)
                    else:
                        e, p_ = 64 * (job % 2), (job - 2) // 2
                        TT(mix_lo[e:e + 64, p_, 0:SEQ], bk[e:e + 64, :], f32(mix_hi[e:e + 64, p_, 0:SEQ]), ALU.subtract).then_inc(avlo_r, 1)

                softplus(0)
                softplus(1)
                for job in range(NJ + 1):
                    if job:
                        evac(job - 1)
                    if job + 2 < NJ:
                        softplus(job + 2)
                    if job:
                        head_norm(job - 1)
                v.wait_ge(hst_s, 32 * (l + 1))
                pn = 4 * l + 1
                a = unit_base(l, "OUT")
                v.wait_ge(mrs_r, l + 1)
                link(nc.vector.reciprocal(mss, mss))
                for b in range(2):
                    ins = TS(mtok[:, b, :], mtok[:, b, :], mss[:, b:b + 1], None, ALU.mult)
                    link(ins) if b == 0 else ins.then_inc(mn_r, 1)
                for m in range(KD):
                    step(a + m + 1)
                    y_tile(l, pn, m)
                root(2 * pn + 1)
                for n_ in range(4):
                    v.wait_ge(mhi_r, 4 * l + n_ + 1)
                    for q in range(2):
                        k = 2 * n_ + q
                        ins = STT(m_lo[:, k, :], BK[2 + n_ % 2][:, q * 256:(q + 1) * 256], gmem(l, k), f32(m_hi[:, k, :]), ALU.mult, ALU.subtract)
                    ins.then_inc(mlo_r, 1)
                a = unit_base(l, "MK")
                for m in range(KD):
                    update(pn, m, 1.0)
                    step(a + m + 1)
                    h_lo_piece(pn + 1, m)
                pn = 4 * l + 2
                a = unit_base(l, "MVQ")
                for m in range(KD):
                    step(a + 2 * m + 1)
                    step(a + 2 * m + 2)
                    if m == 0:
                        root(2 * pn)
                    TT(halves(qx[:, m, :]), PL[1][:, :, 0:HT], halves(rinv[:, :]), ALU.mult).then_inc(tile_e, 1)
                def x_max(b):
                    nt, c0 = rows(b), 4 * (b % 2)
                    v.wait_ge(xs_d, NXA * l + b + 1)
                    link(nc.vector.tensor_reduce(mx[0:nt, c0:c0 + 4],
                                                 PL[b % 2][0:nt, :, :].rearrange("p a (q n) -> p (a q) n", q=2), AX.X, ALU.max))
                    TS(mx[0:nt, c0:c0 + 4], mx[0:nt, c0:c0 + 4], -1.0 / 16.0, None, ALU.mult).then_inc(mx_r, 1)

                def x_norm(b):
                    nt, c0 = rows(b), 4 * (b % 2)
                    v.wait_ge(xe_r, 4 * (NXA * l + b + 1))
                    link(nc.vector.reciprocal(rrec[0:nt, c0:c0 + 4], rsum[0:nt, c0:c0 + 4]))
                    for h in range(MH):
                        TS(pr[b % 2][0:nt, h, :], pr[b % 2][0:nt, h, :], rrec[0:nt, c0 + h:c0 + h + 1], None, ALU.mult).then_inc(pn_r, 1)

                x_max(0)
                for b in range(NXA):
                    if b + 1 < NXA:
                        x_max(b + 1)
                    x_norm(b)
                for n_ in range(8):
                    v.wait_ge(xahi_r, 2 * (8 * l + n_ + 1))
                    link(TT(xo_lo[:, n_, 0:SEQ], PL[n_ % 2][:, 0, :], f32(xo_hi[:, n_, 0:SEQ]), ALU.subtract))
                    TT(xo_lo[:, n_, SEQ:T], PL[n_ % 2][:, 1, 0:DEC], f32(xo_hi[:, n_, SEQ:T]), ALU.subtract).then_inc(xalo_r, 1)
                a = unit_base(l, "MO")
                for m in range(KD):
                    step(a + m + 1)
                    y_tile(l, pn, m)
                root(2 * pn + 1)
                for k in range(KD):
                    update(pn, k, 1.0)
                    if k:
                        h_lo_piece(pn + 1, k - 1)
                h_lo_piece(pn + 1, KD - 1)
                ffn(l, "F2", "D2", 4 * l + 3, 2 * l + 1)
                for k in range(KD):
                    update(4 * l + 3, k, 0.5)
                    if k and l + 1 < DEPTH:
                        h_lo_piece(4 * l + 4, k - 1)
                if l + 1 < DEPTH:
                    h_lo_piece(4 * l + 4, KD - 1)

        @block.gpsimd
        def _(pool):
            def add_squares(n):
                for k in range(1, KD - n % 2):
                    c = (KD - 1) * n + k - 1
                    pool.wait_ge(sq_r, KD * n + k + 1)
                    if k > 1:
                        pool.wait_ge(acc_r, added(n) + k - 1)
                    nc.gpsimd.tensor_tensor(acc[:, :], acc[:, :], sq[:, c % 2, :], ALU.add).then_inc(acc_r, 1)

            dma = pool.dma_start
            dma(cst[:, :, :], i["cf"].rearrange("n p m -> p n m")).then_inc(cst_l, 16)
            dma(lst[:, :, :], i["lm"].rearrange("n p m -> p n m")).then_inc(cst_l, 16)
            dma(gst1[0:64, :], i["norm_pre"].rearrange("l n (k p) -> (l n k) p", p=P)).then_inc(cst_l, 16)
            dma(gst1[64:128, :], i["norm_post"].rearrange("l n (k p) -> (l n k) p", p=P)).then_inc(cst_l, 16)
            dma(gst2[0:16, :], i["mem_norm"].rearrange("l (k p) -> (l k) p", p=P)).then_inc(cst_l, 16)
            dma(gst2[16:28, :], i["conv_w"].rearrange("l j (k p) -> (l j k) p", p=P)).then_inc(cst_l, 16)
            dma(gst2[28:32, :], i["hg_lb"].rearrange("l (k p) -> (l k) p", p=P)).then_inc(cst_l, 16)
            dma(gst2[32:36, :], i["hg_norm"].rearrange("l (k p) -> (l k) p", p=P)).then_inc(cst_l, 16)
            dma(xtok[:, 0:NCH, :], i["x_prompt"][0].rearrange("(b p) d -> p b d", p=P)).then_inc(xin_l, 16)
            dma(xtok[0:DEC, NCH, :], i["x_sample"][0]).then_inc(xin_l, 16)
            add_squares(0)
            for l in range(DEPTH):
                add_squares(8 * l + 1)
                add_squares(8 * l + 2)
                pool.wait_ge(tile_e, tile_base(l, "IN"))
                dma(st_s[:, :, :], i["state_hgrn"][l, 0].rearrange("(j e) k v -> (e k) j v", j=2)).then_inc(s0_l, 16)
                pool.wait_ge(hs_r, NXA * (l + 1))
                pool.wait_ge(ho_e, NXA * (l + 1))
                dma(kpast_tok[:, :, :], i["cache_sb_k"][l, 0].rearrange("(b p) h d -> p b (h d)", p=P)).then_inc(cache_l, 16)
                dma(vpast[:, :, :], i["cache_sb_v"][l, 0].rearrange("(b p) h d -> p b (h d)", p=P)).then_inc(cache_l, 16)
                pool.wait_ge(unit_d, unit_base(l, "IN") + NIN)
                for c in range(2):
                    with nc.allow_non_contiguous_dma(reason="two rows of the convolution's state, feature-major"):
                        dma(cu[:, c, SEQ + 2:SEQ + 4], i["state_conv"][l, 0][:, c * P:(c + 1) * P].rearrange("r p -> p r")).then_inc(conv_l, 16)
                dma(o["hg_p"][l, 0].rearrange("(j e) k v -> (e k) j v", j=2), st_p[:, :, :]).then_inc(hst_s, 16)
                dma(o["hg_s"][l, 0].rearrange("(j e) k v -> (e k) j v", j=2), st_s[:, :, :]).then_inc(hst_s, 16)
                pool.wait_ge(tp_e, 12 * l + NXA)
                dma(o["sb_k_p"][l, 0].rearrange("(b p) h d -> p b (h d)", p=P), ktok[:, 0:NCH, :]).then_inc(kout_s, 16)
                dma(o["sb_k_s"][l, 0].rearrange("p h d -> p (h d)"), ktok[0:DEC, NCH, :]).then_inc(kout_s, 16)
                pool.wait_ge(cu_r, 2 * (l + 1))
                for c in range(2):
                    with nc.allow_non_contiguous_dma(reason="two rows of the convolution's state, feature-major"):
                        dma(o["conv_p"][l, 0][:, c * P:(c + 1) * P].rearrange("r p -> p r"), cu[:, c, SEQ:SEQ + 2]).then_inc(mixst_s, 16)
                        dma(o["conv_s"][l, 0][:, c * P:(c + 1) * P].rearrange("r p -> p r"), cu[:, c, T + 2:T + 4]).then_inc(mixst_s, 16)
                pool.wait_ge(tp_e, 12 * (l + 1))
                dma(o["sb_v_p"][l, 0].rearrange("(b p) h d -> p b (h d)", p=P), vtok[:, 0:NCH, :]).then_inc(y_s, 16)
                dma(o["sb_v_s"][l, 0].rearrange("p h d -> p (h d)"), vtok[0:DEC, NCH, :]).then_inc(y_s, 16)
                pool.wait_ge(avlo_r, NJ * (l + 1))
                pool.wait_ge(avhi_r, NJ * (l + 1))
                pool.wait_ge(mixlo_r, 4 * (l + 1))
                pool.wait_ge(y_s, 48 * l + 32)
                dma(mtok[:, :, :], i["mem_prompt"][0].rearrange("(b p) d -> p b d", p=P)).then_inc(mem_l, 16)
                dma(mv_s[:, :, :], i["cache_mem_v"][l, 0].rearrange("(b p) h d -> p b (h d)", p=P)).then_inc(cv_l, 16)
                add_squares(8 * l + 3)
                pool.wait_ge(mt_d, 4 * (l + 1))
                dma(mtok[:, :, :], i["cache_mem_k"][l, 0].rearrange("(b p) h d -> p b (h d)", p=P)).then_inc(ck_l, 16)
                add_squares(8 * l + 4)
                pool.wait_ge(kr_e, 8 * (l + 1))
                dma(o["mem_v"][l, 0].rearrange("(b p) h d -> p b (h d)", p=P), mv_p[:, :, :]).then_inc(y_s, 16)
                dma(o["mem_k"][l, 0].rearrange("(b p) h d -> p b (h d)", p=P), mtok[:, :, :]).then_inc(kr_s, 16)
                add_squares(8 * l + 5)
                pool.wait_ge(y_s, 48 * (l + 1))
                pool.wait_ge(kr_s, 16 * (l + 1))
                add_squares(8 * l + 6)
                add_squares(8 * l + 7)
                if l + 1 < DEPTH:
                    add_squares(8 * l + 8)
            pool.wait_ge(yt_e, 2 * NXA)
            dma(o["y_p"][0].rearrange("(b p) d -> p b d", p=P), xtok[:, 0:NCH, :]).then_inc(y_s, 16)
            dma(o["y_s"][0], xtok[0:DEC, NCH, :]).then_inc(y_s, 16)
            pool.wait_ge(y_s, 48 * DEPTH + 32)
            pool.wait_ge(kout_s, 32 * DEPTH)
            pool.wait_ge(mixst_s, 64 * DEPTH)
            pool.wait_ge(hst_s, 32 * DEPTH)
            pool.wait_ge(kr_s, 16 * DEPTH)


_INS = ["x_prompt", "x_sample", "mem_prompt", "cache_sb_k", "cache_sb_v", "cache_mem_k", "cache_mem_v", "state_conv",
        "state_hgrn", "norm_pre", "norm_post", "ffn1_gu", "ffn1_down", "w_in", "conv_w", "hg_lb", "hg_norm", "w_out",
        "mem_norm", "w_mk", "w_mv", "w_mq", "w_mo", "ffn2_gu", "ffn2_down"]
_OUTS = [("y_p", (1, SEQ, D)), ("y_s", (1, DEC, D)),
         ("sb_k_p", (DEPTH, 1, SEQ, SBH, HD)), ("sb_v_p", (DEPTH, 1, SEQ, SBH, HD)),
         ("conv_p", (DEPTH, 1, 2, 256)), ("hg_p", (DEPTH, 1, 4, 64, 64)),
         ("mem_k", (DEPTH, 1, NMEM, MH, MHD)), ("mem_v", (DEPTH, 1, NMEM, MH, MHD)),
         ("sb_k_s", (DEPTH, 1, DEC, SBH, HD)), ("sb_v_s", (DEPTH, 1, DEC, SBH, HD)),
         ("conv_s", (DEPTH, 1, 2, 256)), ("hg_s", (DEPTH, 1, 4, 64, 64))]


def constants():
    import numpy as np
    s, t = np.arange(P)[:, None], np.arange(P)[None, :]
    cf = np.stack([s == t, -1.0 * (s >= t), -np.ones((P, P)), np.ones((P, P)), s // 64 == t // 64]).astype(np.float32)
    lm = np.stack([((s ^ t) >> (n - 1) == 1) & (t > s) for n in range(1, LEVELS + 1)]
                  + [NEG * (t <= s)]).astype(np.float32)
    return cf, lm


def kernel(**inputs):
    import numpy as _np
    import concourse.bacc as _bacc
    from concourse import mybir as _mybir
    from concourse.bass_utils import run_bass_kernel_spmd as _run

    nc = _bacc.Bacc("TRN2", target_bir_lowering=False, num_devices=1)
    arrays, ins, outs = {}, {}, {}
    given = {name: _np.ascontiguousarray(inputs[name]) for name in _INS}
    given["cf"], given["lm"] = constants()
    for name, a in given.items():
        arrays[f"in_{name}_dram"] = a
        ins[name] = nc.dram_tensor(f"in_{name}_dram", a.shape, _mybir.dt.from_np(a.dtype), kind="ExternalInput").ap()
    for n, (name, shape) in enumerate(_OUTS):
        outs[name] = nc.dram_tensor(f"out_{n}_dram", shape, _mybir.dt.from_np(_np.dtype("float32")), kind="ExternalOutput").ap()
    hybrid_trunk(nc, ins, outs)
    r = _run(nc, [arrays], core_ids=[0])
    return tuple(r.results[0][f"out_{n}_dram"] for n in range(len(_OUTS)))
```

```python
from contextlib import ExitStack

import concourse.bass as bass
from concourse import mybir

F32 = mybir.dt.float32
F32R = mybir.dt.float32r
BF16 = mybir.dt.bfloat16
U8 = mybir.dt.uint8
ALU = mybir.AluOpType
ACT = mybir.ActivationFunctionType
AX = mybir.AxisListType

P = 128
D = 1024
DEPTH = 2
KD = D // P
SEQ, DEC, PAST, NMEM = 512, 64, 256, 256
T = SEQ + DEC
HT = T // 2
FF = 2816
KF = FF // P
KU = KF // 2
SBH, HD = 8, 64
NCH = SEQ // P
EPS = 1e-6
F_FLOOR = 1e-30
NEG = -1e30
LN_SPLIT = 2.0 ** -60
MH, MHD = 4, 256

Q0, B0, HQ0, K0, C0, HF0, H0, HG0, V0, HI0 = 0, 4, 6, 8, 12, 14, 16, 18, 20, 24
IN_PLACE = ([HQ0, HQ0 + 1, HF0, HF0 + 1, HI0, HI0 + 1, HG0, HG0 + 1]
            + [Q0 + i for i in range(4)] + [K0 + i for i in range(4)] + [V0 + i for i in range(4)]
            + [B0, B0 + 1, C0, C0 + 1, H0, H0 + 1])
NHG = 8
NIN = len(IN_PLACE)

PHASES = [("F1", 2 * KF, KD), ("D1", 2 * KD, KU), ("IN", NIN, KD), ("OUT", KD, KD), ("MK", KD, KD),
          ("MVQ", 2 * KD, KD), ("MO", KD, KD), ("F2", 2 * KF, KD), ("D2", 2 * KD, KU)]
UNITS = sum(n for _, n, _ in PHASES)
TILES = {"F1": 2 * KF, "D1": KD, "IN": NIN, "OUT": KD, "MK": 0, "MVQ": KD, "MO": KD, "F2": 2 * KF, "D2": KD}
NT = sum(TILES.values())
Z_OFF = [0, SEQ, 2 * SEQ, 2 * SEQ - P]
ZW = 2 * SEQ + 2 * P
SW = SBH // 2 * DEC
LEVELS = 7
U_SIG, U_FORGET, U_LN, U_SCAN, U_GATE, U_ITOK, U_DIAG = 4, 5, 6, 7, 8, 9, 10
U_LEV = 8
U_KEND = U_LEV + LEVELS + 1
U_QDEC = U_KEND + 1
U_KTOK = U_KEND + 2
U_OUT = U_KTOK + 1
U_SQ, U_NORM = U_OUT + NCH, U_OUT + NCH + 1


def unit_base(l, phase):
    names = [p[0] for p in PHASES]
    return l * UNITS + sum(n for _, n, _ in PHASES[:names.index(phase)])


def tile_base(l, phase):
    names = [p[0] for p in PHASES]
    return l * NT + sum(TILES[n] for n in names[:names.index(phase)])


def unit_words(u):
    u %= UNITS
    for _, n, k in PHASES:
        if u < n:
            return k * P
        u -= n


NRING = 3 * KD


def ring_place(u):
    at = u % UNITS - unit_base(0, "MK") if isinstance(u, int) else NRING
    return at if 0 <= at < NRING else None


def slot_of(u):
    return u % 2 if ring_place(u) is None else ring_place(u) % 3


def hybrid_trunk(nc, i, o):
    ctx = ExitStack()
    with ctx:
        def place(name, shape, dt, words):
            return nc.alloc_sbuf_tensor_at(name, shape, dt, offset=16512 + 4 * words)

        x = place("x", [P, KD, T], F32, 0)
        H = KD * T
        h_hi = place("h_hi", [P, KD, T], F32R, H)
        h_lo = place("h_lo", [P, KD, T], F32R, H + KD * T)
        y = place("y", [P, KD, T], F32, H + KD * T)
        G = H + 2 * KD * T
        a_hi = place("a_hi", [P, KF, T], F32R, G)
        a_lo = place("a_lo", [P, KF, T], F32R, G + KF * T)
        proj = place("proj", [P, NIN, T], F32, G)
        mix_hi = place("mix_hi", [P, KD, T], F32R, G)
        mix_lo = place("mix_lo", [P, KD, T], F32R, G + KD * T)
        g = G + NIN * T
        vtok = place("vtok", [P, NCH + 1, 512], F32, g)
        kpast = place("kpast", [P, 4, PAST], F32, g + 6144)
        vpast = place("vpast", [P, 2, 512], F32, g + 7168)
        kpast_tok = place("kpast_tok", [P, 2, 512], F32, g + 8192)
        ktok = place("ktok", [P, NCH + 1, 512], F32, H + 4608)
        at_a, at_s, at_w, at_c = ([place(f"at_{n}{s}", [P, w], F32, H + 4480 * s + w0) for s in range(2)]
                                  for n, w, w0 in (("a", ZW, 0), ("s", ZW, ZW), ("w", ZW, 2 * ZW), ("c", 640, 3 * ZW)))
        cu0 = place("cu0", [P, T + 4], F32, g + 2560)
        ct = place("ct", [P, 2, T], F32, g + 9216)
        sacc = place("sacc", [P, 4 * SEQ], F32, g)
        kotok = place("kotok", [P, NCH + 1, 256], F32, g + 2048)
        hE = place("hE", [P, 2, T], F32, g + 3328)
        ot = place("ot", [P, 2, T], F32, g + 4480)
        kf = place("kf", [P, 2, T], F32, g + 5632)
        hQK = [place(f"hQK{s}", [P, 2, T], F32, g + 6784 + 1152 * s) for s in range(2)]
        itok = place("itok", [P, NCH + 1, 256], F32, g + 9088)
        qx = place("qx", [P, KD, T], F32, G)
        xo_hi = place("xo_hi", [P, KD, T], F32R, G)
        xo_lo = place("xo_lo", [P, KD, T], F32R, G + 4608)
        mtok = place("mtok", [P, 2, D], F32, G + 9216)
        m_hi = place("m_hi", [P, KD, NMEM], F32R, G + 11264)
        m_lo = place("m_lo", [P, KD, NMEM], F32R, G + 13312)
        mk_p = place("mk_p", [P, KD, NMEM], F32, G + 15360)
        mv_p = place("mv_p", [P, 2, D], F32, G + 17408)
        mk_s = place("mk_s", [P, KD, NMEM], F32, G + 19456)
        mv_s = place("mv_s", [P, 2, D], F32, G + 21504)
        w3_hi = place("w3_hi", [P, KD * P], F32R, G + 6656)
        w3_lo = place("w3_lo", [P, KD * P], F32R, G + 7680)
        raw3 = place("raw3", [P, KD * P], F32, G + 23552)
        pr = [place(f"pr{s}", [P, MH, NMEM], F32, H + 1024 * s) for s in range(2)]
        pT = place("pT", [P, 8, T], F32, H + 2048)
        mvT = place("mvT", [P, KD, NMEM], F32, G + 4608)
        xtok = place("xtok", [P, NCH + 1, D], F32, G)
        gst1 = place("gst1", [P, P], F32, G + 5120)
        gst2 = place("gst2", [P, P], F32, G + 5248)
        lst = place("lst", [P, LEVELS + 1, P], F32, G + 5376)
        W = G + 2 * KF * T
        raw = place("raw", [P, 2, KU * P], F32, W)
        w_hi = place("w_hi", [P, 2, KU * P], F32R, W + 2 * KU * P)
        w_lo = place("w_lo", [P, 2, KU * P], F32R, W + 4 * KU * P)
        M = W + 6 * KU * P
        sq = place("sq", [P, 2, T], F32, M)
        cu = [cu0, place("cu1", [P, T + 4], F32, M)]
        gt = place("gt", [P, T], F32, M + 2 * T)
        sg = place("sg", [P, T], F32, M + 3 * T)
        ut = place("ut", [P, T], F32, M + 4 * T)
        bT = place("bT", [P, 2, T], F32, M + 2 * T)
        st_p = place("st_p", [P, 2, HD], F32, M + 4 * T)
        st_s = place("st_s", [P, 2, HD], F32, M + 4 * T + P)
        sacc_s = place("sacc_s", [P, 4 * DEC], F32, M + 4 * T + 2 * P)
        acc = place("acc", [P, T], F32, M + 5 * T)
        rinv = place("rinv", [P, T], F32, M + 6 * T)
        m0 = M + 7 * T
        cst = place("cst", [P, 5, P], F32, m0)
        lmask = place("lmask", [P, LEVELS, P], U8, m0 + 640)
        par = place("par", [P, 164], F32, m0 + 896)
        small = place("small", [P, 80], F32, m0 + 1064)
        identb = place("identb", [P, P], BF16, m0 + 1144)
        negb = place("negb", [P, P], BF16, m0 + 1208)
        ident, ntri, nones, ones, bones = (cst[:, n, :] for n in range(5))
        eps = small[:, 0:1]
        lbv = small[:, 1:5]
        oml = small[:, 5:9]
        lt = small[:, 9:21]
        mss = small[:, 21:23]
        mtk, rtok, ntk = small[:, 34:39], small[:, 39:44], small[:, 44:49]
        ebl = small[:, 24:34]
        mx = small[:, 49:57]
        rsum = small[:, 57:65]
        rrec = small[:, 65:73]

        PS = ctx.enter_context(nc.psum_tensor("PS", [P, 8, 512], F32))
        BK = [PS[:, n, :] for n in range(8)]
        PX = [PS[:, 2 * n:2 * n + 2, :] for n in range(2)]
        PL = [PS[:, 4 + 2 * n:6 + 2 * n, :] for n in range(2)]
        SET = [PS[:, 3 * n:3 * n + 3, :].rearrange("p b t -> p (b t)") for n in range(2)]

        def sem(name):
            return ctx.enter_context(nc.semaphore(name))

        cst_l = sem("cst_loaded")
        id_l, lm_l = sem("constants_loaded"), sem("masks_loaded")
        xin_l = [sem(f"x_loaded{c}") for c in range(4)]
        w_l = [sem(f"w_loaded{s}") for s in range(2)]
        wr_l = [sem(f"ring_w_loaded{s}") for s in range(3)]
        whi_r, wlo_r = sem("w_hi_ready"), sem("w_lo_ready")
        unit_d = sem("unit_products_done")
        tile_e = sem("psum_tile_emptied")
        mkv_e = sem("memory_tile_emptied")
        sq_r, acc_r, ms_r, rs_r, ye_r, mt_r, y0_r, rt_r, bc_d = (sem(n) for n in ("square_ready", "squares_added", "mean_square_ready",
                                                            "rinv_ready", "rinv_estimated", "mean_squares_by_token", "root_estimated", "root_refined", "rinv_spread"))
        x_r, hi_r, lo_r = sem("x_ready"), sem("h_hi_ready"), sem("h_lo_ready")
        y_r, yp_r = sem("even_y_scaled"), sem("odd_y_scaled")
        xt_d = sem("x_transposed")
        par_d, par_r = sem("gains_transposed"), sem("gains_ready")
        sg_r, pr_r, ahi_r, alo_r = (sem(n) for n in ("silu_ready", "inner_ready", "a_hi_ready", "a_lo_ready"))
        dch, ach = sem("vector_step"), sem("scalar_step")
        cache_l, conv_l = sem("caches_loaded"), sem("conv_state_loaded")
        tp_d, tp_e = sem("token_major_done"), sem("token_major_emptied")
        kout_s = sem("k_rows_stored")
        mixst_s = sem("mix_outputs_stored")
        cu_r, cvr, cvhi = sem("conv_input_ready"), sem("conv_ready"), sem("conv_hi_ready")
        sig_r, f_r, ln_r = sem("sigmoids_ready"), sem("forget_ready"), sem("logs_ready")
        e_in, e_r, qk_r = sem("decay_exponent_ready"), sem("decay_ready"), sem("decayed_qk_ready")
        sc_d, sc_e = sem("scores_done"), sem("scores_kept")
        it_d, it_e, qk0_r, dg_d, dg_e, qd_r, hu_r = (sem(n) for n in (
            "i_transposed", "i_rows_ready", "qk_own_ready", "diagonal_done", "diagonal_used", "q_decayed", "newton_begun"))
        kk_r, kt_d, kt_e = sem("kout_ready"), sem("kout_transposed"), sem("kout_emptied")
        hs_d, hs_r, ho_e = sem("hg_chunk_done"), sem("hg_state_ready"), sem("hg_out_emptied")
        s0_l, hst_s = sem("hg_state_loaded"), sem("hg_state_stored")
        osq_r, oms_d, ors_r, hgo_r, hghi = (sem(n) for n in ("o_square_ready", "o_mean_done", "o_root_ready", "o_gated", "o_hi_ready"))
        mixlo_r = sem("mix_lo_ready")
        z_d, l_r, sp_r, sum_r, r_d, wx_r, av_d, avhi_r, avlo_r = (
            sem(n) for n in ("z_done", "log1p_ready", "softplus_ready", "later_tiles_summed", "rest_done", "weights_ready",
                             "attended", "attended_hi", "attended_lo"))
        mem_l, mss_r, mrs_r, mn_r, mt_d, mhi_r, mlo_r = (
            sem(n) for n in ("mem_loaded", "mem_squares", "mem_root", "mem_normed", "mem_transposed", "m_hi_ready", "m_lo_ready"))
        ck_l, cv_l, ck_d, ck_e, kr_d, kr_e, kr_s = (
            sem(n) for n in ("cache_k_loaded", "cache_v_loaded", "cache_k_transposed", "cache_k_emptied",
                             "k_rows_done", "k_rows_emptied", "mem_k_stored"))
        xs_d, mx_r, xe_r, pn_r, pt_d, pt_e, xa_d, xahi_r, xalo_r = (
            sem(n) for n in ("x_scores_done", "x_max_ready", "x_exp_ready", "x_probs_ready", "probs_transposed",
                             "probs_emptied", "x_attended", "x_attended_hi", "x_attended_lo"))
        yt_d, yt_e, y_s = sem("y_transposed"), sem("y_emptied"), sem("y_stored")

        rings_before = lambda u: u // UNITS + (u % UNITS >= unit_base(0, "MK") + NRING)
        rawu = lambda s, c: raw[:, s, c] if s < 2 else raw3[:, c]
        whi = lambda s, c: w_hi[:, s, c] if s < 2 else w3_hi[:, c]
        wlo = lambda s, c: w_lo[:, s, c] if s < 2 else w3_lo[:, c]
        gpre = lambda l, n, k: par[:, (l * 4 + n) * 8 + k:(l * 4 + n) * 8 + k + 1]
        gpost = lambda l, n, k: par[:, 64 + (l * 4 + n) * 8 + k:64 + (l * 4 + n) * 8 + k + 1]
        gmem = lambda l, k: par[:, 128 + l * 8 + k:129 + l * 8 + k]
        cw = lambda l, j, c: par[:, 144 + l * 6 + j * 2 + c:145 + l * 6 + j * 2 + c]
        gh = lambda l, c: par[:, 160 + l * 2 + c:161 + l * 2 + c]

        added = lambda n: (2 * KD - 3) * (n // 2) + (KD - 1) * (n % 2)
        def part(ap, n, second):
            w = 1 << n
            c0 = w // 2 * second
            if n < LEVELS:
                return ap[:, :, :].rearrange("p c (n w) -> p (c n) w", w=w)[:, :, c0:c0 + w // 2]
            return ap[:, :, 0:SEQ].rearrange("p c (n w) -> p c n w", w=w)[:, :, :, c0:c0 + w // 2]

        flat = lambda pair: pair.rearrange("p b t -> p (b t)")
        halves = lambda ap: ap.rearrange("p (h t) -> p h t", h=2)
        POST = {"D1": 0, "OUT": 1, "MO": 2, "D2": 3}
        NU = DEPTH * UNITS
        NXA = NCH + 1
        rows = lambda b: P if b < NCH else DEC
        NJ = 2 + SBH

        block = ctx.enter_context(nc.Block())

        @block.sync
        def _(sp):
            def view(w):
                return w.rearrange("(k p) m -> p k m", p=P)

            sp.dma_start(cst[:, :, :], i["cf"].rearrange("n p m -> p n m")).then_inc(id_l, 16)
            for c in range(4):
                cols = slice(c * 256, (c + 1) * 256)
                sp.dma_start(xtok[:, 0:NCH, cols], i["x_prompt"][0].rearrange("(b p) d -> p b d", p=P)[:, :, cols]).then_inc(xin_l[c], 16)
                sp.dma_start(xtok[0:DEC, NCH, cols], i["x_sample"][0][:, cols]).then_inc(xin_l[c], 16)

            def stream(a, n, kt, src):
                def load(r, s):
                    sp.dma_start(raw[:, s, 0:kt * P].rearrange("p (k m) -> p k m", k=kt), src(r, s)).then_inc(w_l[s], 16)
                first = 0
                if a == 0:
                    load(0, 0)
                    load(0, 1)
                    first = 1
                with sp.Fori(first, n // 2) as r:
                    for s in range(2):
                        sp.wait_ge(wlo_r, r * 2 + (a + s - 1))
                        load(r, s)

            for l in range(DEPTH):
                for f, (pu, pd, gu, dn) in enumerate((("F1", "D1", i["ffn1_gu"], i["ffn1_down"]),
                                                      ("F2", "D2", i["ffn2_gu"], i["ffn2_down"]))):
                    if f == 1:
                        for ph, w in (("IN", "w_in"), ("OUT", "w_out"), ("MK", "w_mk"), ("MO", "w_mo")):
                            v = view(i[w][l])
                            if ph == "IN":
                                a = unit_base(l, ph)
                                c0 = (NIN - NHG) * P
                                stream(a, NHG, KD, lambda r, s, v=v: v[:, :, bass.ds(r * 256 + (c0 + s * P), P)])
                                stream(a + NHG, NIN - NHG, KD, lambda r, s, v=v: v[:, :, bass.ds(r * 256 + s * P, P)])
                                continue
                            if ph == "MK":
                                mv, mq = view(i["w_mv"][l]), view(i["w_mq"][l])
                                tiles = [(v, m) for m in range(KD)] + [(w_, m) for m in range(KD) for w_ in (mv, mq)]
                                for n, (w_, m) in enumerate(tiles):
                                    a, s = unit_base(l, ph), n % 3
                                    sp.wait_ge(wlo_r, a + n - 1 if n < 2 else a if n == 2 else a + n - 2)
                                    sp.dma_start(rawu(s, slice(0, KD * P)).rearrange("p (k m) -> p k m", k=KD),
                                                 w_[:, :, m * P:(m + 1) * P]).then_inc(wr_l[s], 16)
                                continue
                            stream(unit_base(l, ph), KD, KD, lambda r, s, v=v: v[:, :, bass.ds(r * 256 + s * P, P)])
                    v = view(gu[l])
                    stream(unit_base(l, pu), 2 * KF, KD, lambda r, s, v=v: v[:, :, bass.ds(r * P + s * FF, P)])
                    v = view(dn[l])
                    stream(unit_base(l, pd), 2 * KD, KU, lambda r, s, v=v: v[:, s * KU:(s + 1) * KU, bass.ds(r * P, P)])

        @block.tensor
        def _(pe):
            mm = nc.tensor.matmul

            def products(s, kt, out, lhs, rhs, first, last):
                n = 0
                for k in range(kt):
                    for a, b in ((0, 0), (0, 1), (1, 0)):
                        m = mm(out, lhs(a, k), rhs(b, k), start=(first and n == 0), stop=(last and n == 3 * kt - 1))
                        n += 1
                return m

            wt = lambda s: (lambda part, k: (whi, wlo)[part](s, slice(k * P, (k + 1) * P)))

            def unit(u, s, hi, lo, kt=KD, k0=0, first=True, last=True, slot=None, gate=None, middle=None, ws=None):
                pe.wait_ge(wlo_r, u + 1)
                slot = s if slot is None else slot
                ws = s if ws is None else ws
                n = 0
                for k in range(kt):
                    if gate:
                        gate(hi_r, k)
                    if middle and k in middle:
                        middle[k]()
                    for a, b in ((0, 0), (1, 0), (0, 1)):
                        if gate and b:
                            gate(lo_r, k)
                        for h in range(2):
                            m = mm(PL[slot][:, h, 0:HT], wt(ws)(a, k), (hi, lo)[b][:, k0 + k, h * HT:(h + 1) * HT],
                                   start=(first and n == 0), stop=(last and n == 3 * kt - 1))
                        n += 1
                m.then_inc(unit_d, 1)

            def mean_square(n):
                pe.wait_ge(acc_r, added(n + 1))
                if n:
                    pe.wait_ge(rs_r, n)
                if n % 2 == 0:
                    for h in range(2):
                        m = mm(PX[0][:, h, 0:HT], ones, acc[:, h * HT:(h + 1) * HT], start=True, stop=True)
                    m.then_inc(ms_r, 1)
                    return
                parts = [acc[:, :], sq[:, ((KD - 1) * (n + 1) - 1) % 2, :]]
                for part in parts:
                    if part is not parts[0]:
                        pe.wait_ge(sq_r, KD * (n + 1))
                    for b in range(NXA):
                        c0 = b * P if b < NCH else T - P
                        m = mm(PX[0][:, 1, 504 + b:505 + b], part[:, c0:c0 + P], ones[:, 0:1], start=(b == 0 and part is parts[0]),
                               stop=(part is parts[-1]), skip_group_check=True)
                m.then_inc(ms_r, 1)

            def spread(n):
                pe.wait_ge(rt_r, n // 2 + 1)
                for b in range(NXA):
                    r0 = P - rows(b)
                    m = mm(PX[0][:, b // NCH, (b % NCH) * P:(b % NCH) * P + rows(b)], rtok[r0:P, b:b + 1].broadcast_to([rows(b), P]),
                           cst[r0:P, 0, r0:P], start=True, stop=True, skip_group_check=True)
                m.then_inc(bc_d, 1)

            def h_gate(pn):
                def gate(ready, k):
                    pe.wait_ge(ready, KD * pn + k + 1)
                return gate

            def norm_beside(pn):
                return {1: lambda: mean_square(2 * pn)}

            def ffn(l, pu, pd, pn, f):
                a, t = unit_base(l, pu), tile_base(l, pu)
                for s in range(2):
                    if t + s >= 2:
                        pe.wait_ge(tile_e, t + s - 1)
                    unit(a + s, s, h_hi, h_lo, gate=h_gate(pn) if s == 0 else None, middle=norm_beside(pn) if s else None)
                with pe.Fori(1, KF) as r:
                    for s in range(2):
                        pe.wait_ge(tile_e, r * 2 + (t + s - 1))
                        unit(r * 2 + (a + s), s, h_hi, h_lo)
                b, t = unit_base(l, pd), tile_base(l, pd)
                for m in range(KD):
                    pe.wait_ge(tile_e, t + m - 1)
                    for s in range(2):
                        if m == 0:
                            pe.wait_ge(alo_r, KF * f + (KU if s == 0 else KF))
                            pe.wait_ge(ahi_r, KF * f + (KU if s == 0 else KF))
                        unit(b + 2 * m + s, s, a_hi, a_lo, kt=KU, k0=s * KU, first=(s == 0), last=(s == 1), slot=m % 2)
                mean_square(2 * pn + 1)
                spread(2 * pn + 1)

            pe.wait_ge(id_l, 16)
            pe.wait_ge(cst_l, 16 * 6)
            nc.tensor.transpose(BK[0][:, 0:P], gst1[:, :], ident)
            nc.tensor.transpose(BK[1][:, 0:36], gst2[0:36, :], cst[0:36, 0, 0:36]).then_inc(par_d, 1)
            for k in range(KD):
                pe.wait_ge(xin_l[k // 2], 32)
                if k >= 2:
                    pe.wait_ge(x_r, k - 1)
                for b in range(NXA):
                    m = nc.tensor.transpose(PL[k % 2][:, b // NCH, (b % NCH) * P:(b % NCH) * P + rows(b)],
                                            xtok[0:rows(b), b, k * P:(k + 1) * P], cst[0:rows(b), 0, 0:rows(b)])
                m.then_inc(xt_d, 1)
            for l in range(DEPTH):
                if l == 0:
                    pe.wait_ge(x_r, KD)
                ffn(l, "F1", "D1", 4 * l, 2 * l)
                pn = 4 * l + 1
                a, t = unit_base(l, "IN"), tile_base(l, "IN")
                for s in range(2):
                    pe.wait_ge(tile_e, t + s - 1)
                    unit(a + s, s, h_hi, h_lo, gate=h_gate(pn) if s == 0 else None, middle=norm_beside(pn) if s else None)
                with pe.Fori(1, NHG // 2) as r:
                    for s in range(2):
                        pe.wait_ge(tile_e, r * 2 + (t + s - 1))
                        unit(r * 2 + (a + s), s, h_hi, h_lo)

                def i_rows():
                    pe.wait_ge(tile_e, t + NHG)
                    pe.wait_ge(rs_r, 2 * pn + 1)
                    for b in range(NXA):
                        for q in range(2):
                            m = nc.tensor.transpose(flat(PX[b // 4])[0:rows(b), b % 4 * 256 + q * P:b % 4 * 256 + (q + 1) * P],
                                                    proj[:, HI0 + q, b * P:b * P + rows(b)], ident)
                    m.then_inc(it_d, 1)

                def diagonal():
                    pe.wait_ge(it_e, 2 * (l + 1))
                    pe.wait_ge(qk0_r, l + 1)
                    for j in range(2):
                        for h in range(2):
                            m = mm(PX[j][:, h, 0:HT], bones, hQK[0][:, j, h * HT:(h + 1) * HT], start=True, stop=True)
                    m.then_inc(dg_d, 1)

                def level(n):
                    pe.wait_ge(qk_r, LEVELS * l + n)
                    if n == 1:
                        pe.wait_ge(dg_e, l + 1)
                    else:
                        pe.wait_ge(sc_e, LEVELS * l + n - 1)
                    w = 1 << n
                    for c in range(NXA if n < LEVELS else NCH):
                        nt, c0 = rows(c), c * P
                        for h in range(4):
                            e, j = 64 * (h % 2), h // 2
                            o0 = j * 256 + (c % NCH) * 64
                            qq = hQK[n % 2][e:e + 64, j, c0:c0 + nt].rearrange("p (n w) -> p n w", w=w)[:, :, w // 2:w]
                            m = mm(PX[c // NCH][0:nt, h % 2, o0:o0 + nt // 2].rearrange("p (n w) -> p n w", w=w // 2),
                                   hQK[n % 2][e:e + 64, j, c0:c0 + nt], qq, start=True, stop=True)
                    m.then_inc(sc_d, 1)

                def k_rows():
                    pe.wait_ge(kk_r, l + 1)
                    pe.wait_ge(sc_e, LEVELS * (l + 1))
                    for c in range(NXA):
                        for j in range(2):
                            m = nc.tensor.transpose(flat(PX[c // 4])[0:rows(c), c % 4 * 256 + j * P:c % 4 * 256 + (j + 1) * P],
                                                    hQK[0][:, j, c * P:c * P + rows(c)], ident)
                    m.then_inc(kt_d, 1)

                def chunk(c):
                    nt, c0 = rows(c), c * P
                    st = st_p if c < NCH else st_s
                    if c == 0:
                        pe.wait_ge(kt_e, 2 * (l + 1))
                        pe.wait_ge(qd_r, l + 1)
                        pe.wait_ge(s0_l, 16 * (l + 1))
                    else:
                        pe.wait_ge(hs_r, NXA * l + c)
                    if c >= 2:
                        pe.wait_ge(ho_e, NXA * l + c - 1)
                    ob, sbk = BK[c % 2], BK[2 + c % 2]
                    for h in range(4):
                        e, j = 64 * (h % 2), h // 2
                        q = 2 * (h % 2) + j
                        inter = c > 0
                        own = sacc[:, q * SEQ + c0:q * SEQ + c0 + P] if c < NCH else sacc_s[:, q * DEC:(q + 1) * DEC]
                        mm(ob[e:e + 64, j * P:j * P + nt], itok[:, c, h * 64:(h + 1) * 64], own, start=True, stop=not inter)
                        if inter:
                            mm(ob[e:e + 64, j * P:j * P + nt], st[e:e + 64, j, :], hQK[1][e:e + 64, j, c0:c0 + nt],
                                   start=False, stop=True)
                    for h in range(4):
                        e, j = 64 * (h % 2), h // 2
                        m = mm(sbk[e:e + 64, j * 64:(j + 1) * 64], kotok[0:nt, c, h * 64:(h + 1) * 64],
                               itok[0:nt, c, h * 64:(h + 1) * 64], start=True, stop=True)
                    m.then_inc(hs_d, 1)

                def head_squares():
                    pe.wait_ge(osq_r, l + 1)
                    for j in range(2):
                        for h in range(2):
                            m = mm(PX[j][:, h, 0:HT], bones, hE[:, j, h * HT:(h + 1) * HT], start=True, stop=True)
                    m.then_inc(oms_d, 1)

                for m in range(NHG, NIN):
                    beside = {}
                    if m == U_ITOK:
                        beside[6] = i_rows
                    elif m == U_DIAG:
                        beside[6] = diagonal
                    elif U_DIAG < m <= U_DIAG + LEVELS:
                        n = m - U_DIAG
                        beside[6] = lambda n=n: level(n)
                    elif m == U_KTOK:
                        beside[6] = k_rows
                    elif U_OUT <= m < U_OUT + NXA:
                        beside[6] = lambda c=m - U_OUT: chunk(c)
                    elif m == U_NORM:
                        beside[6] = head_squares
                    pe.wait_ge(tile_e, t + m - 1)
                    unit(a + m, m % 2, h_hi, h_lo, middle=beside)
                pe.wait_ge(tile_e, t + NIN - 1)
                pe.wait_ge(hu_r, l + 1)
                def rows_of(n, bank, first):
                    b = n % NXA
                    c0 = b * P if b < NCH else SEQ
                    for q in range(4):
                        m = nc.tensor.transpose(BK[bank][0:rows(b), q * P:(q + 1) * P],
                                                proj[:, first + q, c0:c0 + rows(b)], ident)
                    m.then_inc(tp_d, 1)

                for n in range(NXA):
                    if n >= 4:
                        pe.wait_ge(tp_e, 12 * l + n - 3)
                    rows_of(n, n % 4, K0)
                pe.wait_ge(cache_l, 32 * (l + 1))
                for half in range(2):
                    n = NXA + half
                    pe.wait_ge(tp_e, 12 * l + n - 3)
                    for q in range(2):
                        for b in range(2):
                            m = nc.tensor.transpose(BK[n % 4][:, (2 * q + b) * P:(2 * q + b + 1) * P],
                                                    kpast_tok[:, b, (2 * half + q) * P:(2 * half + q + 1) * P], ident)
                    m.then_inc(tp_d, 1)
                pe.wait_ge(tp_e, 12 * l + NXA + 2)
                def scores(job):
                    z = SET[job % 2]
                    if job >= 2:
                        pe.wait_ge(wx_r, NJ * l + job - 1)
                    if job < 2:
                        e = 64 * job
                        for j in range(3):
                            nk = P if j < 2 else DEC
                            for h in range(job, SBH, 2):
                                ks = (kpast[e:e + 64, h // 2, j * P:(j + 1) * P] if j < 2
                                      else proj[e:e + 64, K0 + h // 2, SEQ:T])
                                c0 = j * SW + h // 2 * DEC
                                mm(z[0:nk, c0:c0 + DEC], ks, proj[e:e + 64, Q0 + h // 2, SEQ:T],
                                   start=(h == job and j != 1), stop=True, skip_group_check=True)
                        for q in range(SBH // 2):
                            m = mm(z[0:DEC, 2 * SW + q * DEC:2 * SW + (q + 1) * DEC], identb[e:e + 64, e:e + 64], negb[e:e + 64, e:e + 64],
                                   start=False, stop=True, skip_group_check=True)
                    else:
                        h = job - 2
                        e = 64 * (h % 2)
                        for j in range(NCH):
                            mm(z[:, Z_OFF[j]:Z_OFF[j] + SEQ - j * P], proj[e:e + 64, K0 + h // 2, j * P:(j + 1) * P],
                               proj[e:e + 64, Q0 + h // 2, j * P:SEQ], start=(j < 3), stop=True, skip_group_check=True)
                        for j in range(NCH):
                            m = mm(z[:, Z_OFF[j]:Z_OFF[j] + P], identb[:, :], negb[:, :], start=False, stop=True, skip_group_check=True)
                    m.then_inc(z_d, 1)

                def rest(job):
                    z, s, c = SET[job % 2], at_s[job % 2], at_c[job % 2]
                    pe.wait_ge(sp_r, NJ * l + job + 1)
                    if job < 2:
                        for j in range(3):
                            nk = P if j < 2 else DEC
                            m = mm(z[0:nk, j * SW:(j + 1) * SW], ntri[0:nk, 0:nk], s[0:nk, j * SW:(j + 1) * SW], start=False, stop=True,
                               skip_group_check=True)
                            for j2 in range(j + 1, 3):
                                n2 = P if j2 < 2 else DEC
                                m = mm(z[0:nk, j * SW:(j + 1) * SW], nones[0:n2, 0:nk], s[0:n2, j2 * SW:(j2 + 1) * SW], start=False,
                                       stop=True, skip_group_check=True)
                    else:
                        for c0 in range(0, ZW, 512):
                            c1 = min(c0 + 512, ZW)
                            mm(z[:, c0:c1], ntri, s[:, c0:c1], start=False, stop=True, skip_group_check=True)
                        pe.wait_ge(sum_r, SBH * l + job - 1)
                        for j, later in ((2, s[:, Z_OFF[3]:Z_OFF[3] + P]), (1, c[:, 0:256]), (0, c[:, 256:640])):
                            m = mm(z[:, Z_OFF[j] + P:Z_OFF[j] + SEQ - j * P], nones, later, start=False, stop=True, skip_group_check=True)
                    m.then_inc(r_d, 1)

                def attend(job):
                    bk, w = BK[6 + job % 2], at_w[job % 2]
                    pe.wait_ge(wx_r, NJ * l + job + 1)
                    if job >= 2:
                        pe.wait_ge(avhi_r, NJ * l + job - 1)
                        pe.wait_ge(avlo_r, NJ * l + job - 1)
                    if job < 2:
                        for h in range(job, SBH, 2):
                            e = 64 * (h % 2)
                            for j in range(3):
                                nk = P if j < 2 else DEC
                                vv = (vpast[:, j, h * 64:(h + 1) * 64] if j < 2 else vtok[0:DEC, NCH, h * 64:(h + 1) * 64])
                                c0 = j * SW + h // 2 * DEC
                                m = mm(bk[e:e + 64, (h // 2) * 64:(h // 2 + 1) * 64], vv, w[0:nk, c0:c0 + DEC],
                                       start=(j == 0), stop=(j == 2))
                    else:
                        h = job - 2
                        e = 64 * (h % 2)
                        for j in range(NCH):
                            m = mm(bk[e:e + 64, j * P:SEQ], vtok[:, j, h * 64:(h + 1) * 64],
                                   w[:, Z_OFF[j]:Z_OFF[j] + SEQ - j * P], start=(j == 0), stop=(j == NCH - 1),
                                   skip_group_check=True)
                    m.then_inc(av_d, 1)

                pe.wait_ge(tile_e, t + NIN)
                scores(0)
                scores(1)
                for n in range(NXA):
                    if n >= 2:
                        pe.wait_ge(tp_e, 12 * l + NXA + n + 1)
                    rows_of(n, 6 + n % 2, V0)
                pe.wait_ge(tp_e, 12 * (l + 1))
                for job in range(NJ + 1):
                    if job < NJ:
                        rest(job)
                    if job:
                        attend(job - 1)
                    if job + 2 < NJ:
                        scores(job + 2)
                a, t = unit_base(l, "OUT"), tile_base(l, "OUT")
                pn = 4 * l + 1
                pe.wait_ge(avhi_r, NJ * (l + 1))
                pe.wait_ge(avlo_r, NJ * (l + 1))
                pe.wait_ge(mixlo_r, 4 * (l + 1))
                for m in range(KD):
                    pe.wait_ge(tile_e, t + m - 1)
                    unit(a + m, m % 2, mix_hi, mix_lo)
                mean_square(2 * pn + 1)
                spread(2 * pn + 1)
                pe.wait_ge(mn_r, l + 1)
                for n in range(4):
                    if n >= 2:
                        pe.wait_ge(mlo_r, 4 * l + n - 1)
                    for q in range(2):
                        for b in range(2):
                            m = nc.tensor.transpose(BK[2 + n % 2][:, (2 * q + b) * P:(2 * q + b + 1) * P],
                                                    mtok[:, b, (2 * n + q) * P:(2 * n + q + 1) * P], ident)
                    m.then_inc(mt_d, 1)
                pe.wait_ge(mhi_r, 4 * (l + 1))
                pe.wait_ge(mlo_r, 4 * (l + 1))
                pe.wait_ge(tile_e, t + KD)
                def memory_unit(u, n):
                    pe.wait_ge(wlo_r, u + 1)
                    s = u % 2
                    products(s, KD, PL[s][:, 0, 0:NMEM], wt(slot_of(u)), lambda part, k: (m_hi, m_lo)[part][:, k, :], True, True).then_inc(unit_d, 1)

                a = unit_base(l, "MK")
                for m in range(KD):
                    if m >= 2:
                        pe.wait_ge(mkv_e, 16 * l + m - 1)
                    memory_unit(a + m, m)
                pn = 4 * l + 2
                a, t = unit_base(l, "MVQ"), tile_base(l, "MVQ")
                for m in range(KD):
                    pe.wait_ge(mkv_e, 16 * l + KD + m - (1 if m == 0 else 0))
                    memory_unit(a + 2 * m, KD + m)
                    pe.wait_ge(mkv_e, 16 * l + KD)
                    if m:
                        pe.wait_ge(tile_e, t + m)
                    u = a + 2 * m + 1
                    unit(u, 1, h_hi, h_lo, gate=h_gate(pn) if m == 0 else None, ws=slot_of(u),
                         middle={4: lambda: mean_square(2 * pn)} if m == 0 else None)
                pe.wait_ge(tile_e, t + KD)
                pe.wait_ge(rs_r, 2 * pn + 1)

                def x_scores(b):
                    nt, c0 = rows(b), b * P
                    if b >= 2:
                        pe.wait_ge(xe_r, 4 * (NXA * l + b - 1))
                    for h in range(MH):
                        for kk in range(2):
                            m = mm(PL[b % 2][0:nt, h // 2, (h % 2) * NMEM:(h % 2 + 1) * NMEM], qx[:, 2 * h + kk, c0:c0 + nt],
                                   (mk_p if b < NCH else mk_s)[:, 2 * h + kk, :], start=(kk == 0), stop=(kk == 1))
                    m.then_inc(xs_d, 1)

                def x_turn(b):
                    nt = rows(b)
                    pe.wait_ge(pn_r, 4 * (NXA * l + b + 1))
                    if b >= 2:
                        pe.wait_ge(pt_e, NXA * l + b - 1)
                    for hc in range(8):
                        m = nc.tensor.transpose(PX[b % 2][:, hc // 4, (hc % 4) * P:(hc % 4) * P + nt],
                                                pr[b % 2][0:nt, hc // 2, (hc % 2) * P:(hc % 2 + 1) * P], cst[0:nt, 0, 0:nt])
                    m.then_inc(pt_d, 1)

                x_scores(0)
                x_scores(1)
                pe.wait_ge(ck_l, 16 * (l + 1))
                for n in range(4):
                    if n >= 2:
                        pe.wait_ge(ck_e, 4 * l + n - 1)
                    for q in range(2):
                        for b in range(2):
                            m = nc.tensor.transpose(BK[2 + n % 2][:, (2 * q + b) * P:(2 * q + b + 1) * P],
                                                    mtok[:, b, (2 * n + q) * P:(2 * n + q + 1) * P], ident)
                    m.then_inc(ck_d, 1)
                pe.wait_ge(ck_e, 4 * (l + 1))
                for n in range(8):
                    if n >= 2:
                        pe.wait_ge(kr_e, 8 * l + n - 1)
                    c, n4 = n // 2 % 2, n % 2
                    for q in range(4):
                        m = nc.tensor.transpose(BK[2 + n % 2][:, q * P:(q + 1) * P],
                                                (mk_p if n < 4 else mvT)[:, 4 * n4 + q, c * P:(c + 1) * P], ident)
                    m.then_inc(kr_d, 1)
                pe.wait_ge(kr_e, 8 * (l + 1))
                for b in range(NXA):
                    if b + 2 < NXA:
                        x_scores(b + 2)
                    x_turn(b)
                pe.wait_ge(pt_e, NXA * (l + 1))
                pe.wait_ge(xe_r, 4 * NXA * (l + 1))
                pe.wait_ge(cv_l, 16 * (l + 1))
                for n in range(8):
                    h, dt = n // 2, n % 2
                    if n >= 2:
                        pe.wait_ge(xalo_r, 8 * l + n - 1)
                    for grp in range(2):
                        v = mv_p if grp == 0 else mv_s
                        c0, nt = (0, SEQ) if grp == 0 else (SEQ, DEC)
                        for c in range(2):
                            m = mm(PL[n % 2][:, grp, 0:nt], v[:, c, n * P:(n + 1) * P], pT[:, 2 * h + c, c0:c0 + nt],
                                   start=(c == 0), stop=(c == 1))
                    m.then_inc(xa_d, 1)
                a, t = unit_base(l, "MO"), tile_base(l, "MO")
                pe.wait_ge(xalo_r, 8 * (l + 1))
                for m in range(KD):
                    if m >= 2:
                        pe.wait_ge(tile_e, t + m - 1)
                    unit(a + m, m % 2, xo_hi, xo_lo)
                mean_square(2 * pn + 1)
                spread(2 * pn + 1)
                ffn(l, "F2", "D2", 4 * l + 3, 2 * l + 1)
            for n in range(2 * NXA):
                half, b = n // NXA, n % NXA
                pe.wait_ge(x_r, KD * 4 * DEPTH + 4 * (half + 1))
                if n >= 4:
                    pe.wait_ge(yt_e, n - 3)
                if n == 0:
                    pe.wait_ge(rs_r, 8 * DEPTH)
                for q in range(4):
                    m = nc.tensor.transpose(BK[n % 4][0:rows(b), q * P:(q + 1) * P], x[:, 4 * half + q, b * P:b * P + rows(b)], ident)
                m.then_inc(yt_d, 1)

        @block.scalar
        def _(act):
            A = nc.scalar.activation
            chain = [0]

            def link(ins):
                chain[0] += 1
                ins.then_inc(ach, 1)
                act.wait_ge(ach, chain[0])

            def split(u, s, words, rings=0):
                if ring_place(u) is None:
                    act.wait_ge(w_l[s], u * 8 + (16 - 8 * s - 8 * NRING * rings))
                else:
                    s = slot_of(u)
                    act.wait_ge(wr_l[s], 16 * (NRING // 3 * (u // UNITS) + ring_place(u) // 3 + 1))
                A(whi(s, slice(0, words)), rawu(s, slice(0, words)), ACT.Copy).then_inc(whi_r, 1)

            def ahead(u):
                act.wait_ge(unit_d, u - 2)
                split(u, u % 2, KD * P, rings_before(u))

            def step(u, pn=None):
                act.wait_ge(unit_d, u)
                if pn is not None:
                    post_square(pn, KD - 1)
                if u + 1 < NU:
                    split(u + 1, (u + 1) % 2, unit_words(u + 1), rings_before(u + 1))

            def square_to(n, k):
                if k == 0:
                    if n:
                        act.wait_ge(ms_r, n)
                    return acc[:, :]
                c = (KD - 1) * n + k - 1
                if c >= 2:
                    n2, k2 = (c - 2) // (KD - 1), (c - 2) % (KD - 1) + 1
                    if n2 % 2 and k2 == KD - 1:
                        act.wait_ge(ms_r, n2 + 1)
                    else:
                        act.wait_ge(acc_r, added(n2) + k2)
                return sq[:, c % 2, :]

            def pre_piece(pn, k):
                act.wait_ge(x_r, KD * pn + k + 1)
                l, n = pn // 4, pn % 4
                A(h_hi[:, k, :], x[:, k, :], ACT.Copy, scale=gpre(l, n, k)).then_inc(hi_r, 1)
                A(square_to(2 * pn, k), x[:, k, :], ACT.Square).then_inc(sq_r, 1)

            def root(n):
                if n % 2 == 0:
                    act.wait_ge(ms_r, n + 1)
                    link(A(halves(rinv[:, :]), PX[0][:, :, 0:HT], ACT.Ln, scale=1.0 / D, bias=eps))
                    A(rinv[:, :], rinv[:, :], ACT.Exp, scale=-0.5).then_inc(ye_r, 1)
                    return
                act.wait_ge(mt_r, n // 2 + 1)
                link(A(rtok, mtk, ACT.Ln))
                A(rtok, rtok, ACT.Exp, scale=-0.5).then_inc(y0_r, 1)
                act.wait_ge(bc_d, n // 2 + 1)
                A(rinv[:, :], PX[0][:, :, :].rearrange("p h t -> p (h t)")[:, 0:T], ACT.Copy).then_inc(rs_r, 1)

            def post_square(pn, m):
                A(halves(square_to(2 * pn + 1, m)), PL[m % 2][:, :, 0:HT], ACT.Square).then_inc(sq_r, 1)

            def ffn(l, pu, pd, pn, f):
                a = unit_base(l, pu)
                rings = rings_before(a)

                def first(r, words, norm=False):
                    u = r * 2 + (a + 1)
                    act.wait_ge(unit_d, u)
                    split(u + 1, 0, words, rings)
                    if norm:
                        root(2 * pn)
                        nc.scalar.preload_act_table_set("silu_and_others")
                    act.wait_ge(tile_e, r * 2 + (tile_base(l, pu) + 1))
                    A(sg[:, :], gt[:, :], ACT.Silu).then_inc(sg_r, 1)

                def second(r, words):
                    u = r * 2 + (a + 2)
                    act.wait_ge(unit_d, u)
                    split(u + 1, 1, words, rings)
                    act.wait_ge(pr_r, r + (KF * f + 1))
                    A(a_hi[:, bass.ds(r, 1), :], ut[:, :].rearrange("p (o t) -> p o t", o=1), ACT.Copy).then_inc(ahi_r, 1)

                first(0, KD * P, norm=True)
                second(0, KD * P)
                with act.Fori(1, KF - 1) as r:
                    first(r, KD * P)
                    second(r, KD * P)
                first(KF - 1, KU * P)
                second(KF - 1, KU * P)
                nc.scalar.preload_act_table_set("natural_log_exp_and_others")
                b = unit_base(l, pd)
                for u in range(b + 1, b + 2 * KD + 1):
                    step(u, pn if u == b + 2 * KD else None)
                    if (u - b) % 2 == 0 and u < b + 2 * KD:
                        post_square(pn, (u - b) // 2 - 1)
                act.wait_ge(tile_e, tile_base(l, pd))
                root(2 * pn + 1)

            act.dma_start(gst1[0:64, :], i["norm_pre"].rearrange("l n (k p) -> (l n k) p", p=P)).then_inc(cst_l, 16)
            act.dma_start(gst1[64:128, :], i["norm_post"].rearrange("l n (k p) -> (l n k) p", p=P)).then_inc(cst_l, 16)
            act.dma_start(gst2[0:16, :], i["mem_norm"].rearrange("l (k p) -> (l k) p", p=P)).then_inc(cst_l, 16)
            act.dma_start(gst2[16:28, :], i["conv_w"].rearrange("l j (k p) -> (l j k) p", p=P)).then_inc(cst_l, 16)
            act.dma_start(gst2[28:32, :], i["hg_lb"].rearrange("l (k p) -> (l k) p", p=P)).then_inc(cst_l, 16)
            act.dma_start(gst2[32:36, :], i["hg_norm"].rearrange("l (k p) -> (l k) p", p=P)).then_inc(cst_l, 16)
            nc.scalar.preload_act_table_set("natural_log_exp_and_others")
            for k in range(KD):
                if k in (KD - 4, KD - 2):
                    split((k - (KD - 4)) // 2, (k - (KD - 4)) // 2, unit_words(0))
                pre_piece(0, k)
            act.wait_ge(par_r, 3)
            A(lt[:, 2:6], lt[:, 2:6], ACT.Exp).then_inc(par_r, 1)
            for l in range(DEPTH):
                ffn(l, "F1", "D1", 4 * l, 2 * l)
                pn = 4 * l + 1
                for k in range(KD):
                    pre_piece(pn, k)
                a = unit_base(l, "IN")
                for u in range(a + 1, a + NIN + 1):
                    step(u)
                    m = u - a - 1
                    if m == 0:
                        root(2 * pn)
                    if m == U_SIG:
                        act.wait_ge(tile_e, tile_base(l, "IN") + 4)
                        hf = proj[:, HF0:HF0 + 2, :]
                        A(kf[:, :, :], hf, ACT.Sigmoid, scale=-1.0).then_inc(sig_r, 1)
                        A(bT[:, :, :], hf, ACT.Sigmoid).then_inc(sig_r, 1)
                        nc.scalar.preload_act_table_set("natural_log_exp_and_others")
                    if m == U_LN:
                        act.wait_ge(f_r, l + 1)
                        A(hE[:, :, :], bT[:, :, :], ACT.Ln).then_inc(ln_r, 1)
                        A(hQK[0][:, :, :], hQK[1][:, :, :], ACT.Ln, scale=1.0 / LN_SPLIT).then_inc(ln_r, 1)
                    if m == U_GATE:
                        act.wait_ge(tile_e, tile_base(l, "IN") + NHG)
                        gate = proj[:, HG0:HG0 + 2, :]
                        A(gate, gate, ACT.Silu).then_inc(sig_r, 1)
                        nc.scalar.preload_act_table_set("natural_log_exp_and_others")
                    if m == U_ITOK:
                        act.wait_ge(it_d, l + 1)
                        A(itok[:, 0:NCH, :].rearrange("p b n -> p (b n)"), flat(PX[0]), ACT.Copy).then_inc(it_e, 1)
                        A(itok[0:DEC, NCH, :], BK[2][0:DEC, 0:256], ACT.Copy).then_inc(it_e, 1)
                    if 0 < m - U_LEV <= LEVELS:
                        n = m - U_LEV
                        act.wait_ge(e_in, (LEVELS + 1) * l + n)
                        A(part(hE, n, 0), part(hE, n, 0), ACT.Exp, scale=-1.0)
                        A(part(hE, n, 1), part(hE, n, 1), ACT.Exp).then_inc(e_r, 1)
                    if m == U_KEND:
                        act.wait_ge(e_in, (LEVELS + 1) * (l + 1))
                        A(hE[:, :, :], hE[:, :, :], ACT.Exp, scale=-1.0).then_inc(e_r, 1)
                    if m == U_QDEC:
                        act.wait_ge(kk_r, l + 1)
                        A(hE[:, :, :], bT[:, :, :], ACT.Exp).then_inc(e_r, 1)
                    if m == U_KTOK:
                        act.wait_ge(kt_d, l + 1)
                        A(kotok[:, 0:NCH, :].rearrange("p b n -> p (b n)"), flat(PX[0]), ACT.Copy).then_inc(kt_e, 1)
                        A(kotok[0:DEC, NCH, :], BK[2][0:DEC, 0:256], ACT.Copy).then_inc(kt_e, 1)
                    if m == U_SQ:
                        act.wait_ge(ho_e, NXA * (l + 1))
                        A(hE[:, :, :], ot[:, :, :], ACT.Square).then_inc(osq_r, 1)
                    if m == U_NORM:
                        act.wait_ge(oms_d, l + 1)
                        for j in range(2):
                            ins = A(halves(hE[:, j, :]), PX[j][:, :, 0:HT], ACT.Ln, scale=1.0 / HD, bias=eps)
                        link(ins)
                        A(hE[:, :, :], hE[:, :, :], ACT.Exp, scale=-0.5).then_inc(ors_r, 1)
                for n in range(NXA + 2):
                    act.wait_ge(tp_d, 12 * l + n + 1)
                    if n < NXA:
                        A(ktok[0:rows(n), n, :], BK[n % 4][0:rows(n), :], ACT.Copy).then_inc(tp_e, 1)
                    else:
                        q = 2 * (n - NXA)
                        A(kpast[:, q:q + 2, :], BK[n % 4].rearrange("p (q t) -> p q t", q=2), ACT.Copy).then_inc(tp_e, 1)
                def front(job):
                    z, a_ = SET[job % 2], at_a[job % 2]
                    act.wait_ge(z_d, NJ * l + job + 1)
                    if job == 1:
                        act.wait_ge(kout_s, 16 * 2 * (l + 1))
                    for r_, c0, c1 in ((P, 0, 2 * SW), (DEC, 2 * SW, 3 * SW)) if job < 2 else ((P, 0, ZW),):
                        part = a_[0:r_, c0:c1]
                        link(A(part, z[0:r_, c0:c1], ACT.Abs))
                        link(A(part, part, ACT.Exp, scale=-1.0))
                        ins = A(part, part, ACT.Ln, bias=1.0)
                    ins.then_inc(l_r, 1)

                def back(job):
                    z, w = SET[job % 2], at_w[job % 2]
                    act.wait_ge(r_d, NJ * l + job + 1)
                    if job >= 2:
                        act.wait_ge(av_d, NJ * l + job - 1)
                    if job < 2:
                        A(w[:, 0:2 * SW], z[:, 0:2 * SW], ACT.Exp)
                        A(w[0:DEC, 2 * SW:3 * SW], z[0:DEC, 2 * SW:3 * SW], ACT.Exp).then_inc(wx_r, 1)
                    else:
                        A(w[:, :], z[:, 0:ZW], ACT.Exp).then_inc(wx_r, 1)

                def evac(job):
                    bk = BK[6 + job % 2]
                    act.wait_ge(av_d, NJ * l + job + 1)
                    if job < 2:
                        A(mix_hi[64 * job:64 * job + 64, 0:4, SEQ:T], bk[64 * job:64 * job + 64, 0:256].rearrange("p (q t) -> p q t", q=4), ACT.Copy).then_inc(avhi_r, 1)
                    else:
                        e, p_ = 64 * (job % 2), (job - 2) // 2
                        A(mix_hi[e:e + 64, p_, 0:SEQ], bk[e:e + 64, :], ACT.Copy).then_inc(avhi_r, 1)

                front(0)
                for b in range(NXA):
                    act.wait_ge(tp_d, 12 * l + NXA + 2 + b + 1)
                    A(vtok[0:rows(b), b, :], BK[6 + b % 2][0:rows(b), :], ACT.Copy).then_inc(tp_e, 1)
                front(1)
                for job in range(NJ + 1):
                    if job < NJ:
                        back(job)
                    if job:
                        evac(job - 1)
                    if job + 2 < NJ:
                        front(job + 2)
                    if job == 0:
                        act.wait_ge(cvr, l + 1)
                        A(mix_hi[:, 4:6, :], ct[:, :, :], ACT.Copy).then_inc(cvhi, 1)
                    if job == 4:
                        act.wait_ge(hgo_r, l + 1)
                        A(mix_hi[:, 6:8, :], ot[:, :, :], ACT.Copy).then_inc(hghi, 1)
                a = unit_base(l, "OUT")
                pn = 4 * l + 1
                act.wait_ge(mixst_s, 64 * (l + 1))
                act.wait_ge(mem_l, 16 * (l + 1))
                for b in range(2):
                    A(mk_s[:, 4 * b:4 * b + 4, :].rearrange("p k n -> p (k n)"), mtok[:, b, :], ACT.Square,
                      accum_out=mss[:, b:b + 1]).then_inc(mss_r, 1)
                act.wait_ge(mss_r, 2 * (l + 1))
                A(mss, mss, ACT.Sqrt, scale=1.0 / D, bias=eps).then_inc(mrs_r, 1)
                nc.scalar.preload_act_table_set("natural_log_exp_and_others")
                for m in range(KD):
                    step(a + m + 1, pn if m == KD - 1 else None)
                    if m < KD - 1:
                        post_square(pn, m)
                act.wait_ge(tile_e, tile_base(l, "OUT"))
                root(2 * pn + 1)
                for n in range(4):
                    act.wait_ge(mt_d, 4 * l + n + 1)
                    for q in range(2):
                        ins = A(m_hi[:, 2 * n + q, :], BK[2 + n % 2][:, q * 256:(q + 1) * 256], ACT.Copy, scale=gmem(l, 2 * n + q))
                    ins.then_inc(mhi_r, 1)
                a = unit_base(l, "MK")
                pre_piece(pn + 1, 0)
                for m in range(KD):
                    ahead(a + m + 2)
                    act.wait_ge(unit_d, a + m + 1)
                    A(mk_p[:, m, :], PL[m % 2][:, 0, 0:NMEM], ACT.Copy).then_inc(mkv_e, 1)
                    if m + 1 < KD:
                        pre_piece(pn + 1, m + 1)
                pn = 4 * l + 2
                a = unit_base(l, "MVQ")
                for m in range(KD):
                    ahead(a + 2 * m + 2)
                    act.wait_ge(unit_d, a + 2 * m + 1)
                    A(mvT[:, m, :], PL[0][:, 0, 0:NMEM], ACT.Copy).then_inc(mkv_e, 1)
                    ahead(a + 2 * m + 3)
                    if m == 0:
                        root(2 * pn)
                for n in range(4):
                    act.wait_ge(ck_d, 4 * l + n + 1)
                    A(mk_s[:, 2 * n:2 * n + 2, :], BK[2 + n % 2].rearrange("p (q t) -> p q t", q=2), ACT.Copy).then_inc(ck_e, 1)
                def x_exp(b):
                    nt, c0 = rows(b), 4 * (b % 2)
                    act.wait_ge(mx_r, NXA * l + b + 1)
                    for h in range(MH):
                        A(pr[b % 2][0:nt, h, :], PL[b % 2][0:nt, h // 2, (h % 2) * NMEM:(h % 2 + 1) * NMEM], ACT.Exp,
                          scale=1.0 / 16.0, bias=mx[0:nt, c0 + h:c0 + h + 1], accum_out=rsum[0:nt, c0 + h:c0 + h + 1]).then_inc(xe_r, 1)

                def x_keep(b):
                    nt = rows(b)
                    act.wait_ge(pt_d, NXA * l + b + 1)
                    A(pT[:, :, b * P:b * P + nt], PX[b % 2][:, :, :].rearrange("p a (q t) -> p (a q) t", q=4)[:, :, 0:nt],
                      ACT.Copy).then_inc(pt_e, 1)

                x_exp(0)
                for n in range(8):
                    act.wait_ge(kr_d, 8 * l + n + 1)
                    A((mtok if n < 4 else mv_p)[:, n // 2 % 2, (n % 2) * 512:(n % 2 + 1) * 512], BK[2 + n % 2], ACT.Copy).then_inc(kr_e, 1)
                for b in range(1, NXA):
                    if b >= 2:
                        act.wait_ge(pt_d, NXA * l + b - 1)
                    x_exp(b)
                    x_keep(b - 1)
                x_keep(NXA - 1)
                for n in range(8):
                    act.wait_ge(xa_d, 8 * l + n + 1)
                    A(xo_hi[:, n, 0:SEQ], PL[n % 2][:, 0, :], ACT.Copy).then_inc(xahi_r, 1)
                    A(xo_hi[:, n, SEQ:T], PL[n % 2][:, 1, 0:DEC], ACT.Copy).then_inc(xahi_r, 1)
                a = unit_base(l, "MO")
                for m in range(KD):
                    step(a + m + 1, pn if m == KD - 1 else None)
                    if m < KD - 1:
                        post_square(pn, m)
                act.wait_ge(tile_e, tile_base(l, "MO"))
                root(2 * pn + 1)
                for k in range(KD):
                    pre_piece(4 * l + 3, k)
                ffn(l, "F2", "D2", 4 * l + 3, 2 * l + 1)
                if l + 1 < DEPTH:
                    for k in range(KD):
                        pre_piece(4 * l + 4, k)
            for n in range(2 * NXA):
                half, b = n // NXA, n % NXA
                act.wait_ge(yt_d, n + 1)
                A(xtok[0:rows(b), b, half * 512:(half + 1) * 512], BK[n % 4][0:rows(b), :], ACT.Copy).then_inc(yt_e, 1)

        @block.vector
        def _(v):
            TT, TS, STT = nc.vector.tensor_tensor, nc.vector.tensor_scalar, nc.vector.scalar_tensor_tensor
            chain = [0]

            def link(ins):
                chain[0] += 1
                ins.then_inc(dch, 1)
                v.wait_ge(dch, chain[0])

            f32 = lambda ap: ap.bitcast(F32)

            def split(u, s, words):
                v.wait_ge(whi_r, u + 1)
                if ring_place(u) is not None:
                    s = slot_of(u)
                c = slice(0, words)
                TT(wlo(s, c), rawu(s, c), f32(whi(s, c)), ALU.subtract).then_inc(wlo_r, 1)

            def ahead(u):
                v.wait_ge(unit_d, u - 2)
                split(u, u % 2, KD * P)

            def step(u):
                v.wait_ge(unit_d, u)
                if u + 1 < NU:
                    split(u + 1, (u + 1) % 2, unit_words(u + 1))

            def h_lo_piece(pn, k):
                v.wait_ge(hi_r, KD * pn + k + 1)
                STT(h_lo[:, k, :], x[:, k, :], gpre(pn // 4, pn % 4, k), f32(h_hi[:, k, :]), ALU.mult, ALU.subtract).then_inc(lo_r, 1)

            def root(n, meanwhile=None):
                if n % 2 == 0:
                    v.wait_ge(ye_r, n // 2 + 1)
                    link(TT(gt[:, :], rinv[:, :], rinv[:, :], ALU.mult))
                    link(STT(halves(gt[:, :]), PX[0][:, :, 0:HT], D * EPS, halves(gt[:, :]), ALU.add, ALU.mult))
                    link(TS(gt[:, :], gt[:, :], -0.5 / D, 1.5, ALU.mult, ALU.add))
                    TT(rinv[:, :], rinv[:, :], gt[:, :], ALU.mult).then_inc(rs_r, 1)
                    v.wait_ge(rs_r, n + 1)
                    return
                v.wait_ge(ms_r, n + 1)
                TS(mtk, PX[0][:, 1, 504:504 + NXA], 1.0 / D, EPS, ALU.mult, ALU.add).then_inc(mt_r, 1)
                v.wait_ge(y0_r, n // 2 + 1)
                link(TT(ntk, rtok, rtok, ALU.mult))
                link(TT(ntk, ntk, mtk, ALU.mult))
                link(TS(ntk, ntk, -0.5, 1.5, ALU.mult, ALU.add))
                TT(rtok, rtok, ntk, ALU.mult).then_inc(rt_r, 1)
                if meanwhile:
                    meanwhile()
                v.wait_ge(rs_r, n + 1)

            def y_tile(l, pn, m):
                v.wait_ge(sq_r, KD * (2 * pn + 1) + m + 1)
                TS(halves(y[:, m, :]), PL[m % 2][:, :, 0:HT], gpost(l, pn % 4, m), None, ALU.mult).then_inc(tile_e, 1)

            def update(pn, k, weight):
                if k % 2 == 0:
                    TT(y[:, k, :], y[:, k, :], rinv[:, :], ALU.mult).then_inc(y_r, 1)
                    v.wait_ge(y_r, KD // 2 * pn + k // 2 + 1)
                else:
                    v.wait_ge(yp_r, KD // 2 * pn + k // 2 + 1)
                STT(x[:, k, :], y[:, k, :], weight, x[:, k, :], ALU.mult, ALU.add).then_inc(x_r, 1)

            def last_unit(l, pn, u, m):
                v.wait_ge(unit_d, u)
                y_tile(l, pn, m)
                root(2 * pn + 1, meanwhile=lambda: split(u + 1, (u + 1) % 2, unit_words(u + 1)) if u + 1 < NU else None)

            def ffn(l, pu, pd, pn, f):
                a = unit_base(l, pu)

                def pair(r, words, norm=False):
                    v.wait_ge(unit_d, r * 2 + (a + 1))
                    split(r * 2 + (a + 2), 0, words)
                    if norm:
                        root(2 * pn)
                    TT(halves(gt[:, :]), PL[0][:, :, 0:HT], halves(rinv[:, :]), ALU.mult).then_inc(tile_e, 1)
                    v.wait_ge(unit_d, r * 2 + (a + 2))
                    split(r * 2 + (a + 3), 1, words)
                    TT(halves(ut[:, :]), PL[1][:, :, 0:HT], halves(rinv[:, :]), ALU.mult).then_inc(tile_e, 1)
                    v.wait_ge(tile_e, r * 2 + (tile_base(l, pu) + 2))
                    v.wait_ge(sg_r, r + (KF * f + 1))
                    TT(ut[:, :], ut[:, :], sg[:, :], ALU.mult).then_inc(pr_r, 1)
                    v.wait_ge(ahi_r, r + (KF * f + 1))
                    o1 = "p (o t) -> p o t"
                    TT(a_lo[:, bass.ds(r, 1), :], ut[:, :].rearrange(o1, o=1), f32(a_hi[:, bass.ds(r, 1), :]), ALU.subtract).then_inc(alo_r, 1)

                pair(0, KD * P, norm=True)
                with v.Fori(1, KF - 1) as r:
                    pair(r, KD * P)
                pair(KF - 1, KU * P)
                b = unit_base(l, pd)
                for u in range(b + 1, b + 2 * KD):
                    step(u)
                    if (u - b) % 2 == 0:
                        y_tile(l, pn, (u - b) // 2 - 1)
                last_unit(l, pn, b + 2 * KD, KD - 1)

            nc.vector.memset(eps, EPS).then_inc(dch, 1)
            chain[0] += 1
            v.wait_ge(dch, chain[0])
            v.wait_ge(par_d, 1)
            nc.vector.tensor_copy(par[:, 0:128], BK[0][:, 0:128]).then_inc(par_r, 1)
            nc.vector.tensor_copy(par[:, 128:164], BK[1][:, 0:36]).then_inc(par_r, 1)
            for k in range(KD):
                v.wait_ge(xt_d, k + 1)
                link(nc.vector.tensor_copy(x[:, k, 0:SEQ], PL[k % 2][:, 0, :]))
                nc.vector.tensor_copy(x[:, k, SEQ:T], PL[k % 2][:, 1, 0:DEC]).then_inc(x_r, 1)
                if k >= KD - 2:
                    split(k - (KD - 2), k % 2, unit_words(k - (KD - 2)))
            for k in range(KD):
                h_lo_piece(0, k)
            v.wait_ge(par_r, 2)
            link(TT(lt[:, 0:2], par[:, 156:158], par[:, 158:160], ALU.max))
            link(TT(lt[:, 2:4], par[:, 156:158], lt[:, 0:2], ALU.subtract))
            TT(lt[:, 4:6], par[:, 158:160], lt[:, 0:2], ALU.subtract).then_inc(par_r, 1)
            v.wait_ge(par_r, 4)
            link(TT(lt[:, 6:8], lt[:, 2:4], lt[:, 4:6], ALU.add))
            link(nc.vector.reciprocal(lt[:, 8:10], lt[:, 6:8]))
            link(TT(lt[:, 2:4], lt[:, 2:4], lt[:, 8:10], ALU.mult))
            link(TT(lt[:, 4:6], lt[:, 4:6], lt[:, 8:10], ALU.mult))
            link(TT(lbv[:, 0:2], lt[:, 2:4], lt[:, 2:4], ALU.subtract))
            link(TT(lt[:, 10:12], lt[:, 2:4], lt[:, 4:6], ALU.add))
            link(TT(lbv[:, 2:4], lt[:, 10:12], lt[:, 2:4], ALU.subtract))
            link(TS(oml, lbv, -1.0, 1.0, ALU.mult, ALU.add))
            v.wait_ge(lm_l, 16)
            nc.vector.tensor_copy(lmask[:, :, :], lst[:, 0:LEVELS, :])
            nc.vector.tensor_copy(negb[:, :], lst[:, LEVELS, :])
            nc.vector.tensor_copy(identb[:, :], ident)
            for l in range(DEPTH):
                ffn(l, "F1", "D1", 4 * l, 2 * l)
                for k in range(KD):
                    update(4 * l, k, 0.5)
                    if k:
                        h_lo_piece(4 * l + 1, k - 1)
                h_lo_piece(4 * l + 1, KD - 1)
                pn = 4 * l + 1
                a = unit_base(l, "IN")
                q_ = proj[:, HQ0:HQ0 + 2, :]
                ec, bt = (LEVELS + 2) * l, bT[:, :, :]

                def forget():
                    v.wait_ge(sig_r, 3 * l + 2)
                    for c in range(2):
                        n = 2 * l + c
                        TS(kf[:, c, :], kf[:, c, :], oml[:, n:n + 1], None, ALU.mult)
                        ins = TS(bT[:, c, :], bT[:, c, :], oml[:, n:n + 1], lbv[:, n:n + 1], ALU.mult, ALU.add)
                    link(ins)
                    link(TS(bt, bt, F_FLOOR, None, ALU.max))
                    link(TS(hQK[1][:, :, :], bt, LN_SPLIT, None, ALU.min))
                    TS(bt, bt, LN_SPLIT, None, ALU.max).then_inc(f_r, 1)

                def scan():
                    v.wait_ge(ln_r, 2 * (l + 1))
                    link(TT(hE[:, :, :], hE[:, :, :], hQK[0][:, :, :], ALU.add))
                    for c in range(2):
                        for b in range(NXA):
                            c0, n = b * P, rows(b)
                            nc.vector.tensor_tensor_scan(bT[:, c, c0:c0 + n], ones[:, 0:n], hE[:, c, c0:c0 + n], 0.0, ALU.mult, ALU.add)
                    TT(hQK[0][:, :, :], q_, kf[:, :, :], ALU.mult).then_inc(qk0_r, 1)
                    nc.vector.memset(sacc[:, :], 0.0)
                    nc.vector.memset(itok[DEC:P, NCH, :], 0.0)
                    link(nc.vector.memset(sacc_s[:, :], 0.0))

                def exponent(n):
                    if n < LEVELS:
                        w = 1 << n
                        bb = bt.rearrange("p c (n w) -> p (c n) w", w=w)
                        TT(hE[:, :, :].rearrange("p c (n w) -> p (c n) w", w=w), bb,
                           bb[:, :, w // 2 - 1:w // 2].broadcast_to([P, 2 * T // w, w]), ALU.subtract).then_inc(e_in, 1)
                        return
                    at = P // 2 - 1 if n == LEVELS else P - 1
                    for c in range(2):
                        bb = bT[:, c, 0:SEQ].rearrange("p (n w) -> p n w", w=P)
                        ins = TT(hE[:, c, 0:SEQ].rearrange("p (n w) -> p n w", w=P), bb,
                                 bb[:, :, at:at + 1].broadcast_to([P, NCH, P]), ALU.subtract)
                        if n > LEVELS:
                            ins = TS(hE[:, c, SEQ:T], bT[:, c, SEQ:T], bT[:, c, T - 1:T], None, ALU.subtract)
                    ins.then_inc(e_in, 1)

                def decay(n):
                    v.wait_ge(e_r, ec + n)
                    TT(part(hQK[n % 2], n, 0), part(kf, n, 0), part(hE, n, 0), ALU.mult)
                    TT(part(hQK[n % 2], n, 1), part(proj[:, HQ0:HQ0 + 2, :], n, 1), part(hE, n, 1), ALU.mult).then_inc(qk_r, 1)
                    v.wait_ge(qk_r, LEVELS * l + n)

                def keep(n):
                    v.wait_ge(sc_d, LEVELS * l + n)
                    w = 1 << n
                    for nt, q, dst, src in (((P, 4 * NCH, sacc, PX[0]),) + (((DEC, 4, sacc_s, PX[1]),) if n < LEVELS else ())):
                        src_ = flat(src)[0:nt, :].rearrange("p (q t) -> p q t", q=q)[:, :, 0:nt // 2]
                        mask = lmask[0:nt, n - 1:n, 0:nt].rearrange("p o (n w) -> p o n w", w=w)[:, :, :, w // 2:w]
                        ins = nc.vector.copy_predicated(
                            dst[0:nt, :].rearrange("p (q n w) -> p q n w", q=q, w=w)[:, :, :, w // 2:w],
                            mask.broadcast_to([nt, q, nt // w, w // 2]),
                            src_.rearrange("p q (n w) -> p q n w", w=w // 2))
                    ins.then_inc(sc_e, 1)
                    v.wait_ge(sc_e, LEVELS * l + n)

                def state(c):
                    v.wait_ge(hs_d, NXA * l + c + 1)
                    sbk = BK[2 + c % 2]
                    if c == 0:
                        nc.vector.tensor_copy(st_p[:, :, :], sbk[:, 0:P].rearrange("p (j t) -> p j t", j=2)).then_inc(hs_r, 1)
                    else:
                        st = st_p if c < NCH else st_s
                        STT(st[:, 0, :], st[:, 0, :], ebl[:, c:c + 1], sbk[:, 0:64], ALU.mult, ALU.add)
                        STT(st[:, 1, :], st[:, 1, :], ebl[:, 5 + c:6 + c], sbk[:, 64:128], ALU.mult, ALU.add).then_inc(hs_r, 1)
                    v.wait_ge(hs_r, NXA * l + c + 1)
                    o_ = ot[:, :, c * P:c * P + rows(c)]
                    TT(o_, o_, BK[c % 2][:, 0:256].rearrange("p (j t) -> p j t", j=2)[:, :, 0:rows(c)], ALU.add).then_inc(ho_e, 1)

                for m in range(NIN):
                    step(a + m + 1)
                    if m == 0:
                        root(2 * pn)
                    place_ = IN_PLACE[m]
                    STT(halves(proj[:, place_, :]), PL[m % 2][:, :, 0:HT], 0.125 if Q0 <= place_ < Q0 + 4 else 1.0, halves(rinv[:, :]),
                        ALU.mult, ALU.mult).then_inc(tile_e, 1)
                    if m == U_FORGET:
                        forget()
                    if m == U_SCAN:
                        scan()
                    if m == U_DIAG:
                        v.wait_ge(dg_d, l + 1)
                        for j in range(2):
                            ins = TT(halves(ot[:, j, :]), PX[j][:, :, 0:HT], halves(proj[:, HI0 + j, :]), ALU.mult)
                        ins.then_inc(dg_e, 1)
                    if 0 < m - U_DIAG <= LEVELS:
                        keep(m - U_DIAG)
                    if 0 < m - U_LEV <= LEVELS:
                        decay(m - U_LEV)
                    if 0 <= m - U_LEV <= LEVELS:
                        exponent(m - U_LEV + 1)
                    if m == U_KEND:
                        v.wait_ge(e_r, ec + LEVELS + 1)
                        TT(hQK[0][:, :, :], kf[:, :, :], hE[:, :, :], ALU.mult).then_inc(kk_r, 1)
                    if m == U_QDEC:
                        v.wait_ge(e_r, ec + LEVELS + 2)
                        TT(hQK[1][:, :, :], q_, hE[:, :, :], ALU.mult).then_inc(qd_r, 1)
                        for c in range(2):
                            nc.vector.tensor_copy(ebl[:, 5 * c:5 * c + 4], hE[:, c, P - 1:SEQ:P])
                            ins = nc.vector.tensor_copy(ebl[:, 5 * c + 4:5 * c + 5], hE[:, c, T - 1:T])
                        link(ins)
                    if 0 <= m - U_OUT < NXA:
                        state(m - U_OUT)
                    if m == U_NORM:
                        v.wait_ge(ors_r, l + 1)
                        for j in range(2):
                            ins = STT(halves(bT[:, j, :]), PX[j][:, :, 0:HT], HD * EPS, halves(hE[:, j, :]), ALU.add, ALU.mult)
                        ins.then_inc(hu_r, 1)
                v.wait_ge(tile_e, tile_base(l, "IN") + NIN)
                v.wait_ge(conv_l, 16 * 2 * (l + 1))
                for c in range(2):
                    link(nc.vector.memset(cu[c][:, 0:2], 0.0))
                    link(TT(cu[c][:, 2:2 + SEQ], proj[:, C0 + c, 0:SEQ], proj[:, H0 + c, 0:SEQ], ALU.mult))
                    TT(cu[c][:, 4 + SEQ:4 + T], proj[:, C0 + c, SEQ:T], proj[:, H0 + c, SEQ:T], ALU.mult).then_inc(cu_r, 1)
                    v.wait_ge(cu_r, 2 * l + c + 1)
                    for s0, c0, n in ((0, 0, SEQ), (SEQ + 2, SEQ, DEC)):
                        link(TS(ct[:, c, c0:c0 + n], cu[c][:, s0:s0 + n], cw(l, 0, c), None, ALU.mult))
                        for j in (1, 2):
                            link(STT(ct[:, c, c0:c0 + n], cu[c][:, s0 + j:s0 + j + n], cw(l, j, c), ct[:, c, c0:c0 + n], ALU.mult, ALU.add))
                link(TT(ct[:, 0, :], ct[:, 0, :], proj[:, B0, :], ALU.mult))
                TT(ct[:, 1, :], ct[:, 1, :], proj[:, B0 + 1, :], ALU.mult).then_inc(cvr, 1)
                def head_norm(piece):
                    if piece == 0:
                        v.wait_ge(hu_r, l + 1)
                        v.wait_ge(sig_r, 3 * (l + 1))
                        link(TT(bt, bt, hE[:, :, :], ALU.mult))
                        link(TS(bt, bt, -0.5 / HD, 1.5, ALU.mult, ALU.add))
                    elif piece == 1:
                        link(TT(ot[:, :, :], ot[:, :, :], hE[:, :, :], ALU.mult))
                        for c in range(2):
                            ins = STT(ot[:, c, :], ot[:, c, :], gh(l, c), bT[:, c, :], ALU.mult, ALU.mult)
                        link(ins)
                    elif piece == 2:
                        TT(ot[:, :, :], ot[:, :, :], proj[:, HG0:HG0 + 2, :], ALU.mult).then_inc(hgo_r, 1)
                    elif piece == 4:
                        v.wait_ge(hghi, l + 1)
                        for c in range(2):
                            TT(mix_lo[:, 6 + c, :], ot[:, c, :], f32(mix_hi[:, 6 + c, :]), ALU.subtract).then_inc(mixlo_r, 1)

                def softplus(job):
                    z, a_, s_, c_ = SET[job % 2], at_a[job % 2], at_s[job % 2], at_c[job % 2]
                    v.wait_ge(l_r, NJ * l + job + 1)
                    if job >= 2:
                        v.wait_ge(r_d, NJ * l + job - 1)
                    if job < 2:
                        STT(s_[:, 0:2 * SW], z[:, 0:2 * SW], 0.0, a_[:, 0:2 * SW], ALU.max, ALU.add)
                        own = slice(2 * SW, 3 * SW)
                        STT(s_[0:DEC, own], z[0:DEC, own], 0.0, a_[0:DEC, own], ALU.max, ALU.add).then_inc(sp_r, 1)
                        return
                    STT(s_[:, :], z[:, 0:ZW], 0.0, a_[:, :], ALU.max, ALU.add).then_inc(sp_r, 1)
                    v.wait_ge(sp_r, NJ * l + job + 1)
                    o1, o2, o3 = Z_OFF[1], Z_OFF[2], Z_OFF[3]
                    nc.vector.tensor_copy(c_[:, 0:P], s_[:, o2:o2 + P])
                    nc.vector.tensor_copy(c_[:, 256:384], s_[:, o1:o1 + P])
                    link(TT(c_[:, P:256], s_[:, o2 + P:o2 + 256], s_[:, o3:o3 + P], ALU.add))
                    TT(c_[:, 384:640], s_[:, o1 + P:o1 + 384], c_[:, 0:256], ALU.add).then_inc(sum_r, 1)

                def evac(job):
                    bk = BK[6 + job % 2]
                    v.wait_ge(avhi_r, NJ * l + job + 1)
                    if job < 2:
                        r_ = slice(64 * job, 64 * job + 64)
                        TT(mix_lo[r_, 0:4, SEQ:T], bk[r_, 0:256].rearrange("p (q t) -> p q t", q=4), f32(mix_hi[r_, 0:4, SEQ:T]),
                           ALU.subtract).then_inc(avlo_r, 1)
                    else:
                        e, p_ = 64 * (job % 2), (job - 2) // 2
                        TT(mix_lo[e:e + 64, p_, 0:SEQ], bk[e:e + 64, :], f32(mix_hi[e:e + 64, p_, 0:SEQ]), ALU.subtract).then_inc(avlo_r, 1)

                softplus(0)
                softplus(1)
                for job in range(NJ + 1):
                    if job:
                        evac(job - 1)
                    if job + 2 < NJ:
                        softplus(job + 2)
                    if job == 1:
                        v.wait_ge(cvhi, l + 1)
                        for c in range(2):
                            TT(mix_lo[:, 4 + c, :], ct[:, c, :], f32(mix_hi[:, 4 + c, :]), ALU.subtract).then_inc(mixlo_r, 1)
                    if job:
                        head_norm(job - 1)
                v.wait_ge(hst_s, 32 * (l + 1))
                pn = 4 * l + 1
                a = unit_base(l, "OUT")
                v.wait_ge(mrs_r, l + 1)
                link(nc.vector.reciprocal(mss, mss))
                for b in range(2):
                    ins = TS(mtok[:, b, :], mtok[:, b, :], mss[:, b:b + 1], None, ALU.mult)
                    link(ins) if b == 0 else ins.then_inc(mn_r, 1)
                for m in range(KD - 1):
                    step(a + m + 1)
                    y_tile(l, pn, m)
                last_unit(l, pn, a + KD, KD - 1)
                for n_ in range(4):
                    v.wait_ge(mhi_r, 4 * l + n_ + 1)
                    for q in range(2):
                        k = 2 * n_ + q
                        ins = STT(m_lo[:, k, :], BK[2 + n_ % 2][:, q * 256:(q + 1) * 256], gmem(l, k), f32(m_hi[:, k, :]), ALU.mult, ALU.subtract)
                    ins.then_inc(mlo_r, 1)
                a = unit_base(l, "MK")
                update(pn, 0, 1.0)
                update(pn, 1, 1.0)
                for m in range(KD):
                    ahead(a + m + 2)
                    if m + 2 < KD:
                        update(pn, m + 2, 1.0)
                    h_lo_piece(pn + 1, m)
                pn = 4 * l + 2
                a = unit_base(l, "MVQ")
                for m in range(KD):
                    ahead(a + 2 * m + 2)
                    ahead(a + 2 * m + 3)
                    v.wait_ge(unit_d, a + 2 * m + 2)
                    if m == 0:
                        root(2 * pn)
                    TT(halves(qx[:, m, :]), PL[1][:, :, 0:HT], halves(rinv[:, :]), ALU.mult).then_inc(tile_e, 1)
                def x_max(b):
                    nt, c0 = rows(b), 4 * (b % 2)
                    v.wait_ge(xs_d, NXA * l + b + 1)
                    link(nc.vector.tensor_reduce(mx[0:nt, c0:c0 + 4],
                                                 PL[b % 2][0:nt, :, :].rearrange("p a (q n) -> p (a q) n", q=2), AX.X, ALU.max))
                    TS(mx[0:nt, c0:c0 + 4], mx[0:nt, c0:c0 + 4], -1.0 / 16.0, None, ALU.mult).then_inc(mx_r, 1)

                def x_norm(b):
                    nt, c0 = rows(b), 4 * (b % 2)
                    v.wait_ge(xe_r, 4 * (NXA * l + b + 1))
                    link(nc.vector.reciprocal(rrec[0:nt, c0:c0 + 4], rsum[0:nt, c0:c0 + 4]))
                    for h in range(MH):
                        TS(pr[b % 2][0:nt, h, :], pr[b % 2][0:nt, h, :], rrec[0:nt, c0 + h:c0 + h + 1], None, ALU.mult).then_inc(pn_r, 1)

                x_max(0)
                for b in range(NXA):
                    if b + 1 < NXA:
                        x_max(b + 1)
                    x_norm(b)
                for n_ in range(8):
                    v.wait_ge(xahi_r, 2 * (8 * l + n_ + 1))
                    link(TT(xo_lo[:, n_, 0:SEQ], PL[n_ % 2][:, 0, :], f32(xo_hi[:, n_, 0:SEQ]), ALU.subtract))
                    TT(xo_lo[:, n_, SEQ:T], PL[n_ % 2][:, 1, 0:DEC], f32(xo_hi[:, n_, SEQ:T]), ALU.subtract).then_inc(xalo_r, 1)
                a = unit_base(l, "MO")
                for m in range(KD - 1):
                    step(a + m + 1)
                    y_tile(l, pn, m)
                last_unit(l, pn, a + KD, KD - 1)
                for k in range(KD):
                    update(pn, k, 1.0)
                    if k:
                        h_lo_piece(pn + 1, k - 1)
                h_lo_piece(pn + 1, KD - 1)
                ffn(l, "F2", "D2", 4 * l + 3, 2 * l + 1)
                for k in range(KD):
                    update(4 * l + 3, k, 0.5)
                    if k and l + 1 < DEPTH:
                        h_lo_piece(4 * l + 4, k - 1)
                if l + 1 < DEPTH:
                    h_lo_piece(4 * l + 4, KD - 1)

        @block.gpsimd
        def _(pool):
            def add_squares(n):
                for k in range(1, KD - n % 2):
                    c = (KD - 1) * n + k - 1
                    pool.wait_ge(sq_r, KD * n + k + 1)
                    if k > 1:
                        pool.wait_ge(acc_r, added(n) + k - 1)
                    nc.gpsimd.tensor_tensor(acc[:, :], acc[:, :], sq[:, c % 2, :], ALU.add).then_inc(acc_r, 1)

            def scale_odd(l, phase):
                pn = 4 * l + POST[phase]
                pool.wait_ge(tile_e, tile_base(l, phase) + KD)
                pool.wait_ge(rs_r, 2 * pn + 2)
                for k in range(1, KD, 2):
                    nc.gpsimd.tensor_tensor(y[:, k, :], y[:, k, :], rinv[:, :], ALU.mult).then_inc(yp_r, 1)

            dma = pool.dma_start
            dma(lst[:, :, :], i["lm"].rearrange("n p m -> p n m")).then_inc(lm_l, 16)
            add_squares(0)
            for l in range(DEPTH):
                add_squares(8 * l + 1)
                scale_odd(l, "D1")
                add_squares(8 * l + 2)
                pool.wait_ge(tile_e, tile_base(l, "IN"))
                dma(st_s[:, :, :], i["state_hgrn"][l, 0].rearrange("(j e) k v -> (e k) j v", j=2)).then_inc(s0_l, 16)
                pool.wait_ge(hs_r, NXA * (l + 1))
                pool.wait_ge(ho_e, NXA * (l + 1))
                dma(kpast_tok[:, :, :], i["cache_sb_k"][l, 0].rearrange("(b p) h d -> p b (h d)", p=P)).then_inc(cache_l, 16)
                dma(vpast[:, :, :], i["cache_sb_v"][l, 0].rearrange("(b p) h d -> p b (h d)", p=P)).then_inc(cache_l, 16)
                for c in range(2):
                    with nc.allow_non_contiguous_dma(reason="two rows of the convolution's state, feature-major"):
                        dma(cu[c][:, SEQ + 2:SEQ + 4], i["state_conv"][l, 0][:, c * P:(c + 1) * P].rearrange("r p -> p r")).then_inc(conv_l, 16)
                dma(o["hg_p"][l, 0].rearrange("(j e) k v -> (e k) j v", j=2), st_p[:, :, :]).then_inc(hst_s, 16)
                dma(o["hg_s"][l, 0].rearrange("(j e) k v -> (e k) j v", j=2), st_s[:, :, :]).then_inc(hst_s, 16)
                pool.wait_ge(tp_e, 12 * l + NXA)
                dma(o["sb_k_p"][l, 0].rearrange("(b p) h d -> p b (h d)", p=P), ktok[:, 0:NCH, :]).then_inc(kout_s, 16)
                dma(o["sb_k_s"][l, 0].rearrange("p h d -> p (h d)"), ktok[0:DEC, NCH, :]).then_inc(kout_s, 16)
                pool.wait_ge(cu_r, 2 * (l + 1))
                for c in range(2):
                    with nc.allow_non_contiguous_dma(reason="two rows of the convolution's state, feature-major"):
                        dma(o["conv_p"][l, 0][:, c * P:(c + 1) * P].rearrange("r p -> p r"), cu[c][:, SEQ:SEQ + 2]).then_inc(mixst_s, 16)
                        dma(o["conv_s"][l, 0][:, c * P:(c + 1) * P].rearrange("r p -> p r"), cu[c][:, T + 2:T + 4]).then_inc(mixst_s, 16)
                pool.wait_ge(tp_e, 12 * (l + 1))
                dma(o["sb_v_p"][l, 0].rearrange("(b p) h d -> p b (h d)", p=P), vtok[:, 0:NCH, :]).then_inc(y_s, 16)
                dma(o["sb_v_s"][l, 0].rearrange("p h d -> p (h d)"), vtok[0:DEC, NCH, :]).then_inc(y_s, 16)
                pool.wait_ge(avlo_r, NJ * (l + 1))
                pool.wait_ge(avhi_r, NJ * (l + 1))
                pool.wait_ge(mixlo_r, 4 * (l + 1))
                pool.wait_ge(y_s, 48 * l + 32)
                dma(mtok[:, :, :], i["mem_prompt"][0].rearrange("(b p) d -> p b d", p=P)).then_inc(mem_l, 16)
                dma(mv_s[:, :, :], i["cache_mem_v"][l, 0].rearrange("(b p) h d -> p b (h d)", p=P)).then_inc(cv_l, 16)
                add_squares(8 * l + 3)
                scale_odd(l, "OUT")
                pool.wait_ge(mt_d, 4 * (l + 1))
                dma(mtok[:, :, :], i["cache_mem_k"][l, 0].rearrange("(b p) h d -> p b (h d)", p=P)).then_inc(ck_l, 16)
                add_squares(8 * l + 4)
                pool.wait_ge(kr_e, 8 * (l + 1))
                dma(o["mem_v"][l, 0].rearrange("(b p) h d -> p b (h d)", p=P), mv_p[:, :, :]).then_inc(y_s, 16)
                dma(o["mem_k"][l, 0].rearrange("(b p) h d -> p b (h d)", p=P), mtok[:, :, :]).then_inc(kr_s, 16)
                add_squares(8 * l + 5)
                scale_odd(l, "MO")
                pool.wait_ge(y_s, 48 * (l + 1))
                pool.wait_ge(kr_s, 16 * (l + 1))
                add_squares(8 * l + 6)
                add_squares(8 * l + 7)
                scale_odd(l, "D2")
                if l + 1 < DEPTH:
                    add_squares(8 * l + 8)
            for half in range(2):
                cols = slice(half * 512, (half + 1) * 512)
                pool.wait_ge(yt_e, NXA * (half + 1))
                dma(o["y_p"][0].rearrange("(b p) d -> p b d", p=P)[:, :, cols], xtok[:, 0:NCH, cols]).then_inc(y_s, 16)
                dma(o["y_s"][0][:, cols], xtok[0:DEC, NCH, cols]).then_inc(y_s, 16)
            pool.wait_ge(y_s, 48 * DEPTH + 64)
            pool.wait_ge(kout_s, 32 * DEPTH)
            pool.wait_ge(mixst_s, 64 * DEPTH)
            pool.wait_ge(hst_s, 32 * DEPTH)
            pool.wait_ge(kr_s, 16 * DEPTH)


_INS = ["x_prompt", "x_sample", "mem_prompt", "cache_sb_k", "cache_sb_v", "cache_mem_k", "cache_mem_v", "state_conv",
        "state_hgrn", "norm_pre", "norm_post", "ffn1_gu", "ffn1_down", "w_in", "conv_w", "hg_lb", "hg_norm", "w_out",
        "mem_norm", "w_mk", "w_mv", "w_mq", "w_mo", "ffn2_gu", "ffn2_down"]
_OUTS = [("y_p", (1, SEQ, D)), ("y_s", (1, DEC, D)),
         ("sb_k_p", (DEPTH, 1, SEQ, SBH, HD)), ("sb_v_p", (DEPTH, 1, SEQ, SBH, HD)),
         ("conv_p", (DEPTH, 1, 2, 256)), ("hg_p", (DEPTH, 1, 4, 64, 64)),
         ("mem_k", (DEPTH, 1, NMEM, MH, MHD)), ("mem_v", (DEPTH, 1, NMEM, MH, MHD)),
         ("sb_k_s", (DEPTH, 1, DEC, SBH, HD)), ("sb_v_s", (DEPTH, 1, DEC, SBH, HD)),
         ("conv_s", (DEPTH, 1, 2, 256)), ("hg_s", (DEPTH, 1, 4, 64, 64))]


def constants():
    import numpy as np
    s, t = np.arange(P)[:, None], np.arange(P)[None, :]
    cf = np.stack([s == t, -1.0 * (s >= t), -np.ones((P, P)), np.ones((P, P)), s // 64 == t // 64]).astype(np.float32)
    lm = np.stack([((s ^ t) >> (n - 1) == 1) & (t > s) for n in range(1, LEVELS + 1)]
                  + [NEG * (t <= s)]).astype(np.float32)
    return cf, lm


def kernel(**inputs):
    import numpy as _np
    import concourse.bacc as _bacc
    from concourse import mybir as _mybir
    from concourse.bass_utils import run_bass_kernel_spmd as _run

    nc = _bacc.Bacc("TRN2", target_bir_lowering=False, num_devices=1)
    arrays, ins, outs = {}, {}, {}
    given = {name: _np.ascontiguousarray(inputs[name]) for name in _INS}
    given["cf"], given["lm"] = constants()
    for name, a in given.items():
        arrays[f"in_{name}_dram"] = a
        ins[name] = nc.dram_tensor(f"in_{name}_dram", a.shape, _mybir.dt.from_np(a.dtype), kind="ExternalInput").ap()
    for n, (name, shape) in enumerate(_OUTS):
        outs[name] = nc.dram_tensor(f"out_{n}_dram", shape, _mybir.dt.from_np(_np.dtype("float32")), kind="ExternalOutput").ap()
    hybrid_trunk(nc, ins, outs)
    r = _run(nc, [arrays], core_ids=[0])
    return tuple(r.results[0][f"out_{n}_dram"] for n in range(len(_OUTS)))
```
